# Optimizing a Trainium2 kernel written in Bass

```python
import math
import jax, jax.numpy as jnp
from jax import lax
import numpy as np

D_MODEL = 1024
BATCH = 1
SEQ = 1024
DEPTH = 2
DEC_BATCH = 8
DEC_SEQ = 16
PAST_LEN = 512

CHUNK = 64
N_ATTN_LAYERS = (DEPTH + 1) // 2
N_SSM_LAYERS = DEPTH // 2
EPS = 1e-6
F32 = jnp.float32

A_HEADS = 8
A_KV_HEADS = 2
A_GROUP = A_HEADS // A_KV_HEADS
HEAD_DIM = 64
A_WIDTH = A_HEADS * HEAD_DIM
KV_WIDTH = A_KV_HEADS * HEAD_DIM
WINDOW = 128
BAND_CHUNKS = WINDOW // CHUNK
ROPE_DIM = HEAD_DIM // 4
ROPE_THETA = 500000.0
ATTN_SCALE = HEAD_DIM ** -0.5
WIN_CACHE = min(WINDOW, PAST_LEN)
WIN_PROMPT = min(WINDOW, SEQ)

B_WIDTH = D_MODEL // 2
B_CONV = 3
AB_IN = A_WIDTH + 2 * KV_WIDTH + 3 * B_WIDTH
AB_OUT_IN = A_WIDTH + B_WIDTH

SSM_INNER = 2 * D_MODEL
SSM_HEADDIM = 64
SSM_HEADS = SSM_INNER // SSM_HEADDIM
SSM_GROUPS = 4
SSM_HPG = SSM_HEADS // SSM_GROUPS
SSM_STATE = 128
SSM_CONV = 4
SSM_GN = SSM_GROUPS * SSM_STATE
SSM_CONV_CH = SSM_INNER + 2 * SSM_GN
SSM_IN = 2 * SSM_INNER + 2 * SSM_GN + SSM_HEADS

D_FF = -(-8 * D_MODEL // (3 * 256)) * 256

kernel_name = 'hybrid_chunk_streaming_encoder_step'

def rmsnorm(x, g):
    xf = x.astype(F32)
    xf = xf * lax.rsqrt(jnp.mean(xf * xf, axis=-1, keepdims=True) + EPS)
    return (xf * g.astype(F32)).astype(x.dtype)

def rope_partial(x, pos):
    half = ROPE_DIM // 2
    inv_freq = jnp.power(ROPE_THETA, -jnp.arange(half, dtype=F32) / half)
    ang = pos[:, None] * inv_freq[None, :]
    cos = jnp.cos(ang)[:, None, :].astype(x.dtype)
    sin = jnp.sin(ang)[:, None, :].astype(x.dtype)
    x1 = x[..., :half]
    x2 = x[..., half:ROPE_DIM]
    return jnp.concatenate([x1 * cos - x2 * sin, x2 * cos + x1 * sin, x[..., ROPE_DIM:]], axis=-1)

def sink_attention(q, k, v, sinks, mask):
    s = jnp.einsum('...qkgd,...skd->...kgqs', q, k).astype(F32) * ATTN_SCALE
    if mask is not None:
        s = jnp.where(mask, s, -jnp.inf)
    sink = sinks.astype(F32).reshape(A_KV_HEADS, A_GROUP, 1, 1)
    m = jnp.maximum(jnp.max(s, axis=-1, keepdims=True), sink)
    p = jnp.exp(s - m)
    p = p / (jnp.sum(p, axis=-1, keepdims=True) + jnp.exp(sink - m))
    return jnp.einsum('...kgqs,...skd->...qkgd', p.astype(v.dtype), v)

def band_attention(q, k, v, sinks):
    b, L = q.shape[0], q.shape[1]
    nc = L // CHUNK
    nb = BAND_CHUNKS + 1
    qb = q.reshape(b, nc, CHUNK, A_KV_HEADS, A_GROUP, HEAD_DIM)

    def bands(t):
        tp = jnp.pad(t, ((0, 0), (BAND_CHUNKS * CHUNK, 0), (0, 0), (0, 0)))
        tp = tp.reshape(b, nc + BAND_CHUNKS, CHUNK, A_KV_HEADS, HEAD_DIM)
        return jnp.concatenate([tp[:, j:j + nc] for j in range(nb)], axis=2)

    key_chunk = jnp.arange(nc)[:, None] - BAND_CHUNKS + jnp.arange(nb * CHUNK)[None, :] // CHUNK
    mask = (key_chunk >= 0)[None, :, None, None, None, :]
    o = sink_attention(qb, bands(k), bands(v), sinks, mask)
    return o.reshape(b, L, A_WIDTH)

def causal_dwconv(u, hist, w):
    width = w.shape[0]
    L = u.shape[1]
    up = jnp.concatenate([hist.astype(u.dtype), u], axis=1)
    y = up[:, 0:L] * w[0]
    for j in range(1, width):
        y = y + up[:, j:j + L] * w[j]
    return y, up[:, L:]

def mixer_attn_conv(h, pos, sconv_hist, kv_cache, w_in, w_out, sinks, conv_w):
    b, L, _ = h.shape
    p = h @ w_in
    o1 = A_WIDTH
    o2 = o1 + KV_WIDTH
    o3 = o2 + KV_WIDTH
    o4 = o3 + B_WIDTH
    o5 = o4 + B_WIDTH
    q = rope_partial(p[..., :o1].reshape(b, L, A_HEADS, HEAD_DIM), pos)
    k = rope_partial(p[..., o1:o2].reshape(b, L, A_KV_HEADS, HEAD_DIM), pos)
    v = p[..., o2:o3].reshape(b, L, A_KV_HEADS, HEAD_DIM)
    gate_b = p[..., o3:o4]
    gate_c = p[..., o4:o5]
    hx = p[..., o5:]
    qg = q.reshape(b, L, A_KV_HEADS, A_GROUP, HEAD_DIM)
    if kv_cache is None:
        attn = band_attention(qg, k, v, sinks)
        new_k = k[:, L - WIN_PROMPT:]
        new_v = v[:, L - WIN_PROMPT:]
    else:
        cache_k, cache_v = kv_cache
        k_all = jnp.concatenate([cache_k.astype(k.dtype), k], axis=1)
        v_all = jnp.concatenate([cache_v.astype(v.dtype), v], axis=1)
        attn = sink_attention(qg, k_all, v_all, sinks, None).reshape(b, L, A_WIDTH)
        new_k = k
        new_v = v
    conv_y, new_hist = causal_dwconv(gate_c * hx, sconv_hist, conv_w)
    out = jnp.concatenate([attn, gate_b * conv_y], axis=-1) @ w_out
    return out, new_k, new_v, new_hist

def ssd_scan(x, dt, a, bm, cm, h0):
    b, L = x.shape[0], x.shape[1]
    lc = min(CHUNK, L)
    nc = L // lc
    x = x.reshape(b, nc, lc, SSM_GROUPS, SSM_HPG, SSM_HEADDIM)
    dt = dt.reshape(b, nc, lc, SSM_GROUPS, SSM_HPG)
    bm = bm.reshape(b, nc, lc, SSM_GROUPS, SSM_STATE)
    cm = cm.reshape(b, nc, lc, SSM_GROUPS, SSM_STATE)
    h0 = h0.reshape(b, SSM_GROUPS, SSM_HPG, SSM_HEADDIM, SSM_STATE)
    acum = jnp.cumsum(dt * a.reshape(SSM_GROUPS, SSM_HPG), axis=2)
    causal = jnp.tril(jnp.ones((lc, lc), dtype=bool))[None, None, :, :, None, None]
    seg = acum[:, :, :, None] - acum[:, :, None, :]
    decay = jnp.exp(jnp.where(causal, seg, -jnp.inf))
    cb = jnp.einsum('bclgn,bcsgn->bclsg', cm, bm)
    wgt = cb[..., None] * decay * dt[:, :, None]
    y_diag = jnp.einsum('bclsgr,bcsgrp->bclgrp', wgt, x)
    decay_end = jnp.exp(acum[:, :, -1:] - acum) * dt
    states = jnp.einsum('bclgn,bclgr,bclgrp->bcgrpn', bm, decay_end, x)
    chunk_decay = jnp.exp(acum[:, :, -1])

    def step(hc, inp):
        dec, st = inp
        return hc * dec[..., None, None] + st, hc

    h_last, h_prev = lax.scan(step, h0, (jnp.moveaxis(chunk_decay, 1, 0), jnp.moveaxis(states, 1, 0)))
    h_prev = jnp.moveaxis(h_prev, 0, 1)
    y_off = jnp.einsum('bclgn,bcgrpn->bclgrp', cm, h_prev) * jnp.exp(acum)[..., None]
    y = (y_diag + y_off).reshape(b, L, SSM_HEADS, SSM_HEADDIM)
    return y, h_last.reshape(b, SSM_HEADS, SSM_HEADDIM, SSM_STATE)

def mixer_ssd(h, conv_hist, ssm_state, w_in, conv_w, conv_b, dt_bias, a_log, d_skip, norm_g, w_out):
    b, L, _ = h.shape
    p = h @ w_in
    z = p[..., :SSM_INNER]
    xbc = p[..., SSM_INNER:SSM_INNER + SSM_CONV_CH]
    dt_raw = p[..., SSM_INNER + SSM_CONV_CH:]
    xbc, new_conv = causal_dwconv(xbc, conv_hist, conv_w)
    xbc = jax.nn.silu(xbc + conv_b)
    xs = xbc[..., :SSM_INNER].reshape(b, L, SSM_HEADS, SSM_HEADDIM).astype(F32)
    bm = xbc[..., SSM_INNER:SSM_INNER + SSM_GN].reshape(b, L, SSM_GROUPS, SSM_STATE).astype(F32)
    cm = xbc[..., SSM_INNER + SSM_GN:].reshape(b, L, SSM_GROUPS, SSM_STATE).astype(F32)
    dt = jax.nn.softplus(dt_raw.astype(F32) + dt_bias.astype(F32))
    a = -jnp.exp(a_log.astype(F32))
    y, new_state = ssd_scan(xs, dt, a, bm, cm, ssm_state.astype(F32))
    y = y + d_skip.astype(F32)[:, None] * xs
    g = y.reshape(b, L, SSM_INNER) * jax.nn.silu(z.astype(F32))
    g = g.reshape(b, L, SSM_GROUPS, SSM_INNER // SSM_GROUPS)
    g = g * lax.rsqrt(jnp.mean(g * g, axis=-1, keepdims=True) + EPS)
    g = g.reshape(b, L, SSM_INNER) * norm_g.astype(F32)
    out = g.astype(h.dtype) @ w_out
    return out, new_conv, new_state.astype(ssm_state.dtype)

def swiglu(h, w_gate, w_up, w_down):
    return (jax.nn.silu(h @ w_gate) * (h @ w_up)) @ w_down

def setup_inputs(seed: int = 0) -> dict:
    key = jax.random.key(seed)
    ks = jax.random.split(key, 26)
    NA, NS = N_ATTN_LAYERS, N_SSM_LAYERS

    def nrm(k, shape, scale):
        return jax.random.normal(k, shape, F32) * scale

    dt0 = jnp.exp(jax.random.uniform(ks[20], (NS, SSM_HEADS), F32, math.log(1e-3), math.log(1e-1)))
    return {
        'x_prompt': nrm(ks[0], (BATCH, SEQ, D_MODEL), 1.0),
        'x_sample': nrm(ks[1], (DEC_BATCH, DEC_SEQ, D_MODEL), 1.0),
        'cache_attn_k': nrm(ks[2], (NA, DEC_BATCH, WIN_CACHE, A_KV_HEADS, HEAD_DIM), 1.0),
        'cache_attn_v': nrm(ks[3], (NA, DEC_BATCH, WIN_CACHE, A_KV_HEADS, HEAD_DIM), 1.0),
        'state_sconv': nrm(ks[4], (NA, DEC_BATCH, B_CONV - 1, B_WIDTH), 1.0),
        'state_ssm_conv': nrm(ks[5], (NS, DEC_BATCH, SSM_CONV - 1, SSM_CONV_CH), 1.0),
        'state_ssm': nrm(ks[6], (NS, DEC_BATCH, SSM_HEADS, SSM_HEADDIM, SSM_STATE), 0.1),
        'norm_g': 1.0 + nrm(ks[7], (DEPTH, 4, D_MODEL), 0.05),
        'ab_w_in': nrm(ks[8], (NA, D_MODEL, AB_IN), D_MODEL ** -0.5),
        'ab_w_out': nrm(ks[9], (NA, AB_OUT_IN, D_MODEL), AB_OUT_IN ** -0.5),
        'attn_sinks': nrm(ks[10], (NA, A_HEADS), 0.5),
        'sconv_w': nrm(ks[11], (NA, B_CONV, B_WIDTH), B_CONV ** -0.5),
        'ssm_w_in': nrm(ks[12], (NS, D_MODEL, SSM_IN), D_MODEL ** -0.5),
        'ssm_conv_w': nrm(ks[13], (NS, SSM_CONV, SSM_CONV_CH), SSM_CONV ** -0.5),
        'ssm_conv_b': nrm(ks[14], (NS, SSM_CONV_CH), 0.02),
        'ssm_dt_bias': dt0 + jnp.log(-jnp.expm1(-dt0)),
        'ssm_a_log': jnp.log(jax.random.uniform(ks[15], (NS, SSM_HEADS), F32, 1.0, 16.0)),
        'ssm_d': 1.0 + nrm(ks[16], (NS, SSM_HEADS), 0.1),
        'ssm_norm_g': 1.0 + nrm(ks[17], (NS, SSM_INNER), 0.05),
        'ssm_w_out': nrm(ks[18], (NS, SSM_INNER, D_MODEL), SSM_INNER ** -0.5),
        'ffn_w_gate': nrm(ks[19], (DEPTH, D_MODEL, D_FF), D_MODEL ** -0.5),
        'ffn_w_up': nrm(ks[21], (DEPTH, D_MODEL, D_FF), D_MODEL ** -0.5),
        'ffn_w_down': nrm(ks[22], (DEPTH, D_FF, D_MODEL), D_FF ** -0.5),
    }

def reference(x_prompt, x_sample, cache_attn_k, cache_attn_v, state_sconv, state_ssm_conv, state_ssm,
              norm_g, ab_w_in, ab_w_out, attn_sinks, sconv_w, ssm_w_in, ssm_conv_w, ssm_conv_b,
              ssm_dt_bias, ssm_a_log, ssm_d, ssm_norm_g, ssm_w_out, ffn_w_gate, ffn_w_up, ffn_w_down):
    pos_p = jnp.arange(SEQ, dtype=F32)
    pos_s = PAST_LEN + jnp.arange(DEC_SEQ, dtype=F32)
    xp, xs = x_prompt, x_sample
    kp_l, vp_l, scp_l, ks_l, vs_l, scs_l = [], [], [], [], [], []
    ccp_l, ssp_l, ccs_l, sss_l = [], [], [], []
    for layer in range(DEPTH):
        g = norm_g[layer]
        i = layer // 2
        hp = rmsnorm(xp, g[0])
        hs = rmsnorm(xs, g[0])
        if layer % 2 == 0:
            wts = (ab_w_in[i], ab_w_out[i], attn_sinks[i], sconv_w[i])
            zero_hist = jnp.zeros((BATCH, B_CONV - 1, B_WIDTH), xp.dtype)
            mp, nkp, nvp, nscp = mixer_attn_conv(hp, pos_p, zero_hist, None, *wts)
            ms, nks, nvs, nscs = mixer_attn_conv(hs, pos_s, state_sconv[i],
                                                 (cache_attn_k[i], cache_attn_v[i]), *wts)
            kp_l.append(nkp)
            vp_l.append(nvp)
            scp_l.append(nscp)
            ks_l.append(nks)
            vs_l.append(nvs)
            scs_l.append(nscs)
        else:
            wts = (ssm_w_in[i], ssm_conv_w[i], ssm_conv_b[i], ssm_dt_bias[i], ssm_a_log[i],
                   ssm_d[i], ssm_norm_g[i], ssm_w_out[i])
            zero_conv = jnp.zeros((BATCH, SSM_CONV - 1, SSM_CONV_CH), xp.dtype)
            zero_state = jnp.zeros((BATCH, SSM_HEADS, SSM_HEADDIM, SSM_STATE), state_ssm.dtype)
            mp, nccp, nssp = mixer_ssd(hp, zero_conv, zero_state, *wts)
            ms, nccs, nsss = mixer_ssd(hs, state_ssm_conv[i], state_ssm[i], *wts)
            ccp_l.append(nccp)
            ssp_l.append(nssp)
            ccs_l.append(nccs)
            sss_l.append(nsss)
        xp = xp + rmsnorm(mp, g[1])
        xs = xs + rmsnorm(ms, g[1])
        fw = (ffn_w_gate[layer], ffn_w_up[layer], ffn_w_down[layer])
        xp = xp + rmsnorm(swiglu(rmsnorm(xp, g[2]), *fw), g[3])
        xs = xs + rmsnorm(swiglu(rmsnorm(xs, g[2]), *fw), g[3])
    return (xp, xs,
            jnp.stack(kp_l), jnp.stack(vp_l), jnp.stack(scp_l), jnp.stack(ccp_l), jnp.stack(ssp_l),
            jnp.stack(ks_l), jnp.stack(vs_l), jnp.stack(scs_l), jnp.stack(ccs_l), jnp.stack(sss_l))


_drawn_inputs = setup_inputs


def setup_inputs(seed=0):
    import zlib

    import numpy as np

    out = dict(_drawn_inputs(seed))
    spreads = {}
    factors = {'attn_sinks': 8.0}
    for name, (base, spread) in spreads.items():
        noise = np.random.default_rng([zlib.crc32(name.encode()), seed]).standard_normal(out[name].shape)
        drawn = base * np.exp(spread * noise) if base else spread * noise
        out[name] = __import__('jax').numpy.asarray(drawn.astype(out[name].dtype))
    for name, factor in factors.items():
        out[name] = (out[name] * factor).astype(out[name].dtype)
    return out
```

```python
from contextlib import ExitStack

import numpy as np

import concourse.bass as bass
from concourse import mybir

F32, F16 = mybir.dt.float32, mybir.dt.float16
AF = mybir.ActivationFunctionType
ALU = mybir.AluOpType
AX_X = mybir.AxisListType.X
ds = bass.ds

P = 128
D, SEQ, STREAMS, STEP = 1024, 1024, 8, 16
T = SEQ + STREAMS * STEP
TT = T // P
BLOCKS, BW = 3, T // 3
KD = D // P
HEADS, GROUP, HD, CHUNK = 8, 4, 64, 64
PAST = 512
ROPE = HD // 4
DFF = 2816
FT = DFF // P
DOWN_K = FT // 2
SG, SHPG, SHD, SN = 4, 8, 64, 128
SHEADS = SG * SHPG
GW = SHPG * SHD
UNIT = KD * P
WSCALE = 64.0
EPS = 1e-6
MODEL_SCALE = 1.0 / D
XW = SEQ + 2 + STREAMS * (STEP + 2)
XW3 = SEQ + 3 + STREAMS * (STEP + 3)


def sizes(segment):
    return segment[0].shape[0], segment[1]


class Core:

    def __init__(self, nc, ctx, segments):
        self.nc, self.ctx = nc, ctx
        self.stage_sems = []
        self.segments = segments
        self.starts = [0]
        for w, _ in segments:
            self.starts.append(self.starts[-1] + w.shape[0])
        most = max(f for _, f in segments)
        self.w_raw = self.sbuf("w_raw", [P, 2, most], F32)
        self.w_hi = self.sbuf("w_hi", [P, 2, most], F16)
        self.w_lo = self.sbuf("w_lo", [P, 2, most], F16)
        self.w_loaded = [self.sem("w_loaded0"), self.sem("w_loaded1")]
        self.w_hi_ready = self.sem("w_hi_ready")
        self.w_lo_ready = self.sem("w_lo_ready")
        self.stage_sems = []

    def sbuf(self, name, shape, dtype, ctx=None):
        return (ctx or self.ctx).enter_context(self.nc.sbuf_tensor(name, shape, dtype))

    def psum(self, name, shape, ctx):
        return ctx.enter_context(self.nc.psum_tensor(name, shape, F32))

    def sem(self, name):
        self.stage_sems.append(self.nc.alloc_semaphore(name))
        return self.stage_sems[-1]

    def end_stage(self):
        self.nc.clear_and_free_semaphores(self.stage_sems)
        self.nc.all_engine_barrier()
        self.stage_sems = []

    def segment_of(self, u):
        n = max(k for k, s in enumerate(self.starts[:-1]) if s <= u)
        return self.segments[n], self.starts[n]


    def load_weights(self, sp, u, i=0):
        if u >= self.starts[-1]:
            return
        (w, cols), start = self.segment_of(u)
        if u >= 2:
            sp.wait_ge(self.w_hi_ready, u - 1 + 2 * i)
            sp.wait_ge(self.w_lo_ready, u - 1 + 2 * i)
        src = w[ds(u - start + 2 * i, 1), :, :].rearrange("a p c -> (a p) c") if not isinstance(i, int) \
            else w[u - start + 2 * i, :, :]
        sp.dma_start(self.w_raw[:, u % 2, 0:cols], src).then_inc(self.w_loaded[u % 2], 16)

    def split_hi(self, act, u, i=0, acc=None, acc_value=None):
        if u >= self.starts[-1]:
            return
        cols = self.segment_of(u)[0][1]
        act.wait_ge(self.w_loaded[u % 2], 16 * (u // 2 + 1) + 16 * i)
        if acc is not None:
            act.wait_ge(acc, acc_value)
        self.nc.scalar.activation(self.w_hi[:, u % 2, 0:cols], self.w_raw[:, u % 2, 0:cols], AF.Copy,
                                  scale=WSCALE).then_inc(self.w_hi_ready, 1)

    def split_lo(self, dve, u, i=0, acc=None, acc_value=None):
        if u >= self.starts[-1]:
            return
        cols = self.segment_of(u)[0][1]
        if acc is not None:
            dve.wait_ge(acc, acc_value)
        dve.wait_ge(self.w_hi_ready, u + 1 + 2 * i)
        self.nc.vector.scalar_tensor_tensor(self.w_lo[:, u % 2, 0:cols], self.w_raw[:, u % 2, 0:cols], WSCALE,
                                            self.w_hi[:, u % 2, 0:cols], ALU.mult, ALU.subtract
                                            ).then_inc(self.w_lo_ready, 1)

    def weights_split(self, pe, u, i=0):
        pe.wait_ge(self.w_hi_ready, u + 1 + 2 * i)
        pe.wait_ge(self.w_lo_ready, u + 1 + 2 * i)

    def multiply(self, out, u, k_tiles, x_hi, x_lo, k0, cols, first, last):
        for k in range(k_tiles):
            wh = self.w_hi[:, u % 2, k * P:(k + 1) * P]
            wl = self.w_lo[:, u % 2, k * P:(k + 1) * P]
            xh, xl = x_hi[:, k0 + k, cols], x_lo[:, k0 + k, cols]
            self.nc.tensor.matmul(out, wh, xh, start=(first and k == 0), stop=False)
            self.nc.tensor.matmul(out, wh, xl, start=False, stop=False)
            mm = self.nc.tensor.matmul(out, wl, xh, start=False, stop=(last and k == k_tiles - 1))
        return mm


def blk(b):
    return slice(b * BW, (b + 1) * BW)


def run(engine, n, body):
    body(0, True, n == 1)
    if n > 3:
        with engine.Fori(1, n - 1) as i:
            body(i, False, False)
    else:
        for i in range(1, n - 1):
            body(i, False, False)
    if n > 1:
        body(n - 1, False, True)


def load_ring(c, sp, s, e):
    own = max(0, e - s - 4) // 2
    if own > 0:
        with sp.Fori(0, own) as i:
            c.load_weights(sp, s + 4, i)
            c.load_weights(sp, s + 5, i)
    for u in range(s + 4 + 2 * own, e + 4):
        c.load_weights(sp, u)


def split_u(c, eng, split, s, u, i, last, acc, per=BLOCKS):
    if last:
        n = u + 2 + 2 * i
        split(eng, n, 0, acc, per * (u + 2 * i - s + 1))
    else:
        split(eng, u + 2, i, acc, per * (u - s + 1) + 2 * per * i)



class Norm:

    def __init__(self, c, ctx, tag, bank0):
        self.c = c
        self.acc_ready = c.sem(tag + "_acc_ready")
        self.sum_ready = c.sem(tag + "_sum_ready")
        self.root_ready = c.sem(tag + "_root_ready")
        self.inv_ready = c.sem(tag + "_inv_ready")
        self.spread_ready = c.sem(tag + "_spread_ready")
        self.ps_sum = bank0
        self.ps_spread = [c.psum(f"{tag}_spread{b}", [P, 512], ctx) for b in range(BLOCKS)]
        self.root = c.sbuf(tag + "_root", [P, TT], F32, ctx)
        self.inv = c.sbuf(tag + "_inv", [P, TT], F32, ctx)

    def tensor(self, pe, acc):
        pe.wait_ge(self.acc_ready, 1)
        for t in range(TT):
            mm = pe.matmul(self.ps_sum[:, t:t + 1], acc[:, t * P:(t + 1) * P], self.c.ones[:, 0:1],
                           start=True, stop=True)
        mm.then_inc(self.sum_ready, 1)
        pe.wait_ge(self.inv_ready, 1)
        for t in range(TT):
            mm = pe.matmul(self.ps_spread[t // 3][:, (t % 3) * P:(t % 3 + 1) * P],
                           self.inv[:, t:t + 1].to_broadcast([P, P]), self.c.ident, start=True, stop=True)
        mm.then_inc(self.spread_ready, 1)

    def scalar(self, act):
        act.wait_ge(self.sum_ready, 1)
        self.c.nc.scalar.activation(self.root[:, :], self.ps_sum[:, 0:TT], AF.Sqrt, bias=self.c.eps[:, 0:1],
                                    scale=MODEL_SCALE).then_inc(self.root_ready, 1)

    def vector(self, dve):
        dve.wait_ge(self.root_ready, 1)
        self.c.nc.vector.reciprocal(self.inv[:, :], self.root[:, :]).then_inc(self.inv_ready, 1)
        dve.wait_ge(self.spread_ready, 1)


def normalise(c, ctx, tag, block_fns, norm, src, gain, ready=None):
    tmp = c.sbuf(tag + "_h", [P, 2, T], F32, ctx)
    h_ready, hi_ready, lo_ready = (c.sem(f"{tag}_{n}") for n in ("h_ready", "hi_ready", "lo_ready"))
    nc = c.nc

    def vector(dve):
        for j in range(KD):
            if j >= 2:
                dve.wait_ge(lo_ready, j - 1)
            for b in range(BLOCKS):
                ins = nc.vector.scalar_tensor_tensor(tmp[:, j % 2, blk(b)], src[:, j, blk(b)], gain(j),
                                                     norm.ps_spread[b][:, 0:BW], ALU.mult, ALU.mult)
            ins.then_inc(h_ready, 1)

    def scalar(act):
        for j in range(KD):
            act.wait_ge(h_ready, j + 1)
            nc.scalar.copy(c.x_hi[:, j, :], tmp[:, j % 2, :]).then_inc(hi_ready, 1)

    def gpsimd(pool):
        for j in range(KD):
            pool.wait_ge(hi_ready, j + 1)
            nc.gpsimd.tensor_tensor(c.x_lo[:, j, :], tmp[:, j % 2, :], c.x_hi[:, j, :],
                                    ALU.subtract).then_inc(lo_ready, 1)

    return vector, scalar, gpsimd


def stage_load(c, a):
    nc = c.nc
    with ExitStack() as ctx:
        consts_loaded = c.sem("consts_loaded")
        x_loaded = [c.sem(f"x_loaded{q}") for q in range(4)]
        eps_set, sq_ready, sq_used = c.sem("eps_set"), c.sem("sq_ready"), c.sem("sq_used")
        sq = c.sbuf("sq0", [P, 2, T], F32, ctx)
        bank0 = c.psum("n0_sum", [P, 512], ctx)
        norm = Norm(c, ctx, "n0", bank0)
        h_vector, h_scalar, h_gpsimd = normalise(c, ctx, "n0", None, norm, c.y, lambda j: c.gain(0, 0, j))
        block = ctx.enter_context(nc.Block())

        @block.sync
        def _(sp):
            for q in range(4):
                sp.dma_start(c.y[:, 2 * q:2 * q + 2, :], a["x"][:, 2 * q:2 * q + 2, :]).then_inc(x_loaded[q], 16)
            sp.dma_start(c.consts[:, :], a["consts"]).then_inc(consts_loaded, 16)
            sp.dma_start(c.gains[:, :], a["norm_g"]).then_inc(consts_loaded, 16)
            load_ring(c, sp, -4, 0)

        @block.scalar
        def _(act):
            for j in range(KD):
                act.wait_ge(x_loaded[j // 2], 16)
                if j >= 2:
                    act.wait_ge(sq_used, j - 1)
                nc.scalar.activation(sq[:, j % 2, :], c.y[:, j, :], AF.Square).then_inc(sq_ready, 1)
            c.split_hi(act, 0)
            c.split_hi(act, 1)
            act.wait_ge(eps_set, 1)
            norm.scalar(act)
            h_scalar(act)

        @block.vector
        def _(dve):
            nc.vector.memset(c.eps[:, :], EPS).then_inc(eps_set, 1)
            for j in range(KD):
                dve.wait_ge(sq_ready, j + 1)
                if j == 0:
                    nc.vector.tensor_copy(c.acc[:, :], sq[:, 0, :]).then_inc(sq_used, 1)
                else:
                    dve.wait_ge(sq_used, j)
                    ins = nc.vector.tensor_tensor(c.acc[:, :], c.acc[:, :], sq[:, j % 2, :], ALU.add)
                    ins.then_inc(sq_used if j < KD - 1 else norm.acc_ready, 1)
            c.split_lo(dve, 0)
            c.split_lo(dve, 1)
            dve.wait_ge(consts_loaded, 32)
            norm.vector(dve)
            h_vector(dve)

        @block.gpsimd
        def _(pool):
            h_gpsimd(pool)

        @block.tensor
        def _(pe):
            pe.wait_ge(consts_loaded, 32)
            norm.tensor(pe, c.acc)



def stage_qkv(c, a, s):
    nc, n, rot = c.nc, 6, 5
    with ExitStack() as ctx:
        tables = c.sbuf("rope_tables", [P, 2, T], F32, ctx)
        raw = c.sbuf("qkv_raw", [P, 3, BW], F32, ctx)
        part = c.sbuf("rope_parts", [P, 2, 2, BW], F32, ctx)
        bank = [c.psum(f"qkv{b}", [P, 512], ctx) for b in range(3)]
        swapped = [c.psum(f"swapped{b}", [P, 512], ctx) for b in range(3)]
        tables_loaded, kv_stored = c.sem("tables_loaded"), c.sem("kv_stored")
        acc_ready, raw_ready, swap_ready, v_ready = (c.sem(x) for x in
                                                     ("qkv_acc", "qkv_raw_ready", "qkv_swapped", "v_ready"))
        cos_done, sin_done, rope_done = c.sem("rope_cos"), c.sem("rope_sin"), c.sem("rope_done")
        block = ctx.enter_context(nc.Block())

        def q_parts(j, b):
            lo, hi = b * BW // CHUNK, min((b + 1) * BW, SEQ) // CHUNK
            parts = [(c.q_prompt[:, lo:hi, j, :], 0, (hi - lo) * CHUNK)]
            if b == BLOCKS - 1:
                parts.append((c.q_stream[:, :, j, :], (hi - lo) * CHUNK, BW))
            return parts

        @block.sync
        def _(sp):
            sp.dma_start(tables[:, :, :], a["rope"]).then_inc(tables_loaded, 16)
            load_ring(c, sp, s, s + n)
            sp.wait_ge(rope_done, 3 * rot)
            sp.wait_ge(v_ready, 3)
            sp.dma_start(a["kv_prompt"][0], c.k[:, SEQ - P:SEQ]).then_inc(kv_stored, 16)
            sp.dma_start(a["kv_prompt"][1], c.v[:, SEQ - P:SEQ]).then_inc(kv_stored, 16)
            sp.dma_start(a["kv_sample"][0], c.k[:, SEQ:T]).then_inc(kv_stored, 16)
            sp.dma_start(a["kv_sample"][1], c.v[:, SEQ:T]).then_inc(kv_stored, 16)
            sp.wait_ge(kv_stored, 64)

        @block.tensor
        def _(pe):
            def swap(m):
                pe.wait_ge(raw_ready, m + 1)
                if m >= 3:
                    pe.wait_ge(sin_done, m - 2)
                pe.matmul(swapped[m % 3][:, 0:BW], c.swap, raw[:, m % 3, :], start=True,
                          stop=True).then_inc(swap_ready, 1)

            for j in range(n):
                c.weights_split(pe, s + j)
                for b in range(BLOCKS):
                    m = 3 * j + b
                    if m >= 3:
                        pe.wait_ge(raw_ready, m - 2)
                    c.multiply(bank[b][:, 0:BW], s + j, KD, c.x_hi, c.x_lo, 0, blk(b), True, True
                               ).then_inc(acc_ready, 1)
                    if 1 <= m <= 3 * rot:
                        swap(m - 1)

        @block.scalar
        def _(act):
            for j in range(n):
                for b in range(BLOCKS):
                    m = 3 * j + b
                    act.wait_ge(acc_ready, m + 1)
                    if j < rot:
                        if m >= 3:
                            act.wait_ge(swap_ready, m - 2)
                            act.wait_ge(cos_done, m - 2)
                        nc.scalar.mul(raw[:, b, :], bank[b][:, 0:BW], 1 / WSCALE).then_inc(raw_ready, 1)
                    else:
                        nc.scalar.mul(c.v[:, blk(b)], bank[b][:, 0:BW], 1 / WSCALE).then_inc(v_ready, 1)
                c.split_hi(act, s + j + 2, 0, acc_ready, 3 * (j + 1))

        @block.vector
        def _(dve):
            dve.wait_ge(tables_loaded, 16)
            for j in range(n):
                for b in range(BLOCKS if j < rot else 0):
                    m = 3 * j + b
                    parts = q_parts(j, b) if j < rot - 1 else [(c.k[:, blk(b)], 0, BW)]
                    dve.wait_ge(raw_ready, m + 1)
                    if m >= 2:
                        dve.wait_ge(rope_done, m - 1)
                    nc.vector.tensor_tensor(part[:, 0, m % 2, :], raw[:, b, :], tables[:, 0, blk(b)],
                                            ALU.mult).then_inc(cos_done, 1)
                    dve.wait_ge(swap_ready, m + 1)
                    nc.vector.tensor_tensor(part[:, 1, m % 2, :], swapped[b][:, 0:BW], tables[:, 1, blk(b)],
                                            ALU.mult).then_inc(sin_done, 1)
                    dve.wait_ge(cos_done, m + 1)
                    dve.wait_ge(sin_done, m + 1)
                    for out, lo, hi in parts:
                        x, y = (part[:, k, m % 2, lo:hi] for k in range(2))
                        if len(out.shape) == 3:
                            x, y = (z.rearrange("p (n t) -> p n t", n=out.shape[1]) for z in (x, y))
                        ins = nc.vector.tensor_tensor(out, x, y, ALU.add)
                    ins.then_inc(rope_done, 1)
                c.split_lo(dve, s + j + 2, 0, acc_ready, 3 * (j + 1))


def sequences(view, hist):
    def prompt(shift):
        return view[:, shift:shift + SEQ]

    def streams(shift, n=STEP):
        rest = view[:, SEQ + hist:SEQ + hist + STREAMS * (STEP + hist)]
        return rest.rearrange("p (s t) -> p s t", s=STREAMS)[:, :, shift:shift + n]

    return prompt, streams


def by_stream(view):
    return view[:, SEQ:T].rearrange("p (s t) -> p s t", s=STREAMS)


def stage_conv(c, a, s):
    nc, n = c.nc, 4
    with ExitStack() as ctx:
        gate = c.sbuf("gate_c", [P, T], F32, ctx)
        u = c.sbuf("conv_in", [P, n, XW], F32, ctx)
        bank = [c.psum(f"cv{b}", [P, 512], ctx) for b in range(6)]
        taps = c.sbuf("sconv_taps", [P, 3, n], F32, ctx)
        hist_loaded, zeroed, taps_loaded = c.sem("shist_loaded"), c.sem("shist_zeroed"), c.sem("staps_loaded")
        acc_ready, gate_ready, u_ready, tap_done = (c.sem(x) for x in ("cv_acc", "gate_ready", "u_ready", "tap_done"))
        hist_stored = c.sem("shist_stored")
        block = ctx.enter_context(nc.Block())

        @block.sync
        def _(sp):
            sp.dma_start(taps[:, :, :], a["sconv_w"]).then_inc(taps_loaded, 16)
            for j in range(n):
                rest = u[:, j, SEQ + 2:XW].rearrange("p (s t) -> p s t", s=STREAMS)
                sp.dma_start(rest[:, :, 0:2], a["sconv_hist"][:, j, :, :]).then_inc(hist_loaded, 16)
            load_ring(c, sp, s, s + 2 * n)
            sp.wait_ge(u_ready, 4 * n)
            sp.dma_start(a["new_sconv"][:, :, 0, :], u[:, :, SEQ:SEQ + 2]).then_inc(hist_stored, 16)
            for j in range(n):
                rest = u[:, j, SEQ + 2:XW].rearrange("p (s t) -> p s t", s=STREAMS)
                sp.dma_start(a["new_sconv"][:, j, 1:1 + STREAMS, :], rest[:, :, STEP:STEP + 2]
                             ).then_inc(hist_stored, 16)
            sp.wait_ge(hist_stored, 16 * (n + 1))

        @block.tensor
        def _(pe):
            for j in range(2 * n):
                c.weights_split(pe, s + j)
                for b in range(BLOCKS):
                    if j >= 2:
                        pe.wait_ge(gate_ready if j % 2 == 0 else u_ready,
                                   3 * (j // 2 - 1) + b + 1 if j % 2 == 0 else 4 * (j // 2 - 1) + b + 1)
                    c.multiply(bank[3 * (j % 2) + b][:, 0:BW], s + j, KD, c.x_hi, c.x_lo, 0, blk(b), True, True
                               ).then_inc(acc_ready, 1)

        @block.scalar
        def _(act):
            for j in range(n):
                for b in range(BLOCKS):
                    act.wait_ge(acc_ready, 6 * j + b + 1)
                    if j >= 1:
                        act.wait_ge(u_ready, 4 * (j - 1) + (b + 1 if b < 2 else 4))
                    nc.scalar.mul(gate[:, blk(b)], bank[b][:, 0:BW], 1 / WSCALE).then_inc(gate_ready, 1)
                for k in range(2):
                    c.split_hi(act, s + 2 * j + 2 + k, 0, acc_ready, 3 * (2 * j + k + 1))

        @block.vector
        def _(dve):
            nc.vector.memset(u[:, :, 0:2], 0.0).then_inc(zeroed, 1)
            dve.wait_ge(taps_loaded, 16)
            dve.wait_ge(hist_loaded, 16 * n)
            dve.wait_ge(zeroed, 1)
            for j in range(n):
                prompt, streams = sequences(u[:, j, :], 2)
                for b in range(BLOCKS):
                    dve.wait_ge(acc_ready, 6 * j + 3 + b + 1)
                    dve.wait_ge(gate_ready, 3 * j + b + 1)
                    lo, hi = b * BW, min((b + 1) * BW, SEQ)
                    nc.vector.scalar_tensor_tensor(u[:, j, 2 + lo:2 + hi], bank[3 + b][:, 0:hi - lo], 1 / WSCALE,
                                                   gate[:, lo:hi], ALU.mult, ALU.mult).then_inc(u_ready, 1)
                nc.vector.scalar_tensor_tensor(
                    streams(2), bank[5][:, SEQ - 2 * BW:BW].rearrange("p (s t) -> p s t", s=STREAMS), 1 / WSCALE,
                    by_stream(gate[:, :]), ALU.mult, ALU.mult).then_inc(u_ready, 1)
                dve.wait_ge(u_ready, 4 * (j + 1))
                outs = c.conv[:, j, 0:SEQ], by_stream(c.conv[:, j, :])
                for tap in range(3):
                    if tap:
                        dve.wait_ge(tap_done, 6 * j + 2 * tap)
                    for out, seq in zip(outs, (prompt, streams)):
                        if tap == 0:
                            ins = nc.vector.tensor_scalar(out, seq(0), taps[:, 0, j:j + 1], None, ALU.mult)
                        else:
                            ins = nc.vector.scalar_tensor_tensor(out, seq(tap), taps[:, tap, j:j + 1], out,
                                                                 ALU.mult, ALU.add)
                        ins.then_inc(tap_done, 1)
                for k in range(2):
                    c.split_lo(dve, s + 2 * j + 2 + k, 0, acc_ready, 3 * (2 * j + k + 1))
            dve.wait_ge(tap_done, 6 * n)


def stage_gate_b(c, a, s):
    nc, n = c.nc, 4
    with ExitStack() as ctx:
        prod = c.sbuf("gated", [P, 3, BW], F32, ctx)
        bank = [c.psum(f"gb{b}", [P, 512], ctx) for b in range(3)]
        acc_ready, prod_ready, hi_ready, lo_ready = (c.sem(x) for x in ("gb_acc", "gb_prod", "gb_hi", "gb_lo"))
        block = ctx.enter_context(nc.Block())

        @block.sync
        def _(sp):
            load_ring(c, sp, s, s + n)

        @block.tensor
        def _(pe):
            for j in range(n):
                c.weights_split(pe, s + j)
                for b in range(BLOCKS):
                    if j:
                        pe.wait_ge(prod_ready, 3 * (j - 1) + b + 1)
                    c.multiply(bank[b][:, 0:BW], s + j, KD, c.x_hi, c.x_lo, 0, blk(b), True, True
                               ).then_inc(acc_ready, 1)

        @block.vector
        def _(dve):
            for j in range(n):
                for b in range(BLOCKS):
                    m = 3 * j + b
                    dve.wait_ge(acc_ready, m + 1)
                    if m >= 3:
                        dve.wait_ge(lo_ready, m - 2)
                    nc.vector.scalar_tensor_tensor(prod[:, b, :], bank[b][:, 0:BW], 1 / WSCALE, c.conv[:, j, blk(b)],
                                                   ALU.mult, ALU.mult).then_inc(prod_ready, 1)
                c.split_lo(dve, s + j + 2, 0, acc_ready, 3 * (j + 1))

        @block.scalar
        def _(act):
            for j in range(n):
                for b in range(BLOCKS):
                    act.wait_ge(prod_ready, 3 * j + b + 1)
                    nc.scalar.copy(c.cat_hi[:, 4 + j, blk(b)], prod[:, b, :]).then_inc(hi_ready, 1)
                c.split_hi(act, s + j + 2, 0, acc_ready, 3 * (j + 1))

        @block.gpsimd
        def _(pool):
            for j in range(n):
                for b in range(BLOCKS):
                    pool.wait_ge(hi_ready, 3 * j + b + 1)
                    nc.gpsimd.tensor_tensor(c.cat_lo[:, 4 + j, blk(b)], prod[:, b, :], c.cat_hi[:, 4 + j, blk(b)],
                                            ALU.subtract).then_inc(lo_ready, 1)


def stage_attention(c, a):
    nc = c.nc
    scale = HD ** -0.5
    steps = [("prompt", n) for n in range(SEQ // CHUNK)] + [("stream", n) for n in range(STREAMS)]
    with ExitStack() as ctx:
        cache = c.sbuf("kv_cache", [P, 2, STREAMS, P], F32, ctx)
        sinks = c.sbuf("sinks", [P, 2, 8], F32, ctx)
        neg_sinks = c.sbuf("neg_sinks", [P, 2, 8], F32, ctx)
        prob = c.sbuf("prob", [P, 2, 4, 192], F32, ctx)
        prob_t = c.sbuf("prob_t", [P, 2, 2, 512], F32, ctx)
        vals = c.sbuf("vals", [P, 2, 2, P], F32, ctx)
        small = c.sbuf("softmax_small", [P, 2, 6, 4], F32, ctx)
        ps_s = [[c.psum(f"scores{p}{g}", [P, 512], ctx) for g in range(2)] for p in range(2)]
        ps_p = [c.psum(f"prob_t{n}", [P, 512], ctx) for n in range(2)]
        ps_v = c.psum("vals_t", [P, 512], ctx)
        ps_o = c.psum("attn_out", [P, 512], ctx)
        cache_loaded, sinks_loaded, neg_ready = c.sem("cache_loaded"), c.sem("sinks_loaded"), c.sem("neg_sinks_ready")
        s_ready, max_ready, cap_ready, negm_ready, sinkm_ready, exp_ready, sinke_ready = (
            c.sem("at_" + x) for x in ("scores", "max", "scaled", "negm", "sinkm", "exp", "sinke"))
        den_ready, inv_ready, prob_ready, pt_ready, pta_copied, ptb_copied = (
            c.sem("at_" + x) for x in ("den", "inv", "prob", "pt", "pta_copied", "ptb_copied"))
        v_ready, v_copied, o_ready, out_ready, hi_ready, lo_ready = (
            c.sem("at_" + x) for x in ("vt", "v_copied", "o", "out", "hi", "lo"))
        out = c.sbuf("attn_out_sb", [P, 2, 256], F32, ctx)
        block = ctx.enter_context(nc.Block())

        def shape(step):
            kind, n = step
            if kind == "stream":
                return STEP, 1, GROUP * STEP, P, STEP
            keys = CHUNK * min(n + 1, 3)
            return CHUNK, 2, 2 * CHUNK, min(keys, P), keys - min(keys, P)

        def token(step):
            kind, n = step
            return SEQ + STEP * n if kind == "stream" else CHUNK * n

        def first_key(step):
            return max(0, token(step) - 2 * CHUNK)

        @block.sync
        def _(sp):
            sp.dma_start(cache[:, 0], a["cache_k"]).then_inc(cache_loaded, 16)
            sp.dma_start(cache[:, 1], a["cache_v"]).then_inc(cache_loaded, 16)
            sp.dma_start(sinks[:, :, :], a["sinks"]).then_inc(sinks_loaded, 16)

        @block.tensor
        def _(pe):
            def front(i):
                step = steps[i]
                nq, units, rows, na, nb = shape(step)
                t0, k0 = token(step), first_key(step)
                if i >= 2:
                    pe.wait_ge(exp_ready, i - 1)
                if step == ("stream", 0):
                    pe.wait_ge(cache_loaded, 32)
                for g in range(2):
                    half = slice(64 * g, 64 * g + 64)
                    for w in range(units):
                        q = c.q_stream if step[0] == "stream" else c.q_prompt
                        lhs = q[half, step[1], w * 4 // units:(w + 1) * 4 // units, :].rearrange("p t q -> p (t q)")
                        o = ps_s[i % 2][g]
                        if step[0] == "stream":
                            pe.matmul(o[0:rows, 0:P], lhs, cache[half, 0, step[1], :], start=True, stop=True)
                            mm = pe.matmul(o[0:rows, P:P + nb], lhs, c.k[half, t0:t0 + nb], start=True, stop=True)
                        else:
                            mm = pe.matmul(o[0:rows, w * 192:w * 192 + na + nb], lhs, c.k[half, k0:k0 + na + nb],
                                           start=True, stop=True)
                mm.then_inc(s_ready, 1)
                if i >= 1:
                    pe.wait_ge(v_copied, i)
                if step[0] == "stream":
                    mm = pe.transpose(ps_v[0:nb, P:2 * P], c.v[:, t0:t0 + nb], c.ident)
                else:
                    mm = pe.transpose(ps_v[0:na, 0:P], c.v[:, k0:k0 + na], c.ident)
                    if nb:
                        mm = pe.transpose(ps_v[0:nb, P:2 * P], c.v[:, k0 + na:k0 + na + nb], c.ident)
                mm.then_inc(v_ready, 1)

            def back(i):
                step = steps[i]
                nq, units, rows, na, nb = shape(step)
                pe.wait_ge(prob_ready, i + 1)
                if i >= 1:
                    pe.wait_ge(pta_copied, i)
                    pe.wait_ge(ptb_copied, i)
                for n in range(2 * units):
                    mm = pe.transpose(ps_p[0][0:na, n * rows:(n + 1) * rows], prob[0:rows, i % 2, n, 0:na],
                                      c.ident[0:rows, 0:rows])
                    if nb:
                        mm = pe.transpose(ps_p[1][0:nb, n * rows:(n + 1) * rows], prob[0:rows, i % 2, n, na:na + nb],
                                          c.ident[0:rows, 0:rows])
                mm.then_inc(pt_ready, 1)
                pe.wait_ge(pta_copied, i + 1)
                pe.wait_ge(ptb_copied, i + 1)
                pe.wait_ge(v_copied, i + 1)
                if i >= 1:
                    pe.wait_ge(out_ready, i)
                for g in range(2):
                    half = slice(64 * g, 64 * g + 64)
                    for w in range(units):
                        n = g * units + w
                        o = ps_o[half, w * rows:(w + 1) * rows]
                        va = cache[:, 1, step[1], half] if step[0] == "stream" else vals[0:na, i % 2, 0, half]
                        mm = pe.matmul(o, va, prob_t[0:na, i % 2, 0, n * rows:(n + 1) * rows], start=True, stop=not nb)
                        if nb:
                            mm = pe.matmul(o, vals[0:nb, i % 2, 1, half],
                                           prob_t[0:nb, i % 2, 1, n * rows:(n + 1) * rows], start=False, stop=True)
                mm.then_inc(o_ready, 1)

            for i in range(len(steps) + 1):
                if i < len(steps):
                    front(i)
                if i >= 1:
                    back(i - 1)

        @block.vector
        def _(dve):
            dve.wait_ge(sinks_loaded, 16)
            nc.vector.tensor_scalar(neg_sinks[:, :, :], sinks[:, :, :], -1.0, None, ALU.mult).then_inc(neg_ready, 1)
            dve.wait_ge(neg_ready, 1)

            def front(i):
                step = steps[i]
                nq, units, rows, na, nb = shape(step)
                kind = 1 if step[0] == "stream" else 0
                nu, p = 2 * units, i % 2
                dve.wait_ge(s_ready, i + 1)
                if i >= 2:
                    dve.wait_ge(prob_ready, i - 1)
                for g in range(2):
                    src = ps_s[p][g][0:rows, 0:192 * units].rearrange("p (w k) -> p w k", w=units)[:, :, 0:na + nb]
                    ins = nc.vector.reduce_max(small[0:rows, p, 0, g * units:(g + 1) * units], src, AX_X)
                ins.then_inc(max_ready, 1)
                dve.wait_ge(max_ready, i + 1)
                nc.vector.tensor_scalar(small[0:rows, p, 1, 0:nu], small[0:rows, p, 0, 0:nu], -scale, None,
                                        ALU.mult).then_inc(cap_ready, 1)
                dve.wait_ge(cap_ready, i + 1)
                nc.vector.tensor_tensor(small[0:rows, p, 2, 0:nu], small[0:rows, p, 1, 0:nu],
                                        neg_sinks[0:rows, kind, 0:nu], ALU.min).then_inc(negm_ready, 1)
                dve.wait_ge(negm_ready, i + 1)
                nc.vector.tensor_tensor(small[0:rows, p, 3, 0:nu], small[0:rows, p, 2, 0:nu],
                                        sinks[0:rows, kind, 0:nu], ALU.add).then_inc(sinkm_ready, 1)
                dve.wait_ge(v_ready, i + 1)
                if i >= 2:
                    dve.wait_ge(o_ready, i - 1)
                if step[0] == "prompt":
                    ins = nc.vector.tensor_copy(vals[0:na, p, 0, :], ps_v[0:na, 0:P])
                if nb:
                    ins = nc.vector.tensor_copy(vals[0:nb, p, 1, :], ps_v[0:nb, P:2 * P])
                ins.then_inc(v_copied, 1)

            def back(i):
                step = steps[i]
                nq, units, rows, na, nb = shape(step)
                nu, p = 2 * units, i % 2
                dve.wait_ge(sinke_ready, i + 1)
                nc.vector.tensor_tensor(small[0:rows, p, 5, 0:nu], small[0:rows, p, 4, 0:nu], small[0:rows, p, 3, 0:nu],
                                        ALU.add).then_inc(den_ready, 1)
                dve.wait_ge(den_ready, i + 1)
                nc.vector.reciprocal(small[0:rows, p, 5, 0:nu], small[0:rows, p, 5, 0:nu]).then_inc(inv_ready, 1)
                dve.wait_ge(inv_ready, i + 1)
                nc.vector.tensor_tensor(prob[0:rows, p, 0:nu, 0:na + nb], prob[0:rows, p, 0:nu, 0:na + nb],
                                        small[0:rows, p, 5, 0:nu].unsqueeze(2).to_broadcast([rows, nu, na + nb]),
                                        ALU.mult).then_inc(prob_ready, 1)
                dve.wait_ge(pt_ready, i + 1)
                if nb:
                    nc.vector.tensor_copy(prob_t[0:nb, p, 1, 0:nu * rows], ps_p[1][0:nb, 0:nu * rows]
                                          ).then_inc(ptb_copied, 1)
                else:
                    nc.vector.sem_inc(ptb_copied, 1)
                dve.wait_ge(o_ready, i + 1)
                if i >= 2:
                    dve.wait_ge(lo_ready, i - 1)
                nc.vector.tensor_copy(out[:, p, 0:4 * nq], ps_o[:, 0:4 * nq]).then_inc(out_ready, 1)

            for i in range(len(steps) + 1):
                if i < len(steps):
                    front(i)
                if i >= 1:
                    back(i - 1)

        @block.scalar
        def _(act):
            def front(i):
                step = steps[i]
                nq, units, rows, na, nb = shape(step)
                nu, p = 2 * units, i % 2
                act.wait_ge(negm_ready, i + 1)
                if i >= 2:
                    act.wait_ge(pt_ready, i - 1)
                for n in range(nu):
                    w = n % units
                    ins = nc.scalar.activation(prob[0:rows, p, n, 0:na + nb],
                                               ps_s[p][n // units][0:rows, w * 192:w * 192 + na + nb],
                                               AF.Exp, bias=small[0:rows, p, 2, n:n + 1], scale=scale,
                                               accum_out=small[0:rows, p, 4, n:n + 1])
                ins.then_inc(exp_ready, 1)
                act.wait_ge(sinkm_ready, i + 1)
                nc.scalar.activation(small[0:rows, p, 3, 0:nu], small[0:rows, p, 3, 0:nu], AF.Exp
                                     ).then_inc(sinke_ready, 1)

            def back(i):
                step = steps[i]
                nq, units, rows, na, nb = shape(step)
                p, t0 = i % 2, token(step)
                act.wait_ge(pt_ready, i + 1)
                nc.scalar.copy(prob_t[0:na, p, 0, 0:2 * units * rows], ps_p[0][0:na, 0:2 * units * rows]
                               ).then_inc(pta_copied, 1)
                act.wait_ge(out_ready, i + 1)
                nc.scalar.copy(c.cat_hi[:, 0:4, t0:t0 + nq],
                               out[:, p, 0:4 * nq].rearrange("p (t q) -> p t q", t=4)).then_inc(hi_ready, 1)

            for i in range(len(steps) + 1):
                if i < len(steps):
                    front(i)
                if i >= 1:
                    back(i - 1)

        @block.gpsimd
        def _(pool):
            for i, step in enumerate(steps):
                nq, t0 = shape(step)[0], token(step)
                pool.wait_ge(hi_ready, i + 1)
                nc.gpsimd.tensor_tensor(c.cat_lo[:, 0:4, t0:t0 + nq],
                                        out[:, i % 2, 0:4 * nq].rearrange("p (t q) -> p t q", t=4),
                                        c.cat_hi[:, 0:4, t0:t0 + nq], ALU.subtract).then_inc(lo_ready, 1)



def stage_project_y(c, tag, s, per, k_tiles, x_hi, x_lo):
    nc = c.nc
    steps = KD * per // 2
    tiles = 2 // per
    with ExitStack() as ctx:
        sq = c.sbuf(tag + "_sq", [P, 3, BW], F32, ctx)
        bank = [c.psum(f"{tag}{b}", [P, 512], ctx) for b in range(3)]
        acc_ready, y_ready, sq_ready, sum_done = (c.sem(f"{tag}_{x}") for x in ("acc", "y", "sq", "sum"))
        block = ctx.enter_context(nc.Block())

        @block.sync
        def _(sp):
            load_ring(c, sp, s, s + KD * per)

        @block.tensor
        def _(pe):
            def body(i, first, last):
                for j in range(2):
                    begins = per == 1 or j == 0
                    c.weights_split(pe, s + j, i)
                    for b in range(BLOCKS):
                        m = (3 * (j if per == 1 else 0) + b) - 3
                        if begins and not (first and m < 0):
                            pe.wait_ge(sq_ready, m + 1 + 3 * tiles * i)
                        c.multiply(bank[b][:, 0:BW], s + j, k_tiles, x_hi, x_lo,
                                   0 if per == 1 else j * k_tiles, blk(b), begins, per == 1 or j == 1
                                   ).then_inc(acc_ready, 1)

            run(pe, steps, body)

        @block.scalar
        def _(act):
            def body(i, first, last):
                for j in range(2):
                    if per == 1 or j == 1:
                        t = j if per == 1 else 0
                        for b in range(BLOCKS):
                            m = 3 * t + b
                            act.wait_ge(acc_ready, 3 * j + b + 1 + 6 * i)
                            nc.scalar.mul(c.y[:, ds(tiles * i + t, 1), blk(b)], bank[b][:, 0:BW].unsqueeze(1),
                                          1 / WSCALE).then_inc(y_ready, 1)
                            if not (first and m < 3):
                                act.wait_ge(sum_done, m - 2 + 3 * tiles * i)
                            nc.scalar.activation(sq[:, b, :], bank[b][:, 0:BW], AF.Square, scale=1 / WSCALE
                                                 ).then_inc(sq_ready, 1)
                    split_u(c, act, c.split_hi, s, s + j, i, last, acc_ready)

            run(act, steps, body)

        @block.vector
        def _(dve):
            def body(i, first, last):
                for j in range(2):
                    if per == 1 or j == 1:
                        t = j if per == 1 else 0
                        for b in range(BLOCKS):
                            m = 3 * t + b
                            dve.wait_ge(sq_ready, m + 1 + 3 * tiles * i)
                            if first and t == 0:
                                nc.vector.tensor_copy(c.acc[:, blk(b)], sq[:, b, :]).then_inc(sum_done, 1)
                            else:
                                dve.wait_ge(sum_done, m - 2 + 3 * tiles * i)
                                nc.vector.tensor_tensor(c.acc[:, blk(b)], c.acc[:, blk(b)], sq[:, b, :], ALU.add
                                                        ).then_inc(sum_done, 1)
                    split_u(c, dve, c.split_lo, s, s + j, i, last, acc_ready)

            run(dve, steps, body)


def stage_residual(c, tag, layer, which, x_in, x_out, final):
    nc = c.nc
    with ExitStack() as ctx:
        xr = c.sbuf(tag + "_x", [P, 2, T], F32, ctx)
        sq = c.sbuf(tag + "_sq", [P, 2, T], F32, ctx)
        bank = c.psum(tag + "_sum", [P, 512], ctx)
        post = Norm(c, ctx, tag + "p", bank)
        x_loaded = [c.sem(f"{tag}_x_loaded{k}") for k in range(2)]
        scaled, x_ready, sq_ready, sum_done, x_stored = (
            c.sem(f"{tag}_{x}") for x in ("scaled", "x_ready", "sq_ready", "sum", "stored"))
        if not final:
            nxt = (layer, 2) if which == 1 else (layer + 1, 0)
            pre = NormReuse(c, ctx, tag + "n", post)
            h_vector, h_scalar, h_gpsimd = normalise(c, ctx, tag, None, pre, c.y, lambda j: c.gain(*nxt, j))
        block = ctx.enter_context(nc.Block())

        @block.sync
        def _(sp):
            for j in range(KD):
                if j >= 2:
                    sp.wait_ge(x_ready, j - 1)
                sp.dma_start(xr[:, j % 2, :], x_in[:, j, :]).then_inc(x_loaded[j % 2], 16)
            for j in range(KD):
                sp.wait_ge(x_ready, j + 1)
                sp.dma_start(x_out[:, j, :], c.y[:, j, :]).then_inc(x_stored, 16)
            sp.wait_ge(x_stored, 16 * KD)

        @block.tensor
        def _(pe):
            post.tensor(pe, c.acc)
            if not final:
                pre.tensor(pe, c.acc)

        @block.vector
        def _(dve):
            nc.vector.sem_inc(post.acc_ready, 1)
            post.vector(dve)
            for j in range(KD):
                for b in range(BLOCKS):
                    ins = nc.vector.tensor_tensor(c.y[:, j, blk(b)], c.y[:, j, blk(b)], post.ps_spread[b][:, 0:BW],
                                                  ALU.mult)
                ins.then_inc(scaled, 1)
                dve.wait_ge(scaled, j + 1)
                dve.wait_ge(x_loaded[j % 2], 16 * (j // 2 + 1))
                nc.vector.scalar_tensor_tensor(c.y[:, j, :], c.y[:, j, :], c.gain(layer, which, j), xr[:, j % 2, :],
                                               ALU.mult, ALU.add).then_inc(x_ready, 1)
            if not final:
                pre.vector(dve)
                h_vector(dve)

        @block.scalar
        def _(act):
            post.scalar(act)
            if not final:
                for j in range(KD):
                    act.wait_ge(x_ready, j + 1)
                    if j >= 2:
                        act.wait_ge(sum_done, j - 1)
                    nc.scalar.activation(sq[:, j % 2, :], c.y[:, j, :], AF.Square).then_inc(sq_ready, 1)
                pre.scalar(act)
                h_scalar(act)

        @block.gpsimd
        def _(pool):
            if final:
                return
            pool.wait_ge(post.sum_ready, 1)
            for j in range(KD):
                pool.wait_ge(sq_ready, j + 1)
                if j:
                    pool.wait_ge(sum_done, j)
                if j == 0:
                    nc.gpsimd.tensor_copy(c.acc[:, :], sq[:, 0, :]).then_inc(sum_done, 1)
                else:
                    nc.gpsimd.tensor_tensor(c.acc[:, :], c.acc[:, :], sq[:, j % 2, :], ALU.add
                                            ).then_inc(sum_done if j < KD - 1 else pre.acc_ready, 1)
            h_gpsimd(pool)


class NormReuse(Norm):

    def __init__(self, c, ctx, tag, other):
        self.c = c
        self.acc_ready, self.sum_ready, self.root_ready, self.inv_ready, self.spread_ready = (
            c.sem(f"{tag}_{x}") for x in ("acc_ready", "sum_ready", "root_ready", "inv_ready", "spread_ready"))
        self.ps_sum, self.ps_spread = other.ps_sum, other.ps_spread
        self.root, self.inv = c.sbuf(tag + "_root", [P, TT], F32, ctx), c.sbuf(tag + "_inv", [P, TT], F32, ctx)



def stage_gate_up(c, tag, s, mid_hi, mid_lo):
    nc = c.nc
    with ExitStack() as ctx:
        sil = c.sbuf(tag + "_silu", [P, 3, BW], F32, ctx)
        mid = c.sbuf(tag + "_mid", [P, 3, BW], F32, ctx)
        bank = [c.psum(f"{tag}{b}", [P, 512], ctx) for b in range(6)]
        acc_ready, sil_ready, mid_ready, hi_ready, lo_ready = (
            c.sem(f"{tag}_{x}") for x in ("acc", "sil", "mid", "hi", "lo"))
        block = ctx.enter_context(nc.Block())

        @block.sync
        def _(sp):
            load_ring(c, sp, s, s + 2 * FT)

        @block.tensor
        def _(pe):
            def body(i, first, last):
                for j, used in enumerate((sil_ready, mid_ready)):
                    c.weights_split(pe, s + j, i)
                    for b in range(BLOCKS):
                        if not first:
                            pe.wait_ge(used, b - 2 + 3 * i)
                        c.multiply(bank[3 * j + b][:, 0:BW], s + j, KD, c.x_hi, c.x_lo, 0, blk(b), True, True
                                   ).then_inc(acc_ready, 1)

            run(pe, FT, body)

        @block.scalar
        def _(act):
            def body(i, first, last):
                for b in range(BLOCKS):
                    act.wait_ge(acc_ready, b + 1 + 6 * i)
                    if not first:
                        act.wait_ge(mid_ready, b - 2 + 3 * i)
                    nc.scalar.activation(sil[:, b, :], bank[b][:, 0:BW], AF.Silu, scale=1 / WSCALE
                                         ).then_inc(sil_ready, 1)
                split_u(c, act, c.split_hi, s, s, i, last, acc_ready)
                for b in range(BLOCKS):
                    act.wait_ge(mid_ready, b + 1 + 3 * i)
                    nc.scalar.copy(mid_hi[:, ds(i, 1), blk(b)], mid[:, b, :].unsqueeze(1)).then_inc(hi_ready, 1)
                split_u(c, act, c.split_hi, s, s + 1, i, last, acc_ready)

            run(act, FT, body)

        @block.vector
        def _(dve):
            def body(i, first, last):
                split_u(c, dve, c.split_lo, s, s, i, last, acc_ready)
                for b in range(BLOCKS):
                    dve.wait_ge(acc_ready, 3 + b + 1 + 6 * i)
                    dve.wait_ge(sil_ready, b + 1 + 3 * i)
                    if not first:
                        dve.wait_ge(lo_ready, b - 2 + 3 * i)
                    nc.vector.scalar_tensor_tensor(mid[:, b, :], bank[3 + b][:, 0:BW], 1 / WSCALE, sil[:, b, :],
                                                   ALU.mult, ALU.mult).then_inc(mid_ready, 1)
                split_u(c, dve, c.split_lo, s, s + 1, i, last, acc_ready)

            run(dve, FT, body)

        @block.gpsimd
        def _(pool):
            with pool.Fori(0, FT) as i:
                for b in range(BLOCKS):
                    pool.wait_ge(hi_ready, b + 1 + 3 * i)
                    nc.gpsimd.tensor_tensor(mid_lo[:, ds(i, 1), blk(b)], mid[:, b, :].unsqueeze(1),
                                            mid_hi[:, ds(i, 1), blk(b)], ALU.subtract).then_inc(lo_ready, 1)


def feed_forward(c, tag, s, layer, x_in, x_out, final):
    with ExitStack() as ctx:
        mid_hi = c.sbuf(tag + "_mid_hi", [P, FT, T], F16, ctx)
        mid_lo = c.sbuf(tag + "_mid_lo", [P, FT, T], F16, ctx)
        stage_gate_up(c, tag + "_gu", s, mid_hi, mid_lo)
        c.end_stage()
        stage_project_y(c, tag + "_dn", s + 2 * FT, 2, DOWN_K, mid_hi, mid_lo)
        c.end_stage()
    stage_residual(c, tag + "_r", layer, 3, x_in, x_out, final)
    c.end_stage()



class SSM:

    def __init__(self, c, ctx):
        shape = [P, TT, SHEADS]
        self.dt, self.da, self.ea, self.dend = (c.sbuf("ssm_" + n, shape, F32, ctx) for n in ("dt", "da", "ea", "dend"))
        self.chunk_decay = c.sbuf("ssm_chunk_decay", [P, SEQ // P, SHEADS], F32, ctx)
        self.stream_decay = c.sbuf("ssm_stream_decay", [P, STREAMS, SHEADS], F32, ctx)
        self.d = c.sbuf("ssm_d", [P, SHEADS], F32, ctx)


def stage_dt(c, a, s, m):
    nc, n = c.nc, TT * SHEADS
    np_ = SEQ // P * SHEADS
    with ExitStack() as ctx:
        rows = c.sbuf("ssm_rows", [P, 3, SHEADS], F32, ctx)
        neg_a = c.sbuf("ssm_neg_a", [P, SHEADS], F32, ctx)
        work = c.sbuf("ssm_work", [P, 6, n], F32, ctx)
        by_s = c.sbuf("ssm_by_stream", [P, STREAMS, SHEADS], F32, ctx)
        ps_dt, ps_cum, ps_tot, ps_str = (c.psum("dt_" + x, [P, 512], ctx) for x in ("raw", "cum", "tot", "str"))
        rows_loaded, acc_ready, sums_ready = c.sem("ssm_rows_loaded"), c.sem("dt_acc"), c.sem("dt_sums")
        neg_abs, exp_done, u_ready, ln_done, da_ready, a_ready = (
            c.sem("dt_" + x) for x in ("neg_abs", "exp", "u", "ln", "da", "a"))
        step, diff_ready, decays = c.sem("dt_step"), c.sem("dt_diff"), c.sem("dt_decays")
        block = ctx.enter_context(nc.Block())

        def flat(t):
            return t[:, :, :].rearrange("p a b -> p (a b)")

        def w(k):
            return work[:, k, :]

        @block.sync
        def _(sp):
            sp.dma_start(rows[:, :, :], a["ssm_rows"]).then_inc(rows_loaded, 16)
            load_ring(c, sp, s, s + 1)

        @block.tensor
        def _(pe):
            c.weights_split(pe, s)
            wh = c.w_hi[:, s % 2, 0:KD * SHEADS].rearrange("p (k h) -> p k h", k=KD)
            wl = c.w_lo[:, s % 2, 0:KD * SHEADS].rearrange("p (k h) -> p k h", k=KD)
            for t in range(TT):
                out = ps_dt[:, t * SHEADS:(t + 1) * SHEADS]
                for k in range(KD):
                    xh, xl = (x[:, k, t * P:(t + 1) * P] for x in (c.x_hi, c.x_lo))
                    pe.matmul(out, xh, wh[:, k, :], start=(k == 0), stop=False)
                    pe.matmul(out, xl, wh[:, k, :], start=False, stop=False)
                    mm = pe.matmul(out, xh, wl[:, k, :], start=False, stop=(k == KD - 1))
                if t == TT - 1:
                    mm.then_inc(acc_ready, 1)
            pe.wait_ge(da_ready, 2)
            da = flat(m.da)
            pe.matmul(ps_cum[:, 0:np_], c.tri_incl, da[:, 0:np_], start=True, stop=True)
            pe.matmul(ps_cum[:, np_:n], c.tri_block, da[:, np_:n], start=True, stop=True)
            pe.matmul(ps_tot[:, 0:np_], c.ones, da[:, 0:np_], start=True, stop=True)
            pe.matmul(ps_tot[:, np_:n], c.block_ones, da[:, np_:n], start=True, stop=True)
            pe.matmul(ps_str[:, 0:STREAMS * SHEADS], c.ones, flat(by_s), start=True, stop=True
                      ).then_inc(sums_ready, 1)

        @block.vector
        def _(dve):
            v = nc.vector
            dve.wait_ge(rows_loaded, 16)
            dve.wait_ge(acc_ready, 1)
            bias = rows[:, 0, :].unsqueeze(1).to_broadcast([P, TT, SHEADS])
            v.scalar_tensor_tensor(w(0).rearrange("p (a b) -> p a b", a=TT),
                                   ps_dt[:, 0:n].rearrange("p (a b) -> p a b", a=TT), 1 / WSCALE, bias,
                                   ALU.mult, ALU.add).then_inc(step, 1)
            dve.wait_ge(step, 1)
            v.tensor_scalar(w(1), w(0), -1.0, None, ALU.mult).then_inc(step, 1)
            dve.wait_ge(step, 2)
            v.tensor_tensor(w(1), w(0), w(1), ALU.min).then_inc(neg_abs, 1)
            v.tensor_scalar(w(0), w(0), 0.0, None, ALU.max).then_inc(step, 1)
            dve.wait_ge(exp_done, 2)
            v.tensor_scalar(w(3), w(2), 1.0, None, ALU.add).then_inc(u_ready, 1)
            dve.wait_ge(u_ready, 1)
            v.tensor_scalar(w(4), w(3), -1.0, None, ALU.add).then_inc(step, 1)
            v.reciprocal(w(5), w(3)).then_inc(step, 1)
            dve.wait_ge(step, 5)
            v.tensor_tensor(w(4), w(2), w(4), ALU.subtract).then_inc(step, 1)
            dve.wait_ge(step, 6)
            v.tensor_tensor(w(4), w(4), w(5), ALU.mult).then_inc(step, 1)
            dve.wait_ge(step, 7)
            v.tensor_tensor(w(0), w(0), w(4), ALU.add).then_inc(step, 1)
            dve.wait_ge(step, 8)
            dve.wait_ge(ln_done, 1)
            v.tensor_tensor(flat(m.dt), w(0), w(1), ALU.add).then_inc(step, 1)
            v.tensor_scalar(neg_a[:, :], neg_a[:, :], -1.0, None, ALU.mult).then_inc(a_ready, 1)
            v.tensor_copy(m.d[:, :], rows[:, 2, :]).then_inc(step, 1)
            dve.wait_ge(step, 9)
            dve.wait_ge(a_ready, 1)
            v.tensor_tensor(m.da[:, :, :], m.dt[:, :, :], neg_a[:, :].unsqueeze(1).to_broadcast([P, TT, SHEADS]),
                            ALU.mult).then_inc(da_ready, 1)
            dve.wait_ge(da_ready, 1)
            v.tensor_tensor(by_s[:, :, :], m.da[:, TT - 1, :].unsqueeze(1).to_broadcast([P, STREAMS, SHEADS]),
                            c.stream_mask.unsqueeze(2).to_broadcast([P, STREAMS, SHEADS]), ALU.mult
                            ).then_inc(da_ready, 1)
            c.split_lo(dve, s + 2, 0, acc_ready, 1)
            dve.wait_ge(sums_ready, 1)
            v.tensor_copy(w(2), ps_cum[:, 0:n]).then_inc(step, 1)
            dve.wait_ge(step, 11)
            v.tensor_tensor(w(3), ps_tot[:, 0:n], w(2), ALU.subtract).then_inc(diff_ready, 1)

        @block.scalar
        def _(act):
            act.wait_ge(neg_abs, 1)
            nc.scalar.activation(w(2), w(1), AF.Exp).then_inc(exp_done, 1)
            nc.scalar.activation(neg_a[:, :], rows[:, 1, :], AF.Exp).then_inc(exp_done, 1)
            act.wait_ge(u_ready, 1)
            nc.scalar.activation(w(1), w(3), AF.Ln).then_inc(ln_done, 1)
            c.split_hi(act, s + 2, 0, acc_ready, 1)
            act.wait_ge(sums_ready, 1)
            nc.scalar.activation(flat(m.stream_decay), ps_str[:, 0:STREAMS * SHEADS], AF.Exp).then_inc(decays, 1)
            act.wait_ge(diff_ready, 1)
            nc.scalar.activation(flat(m.ea), ps_cum[:, 0:n], AF.Exp).then_inc(decays, 1)
            nc.scalar.activation(flat(m.chunk_decay), ps_tot[:, 0:np_], AF.Exp).then_inc(decays, 1)
            nc.scalar.activation(flat(m.dend), w(3), AF.Exp).then_inc(decays, 1)
            act.wait_ge(decays, 4)


def stage_ssm(c, a, s, m, g_hi, g_lo):
    nc = c.nc
    n_units, n_conv, n_z = 10, 6, 4
    with ExitStack() as ctx:
        sb = lambda name, shape, dt=F32: c.sbuf("ss_" + name, shape, dt, ctx)
        zs = sb("z", [P, n_z, T])
        pad = sb("pad", [P, 2, XW3])
        hist = sb("hist", [P, SG * n_conv, 1 + STREAMS, 3])
        taps = sb("taps", [P, 4, SG * n_conv])
        bias = sb("bias", [P, SG * n_conv])
        gains = sb("gains", [P, SG * 4])
        flat = pad[:, :, :].rearrange("p a b -> p (a b)")
        x_tok, xdt, decayed = (flat[:, k * GW:(k + 1) * GW] for k in range(3))
        b_tok, cbm = flat[:, 3 * GW:3 * GW + P], flat[:, 3 * GW + P:3 * GW + 2 * P]
        junk = flat[:, 3 * GW + 2 * P:3 * GW + 2 * P + GW // 2].bitcast(F16)
        xdec, yt = c.acc[:, 0:GW], c.acc[:, GW:2 * GW]
        state = sb("state", [P, 3, GW])
        ssq, root, inv = sb("ssq", [P, TT]), sb("root", [P, TT]), sb("inv", [P, TT])
        seg_l = c.y[:, 6, 0:SHPG * P].rearrange("p (h k) -> p h k", h=SHPG)
        e = c.y[:, 7, 0:SHPG * P].rearrange("p (h k) -> p h k", h=SHPG)
        ps_yo, ps_yd, ps_st = (c.psum("ss_" + x, [P, 512], ctx) for x in ("yo", "yd", "st"))
        ps_x, ps_z, ps_bc = (c.psum("ss_" + x, [P, 512], ctx) for x in ("x", "zt", "bc"))
        ps_seg = [c.psum(f"ss_seg{k}", [P, 512], ctx) for k in range(2)]
        bank = [ps_yo, ps_yd, ps_st]

        sem = lambda name: c.sem("ss_" + name)
        small_loaded, acc_ready = sem("small_loaded"), sem("acc")
        pad_ready, hist_put, hist_kept, tap_done, xbc_ready, z_ready = (
            sem(x) for x in ("pad", "hist_put", "hist_kept", "tap", "xbc", "z_ready"))
        xt_ready, x_copied, bc_ready, b_ready, cb_ready = (sem(x) for x in ("xt", "x_copied", "bcr", "b", "cb"))
        segl_ready, seg_ready, exp_ready, w_ready = (sem(x) for x in ("segl", "seg", "exp", "w"))
        xdt_ready, xd_ready, xdec_ready, zt_ready = (sem(x) for x in ("xdt_ready", "xd", "xdec", "zt_ready"))
        yo_ready, yo_used, yd_ready, yd_used, y_done, gated, sq_done = (
            sem(x) for x in ("yo_ready", "yo_used", "yd_ready", "yd_used", "y_done", "gated", "sq_done"))
        st_ready, dec_ready, h_ready = (sem(x) for x in ("st_ready", "dec", "h"))
        cm_zero, cm_ready, bm_ready = (sem(x) for x in ("cm_zero", "cm", "bm"))
        root_ready, inv_ready, yn_ready, t_ready, ghi_ready, glo_ready = (
            sem(x) for x in ("root_ready", "inv_ready", "yn", "t", "ghi", "glo"))
        state_loaded = [sem(f"state_loaded{r}") for r in range(3)]
        state_stored = [sem(f"state_stored{r}") for r in range(3)]
        hist_stored, waits_alone = sem("hist_stored"), sem("waits_alone")
        block = ctx.enter_context(nc.Block())

        def chunk(t):
            return slice(t * P, (t + 1) * P)

        def wait_ge(engine, semaphore, value):
            if not isinstance(value, int) or value > 0:
                engine.wait_ge(semaphore, value)

        def each_group(engine, body):
            body(0)
            with engine.Fori(1, SG) as g:
                body(g)

        def alone(engine):
            engine.sem_inc(waits_alone, 1)

        LAST = TT - 1
        PER_H = LAST + 1 + STREAMS
        ring = [(k + 1) % 3 for k in range(STREAMS)]
        uses = [ring.count(r) for r in range(3)]
        turn = [ring[:k].count(ring[k]) for k in range(STREAMS)]

        def of_heads(t, v):
            return v.unsqueeze(2).to_broadcast([P, SHPG, SHD])

        def heads(t):
            return t.rearrange("p (h d) -> p h d", h=SHPG)

        @block.sync
        def _(sp):
            sp.dma_start(hist[:, :, :, :], a["ssm_hist"]).then_inc(small_loaded, 16)
            sp.dma_start(taps[:, :, :], a["ssm_taps"]).then_inc(small_loaded, 16)
            sp.dma_start(bias[:, :], a["ssm_bias"]).then_inc(small_loaded, 16)
            sp.dma_start(gains[:, :], a["ssm_gains"]).then_inc(small_loaded, 16)

            def load_state(g, k):
                sp.dma_start(state[:, ring[k], :], a["state"][k, :, ds(g * GW, GW)]
                             ).then_inc(state_loaded[ring[k]], 16)

            def group(g):
                for j in range(n_units):
                    u = s + 4 + j
                    wait_ge(sp, c.w_hi_ready, u - 1 + n_units * g)
                    wait_ge(sp, c.w_lo_ready, u - 1 + n_units * g)
                    src = a["ssm_w"][ds(4 + j + n_units * g, 1), :, :].rearrange("a p c -> (a p) c")
                    sp.dma_start(c.w_raw[:, u % 2, 0:UNIT], src).then_inc(c.w_loaded[u % 2], 16)
                load_state(g, 0)
                load_state(g, 1)
                wait_ge(sp, h_ready, (LAST + 1) + PER_H * g)
                sp.dma_start(a["new_state_prompt"][:, ds(g * GW, GW)], state[:, 0, :]
                             ).then_inc(state_stored[0], 16)
                for k in range(STREAMS):
                    if k == 2:
                        wait_ge(sp, state_stored[0], 16 + 16 * (uses[0] + 1) * g)
                        load_state(g, 2)
                    wait_ge(sp, h_ready, (LAST + 2 + k) + PER_H * g)
                    r, extra = ring[k], 1 if ring[k] == 0 else 0
                    sp.dma_start(a["new_state"][k, :, ds(g * GW, GW)], state[:, r, :]).then_inc(state_stored[r], 16)
                    wait_ge(sp, state_stored[r], 16 * (turn[k] + 1 + extra) + 16 * (uses[r] + extra) * g)
                    alone(sp)
                    if k + 3 < STREAMS:
                        load_state(g, k + 3)

            each_group(sp, group)
            sp.wait_ge(hist_kept, SG * n_conv)
            sp.dma_start(a["new_ssm_hist"], hist[:, :, :, :]).then_inc(hist_stored, 16)
            sp.wait_ge(hist_stored, 16)

        @block.tensor
        def _(pe):
            def project(g):
                for j in range(n_units):
                    wait_ge(pe, c.w_hi_ready, s + j + 1 + n_units * g)
                    wait_ge(pe, c.w_lo_ready, s + j + 1 + n_units * g)
                    for b in range(BLOCKS):
                        if j == 0:
                            wait_ge(pe, (yo_used, yd_used, h_ready)[b], (TT * g, TT * g, PER_H * g)[b])
                        elif j <= n_conv:
                            wait_ge(pe, pad_ready, 4 * (j - 1) + (b + 1 if b < 2 else 4) + 4 * n_conv * g)
                        else:
                            wait_ge(pe, z_ready, 3 * (j - 1 - n_conv) + b + 1 + 3 * n_z * g)
                        c.multiply(bank[b][:, 0:BW], s + j, KD, c.x_hi, c.x_lo, 0, blk(b), True, True
                                   ).then_inc(acc_ready, 1)

            def chunk_front(g, t):
                v = TT * g + t
                cols = chunk(t)
                wait_ge(pe, x_copied, v)
                for j in range(4):
                    mm = pe.transpose(ps_x[:, j * P:(j + 1) * P], c.y[:, j, cols], c.ident)
                mm.then_inc(xt_ready, 1)
                wait_ge(pe, b_ready, v)
                wait_ge(pe, cb_ready, v)
                pe.transpose(ps_bc[:, 0:P], c.y[:, 4, cols], c.ident)
                pe.matmul(ps_bc[:, P:2 * P], c.y[:, 4, cols], c.y[:, 5, cols], start=True, stop=True
                          ).then_inc(bc_ready, 1)
                wait_ge(pe, segl_ready, v + 1)
                wait_ge(pe, exp_ready, v)
                for h in range(SHPG):
                    mm = pe.matmul(ps_seg[h // 4][:, (h % 4) * P:(h % 4 + 1) * P], seg_l[:, h, :], c.tri_incl,
                                   start=True, stop=True)
                mm.then_inc(seg_ready, 1)

            def chunk_back(g, t):
                v = TT * g + t
                cols = chunk(t)
                wait_ge(pe, gated, v)
                for j in range(4):
                    mm = pe.transpose(ps_z[:, j * P:(j + 1) * P], zs[:, j, cols], c.ident)
                mm.then_inc(zt_ready, 1)
                wait_ge(pe, w_ready, v + 1)
                wait_ge(pe, xdt_ready, v + 1)
                wait_ge(pe, yd_used, v)
                for h in range(SHPG):
                    mm = pe.matmul(ps_yd[:, h * SHD:(h + 1) * SHD], e[:, h, :], xdt[:, h * SHD:(h + 1) * SHD],
                                   start=True, stop=True)
                mm.then_inc(yd_ready, 1)
                wait_ge(pe, yo_used, v)
                wait_ge(pe, xdec_ready, v + 1)
                if t < LAST:
                    wait_ge(pe, h_ready, t + 1 + PER_H * g)
                    pe.matmul(ps_yo[:, :], c.y[:, 5, cols], state[:, 0, :], start=True, stop=True
                              ).then_inc(yo_ready, 1)
                    wait_ge(pe, b_ready, v + 1)
                    pe.matmul(ps_st[:, :], b_tok, xdec, start=True, stop=True).then_inc(st_ready, 1)
                    return
                wait_ge(pe, cm_ready, STREAMS + STREAMS * g)
                wait_ge(pe, bm_ready, 1 + g)
                for k in range(STREAMS):
                    r = ring[k]
                    wait_ge(pe, state_loaded[r], 16 * (turn[k] + 1) + 16 * uses[r] * g)
                    mm = pe.matmul(ps_yo[:, :], seg_l[:, k, :], state[:, r, :], start=(k == 0),
                                   stop=(k == STREAMS - 1))
                    if k == STREAMS - 1:
                        mm.then_inc(yo_ready, 1)
                    wait_ge(pe, h_ready, LAST + 1 + k + PER_H * g)
                    pe.matmul(ps_st[:, :], e[:, k, :], xdec, start=True, stop=True).then_inc(st_ready, 1)

            def turn_back(g):
                for j in range(4):
                    for q, tiles in enumerate(((0, 1, 2, 3), (4, 5, 6, 7), (8,))):
                        n = 3 * j + q
                        wait_ge(pe, glo_ready, max(0, n - 1) + 12 * g)
                        wait_ge(pe, yn_ready, tiles[-1] + 1 + TT * g)
                        for k, t in enumerate(tiles):
                            mm = pe.transpose((ps_x, ps_z)[n % 2][:, k * P:(k + 1) * P], c.y[:, j, chunk(t)], c.ident)
                        mm.then_inc(t_ready, 1)

            def group(g):
                project(g)
                wait_ge(pe, xbc_ready, n_conv + n_conv * g)
                wait_ge(pe, z_ready, 3 * n_z + 3 * n_z * g)
                wait_ge(pe, glo_ready, 12 * g)
                for t in range(TT + 1):
                    if t < TT:
                        chunk_front(g, t)
                    if t >= 1:
                        chunk_back(g, t - 1)
                turn_back(g)

            each_group(pe, group)

        @block.scalar
        def _(act):
            act.wait_ge(small_loaded, 64)
            def group(g):
                for j in range(n_conv + n_z):
                    for b in range(BLOCKS):
                        wait_ge(act, acc_ready, 3 * j + b + 1 + 3 * n_units * g)
                        if j < n_conv:
                            if j < 2 and b == 0:
                                wait_ge(act, t_ready, 12 * g)
                            elif b == 0:
                                wait_ge(act, tap_done, 8 * (j - 1) + 8 * n_conv * g)
                                wait_ge(act, hist_kept, j - 1 + n_conv * g)
                            lo, hi = b * BW, min((b + 1) * BW, SEQ)
                            nc.scalar.mul(pad[:, j % 2, 3 + lo:3 + hi], bank[b][:, 0:hi - lo], 1 / WSCALE
                                          ).then_inc(pad_ready, 1)
                        else:
                            if j == n_conv and b == 0:
                                wait_ge(act, zt_ready, TT * g)
                            nc.scalar.activation(zs[:, j - n_conv, blk(b)], bank[b][:, 0:BW], AF.Silu,
                                                 scale=1 / WSCALE).then_inc(z_ready, 1)
                    if j < n_conv:
                        _, streams = sequences(pad[:, j % 2, :], 3)
                        nc.scalar.mul(streams(3), bank[2][:, SEQ - 2 * BW:BW].rearrange("p (s t) -> p s t", s=STREAMS),
                                      1 / WSCALE).then_inc(pad_ready, 1)
                    if 1 <= j <= n_conv:
                        wait_ge(act, tap_done, 8 * j + 8 * n_conv * g)
                        nc.scalar.activation(c.y[:, j - 1, :], c.y[:, j - 1, :], AF.Silu,
                                             bias=bias[:, ds(n_conv * g + j - 1, 1)]).then_inc(xbc_ready, 1)
                    wait_ge(act, c.w_loaded[(s + j) % 2], 16 * ((s + j + 2) // 2 + 1) + 16 * (n_units // 2) * g)
                    nc.scalar.activation(c.w_hi[:, (s + j) % 2, 0:UNIT], c.w_raw[:, (s + j) % 2, 0:UNIT], AF.Copy,
                                         scale=WSCALE).then_inc(c.w_hi_ready, 1)
                wait_ge(act, hist_kept, n_conv + n_conv * g)
                for t in range(TT):
                    v = TT * g + t
                    wait_ge(act, xt_ready, v + 1)
                    wait_ge(act, xdt_ready, v)
                    wait_ge(act, y_done, v)
                    nc.scalar.copy(x_tok, ps_x[:, :]).then_inc(x_copied, 1)
                    wait_ge(act, seg_ready, v + 1)
                    wait_ge(act, yd_ready, v)
                    if t == 0:
                        wait_ge(act, st_ready, (LAST + STREAMS) * g)
                    for q in range(2):
                        ins = nc.scalar.activation(e[:, 4 * q:4 * q + 4, :],
                                                   ps_seg[q][:, :].rearrange("p (h k) -> p h k", h=4), AF.Exp)
                    ins.then_inc(exp_ready, 1)
                    wait_ge(act, gated, v + 1)
                    nc.scalar.activation(junk.rearrange("p (j k) -> p j k", j=4), c.y[:, 0:4, chunk(t)],
                                         AF.Square, accum_out=ssq[:, t:t + 1]).then_inc(sq_done, 1)
                wait_ge(act, sq_done, TT + TT * g)
                nc.scalar.activation(root[:, :], ssq[:, :], AF.Sqrt, bias=c.eps[:, 0:1], scale=1.0 / GW
                                     ).then_inc(root_ready, 1)
                for j in range(4):
                    for q, (lo, hi) in enumerate(((0, 512), (512, 1024), (1024, T))):
                        n = 3 * j + q
                        wait_ge(act, t_ready, n + 1 + 12 * g)
                        nc.scalar.activation(g_hi[:, ds(4 * g + j, 1), lo:hi],
                                             (ps_x, ps_z)[n % 2][:, 0:hi - lo].unsqueeze(1), AF.Copy,
                                             scale=gains[:, ds(4 * g + j, 1)]).then_inc(ghi_ready, 1)

            each_group(act, group)

        @block.vector
        def _(dve):
            v_ = nc.vector
            dve.wait_ge(small_loaded, 64)
            def group(g):
                wait_ge(dve, t_ready, 12 * g)
                for j in range(n_conv + n_z):
                    if j < n_conv:
                        wait_ge(dve, pad_ready, 4 * (j + 1) + 4 * n_conv * g)
                        wait_ge(dve, hist_put, j + 1 + n_conv * g)
                        seqs = sequences(pad[:, j % 2, :], 3)
                        outs = c.y[:, j, 0:SEQ], by_stream(c.y[:, j, :])
                        for tap in range(4):
                            wt = taps[:, tap, ds(n_conv * g + j, 1)]
                            if tap:
                                wait_ge(dve, tap_done, 8 * j + 2 * tap + 8 * n_conv * g)
                            for out, seq in zip(outs, seqs):
                                if tap == 0:
                                    ins = v_.tensor_scalar(out, seq(0), wt, None, ALU.mult)
                                else:
                                    ins = v_.scalar_tensor_tensor(out, seq(tap), wt, out, ALU.mult, ALU.add)
                                ins.then_inc(tap_done, 1)
                    wait_ge(dve, acc_ready, 3 * (j + 1) + 3 * n_units * g)
                    wait_ge(dve, c.w_hi_ready, s + j + 3 + n_units * g)
                    v_.scalar_tensor_tensor(c.w_lo[:, (s + j) % 2, 0:UNIT], c.w_raw[:, (s + j) % 2, 0:UNIT], WSCALE,
                                            c.w_hi[:, (s + j) % 2, 0:UNIT], ALU.mult, ALU.subtract
                                            ).then_inc(c.w_lo_ready, 1)
                for r in range(3):
                    wait_ge(dve, state_stored[r], 16 * (uses[r] + (r == 0)) * g)
                v_.memset(state[:, 0, :], 0.0).then_inc(h_ready, 1)

                def chunk_front(t):
                    v = TT * g + t
                    wait_ge(dve, bc_ready, v + 1)
                    if t:
                        wait_ge(dve, st_ready, t + (LAST + STREAMS) * g)
                    else:
                        wait_ge(dve, bm_ready, g)
                    v_.tensor_copy(b_tok, ps_bc[:, 0:P]).then_inc(b_ready, 1)
                    v_.tensor_tensor(cbm, ps_bc[:, P:2 * P], c.tri_incl if t < LAST else c.tri_block, ALU.mult
                                     ).then_inc(cb_ready, 1)
                    wait_ge(dve, cb_ready, v + 1)
                    wait_ge(dve, exp_ready, v + 1)
                    v_.tensor_tensor(e, e, cbm.unsqueeze(1).to_broadcast([P, SHPG, P]), ALU.mult
                                     ).then_inc(w_ready, 1)
                    wait_ge(dve, xdt_ready, v + 1)
                    v_.tensor_tensor(heads(xdec), heads(xdt), of_heads(t, m.dend[:, t, ds(SHPG * g, SHPG)]),
                                     ALU.mult).then_inc(xdec_ready, 1)

                def chunk_back(t):
                    v = TT * g + t
                    if t < LAST:
                        wait_ge(dve, st_ready, t + 1 + (LAST + STREAMS) * g)
                        wait_ge(dve, dec_ready, t + 1 + (LAST + STREAMS) * g)
                        v_.tensor_tensor(state[:, 0, :], decayed, ps_st[:, :], ALU.add).then_inc(h_ready, 1)
                    else:
                        for k in range(STREAMS):
                            wait_ge(dve, st_ready, t + 1 + k + (LAST + STREAMS) * g)
                            wait_ge(dve, dec_ready, t + 1 + k + (LAST + STREAMS) * g)
                            v_.tensor_tensor(state[:, ring[k], :], decayed, ps_st[:, :], ALU.add
                                             ).then_inc(h_ready, 1)
                    wait_ge(dve, yo_ready, v + 1)
                    wait_ge(dve, gated, v)
                    v_.tensor_tensor(heads(yt), heads(ps_yo[:, :]), of_heads(t, m.ea[:, t, ds(SHPG * g, SHPG)]),
                                     ALU.mult).then_inc(yo_used, 1)
                    wait_ge(dve, yo_used, v + 1)
                    wait_ge(dve, yd_ready, v + 1)
                    v_.tensor_tensor(yt, ps_yd[:, :], yt, ALU.add).then_inc(yd_used, 1)
                    wait_ge(dve, yd_used, v + 1)
                    wait_ge(dve, xd_ready, v + 1)
                    v_.tensor_tensor(yt, yt, x_tok, ALU.add).then_inc(y_done, 1)
                    wait_ge(dve, y_done, v + 1)
                    wait_ge(dve, zt_ready, v + 1)
                    v_.tensor_tensor(c.y[:, 0:4, chunk(t)], ps_z[:, :].rearrange("p (j k) -> p j k", j=4),
                                     yt.rearrange("p (j k) -> p j k", j=4), ALU.mult).then_inc(gated, 1)

                for t in range(TT):
                    chunk_front(t)
                    chunk_back(t)
                wait_ge(dve, root_ready, 1 + g)
                v_.reciprocal(inv[:, :], root[:, :]).then_inc(inv_ready, 1)
                wait_ge(dve, inv_ready, 1 + g)
                for t in range(TT):
                    yc = c.y[:, 0:4, chunk(t)]
                    v_.tensor_scalar(yc, yc, inv[:, t:t + 1], None, ALU.mult).then_inc(yn_ready, 1)
                for j in range(4):
                    for q, (lo, hi) in enumerate(((0, 512), (512, 1024), (1024, T))):
                        n = 3 * j + q
                        wait_ge(dve, ghi_ready, n + 1 + 12 * g)
                        v_.scalar_tensor_tensor(g_lo[:, ds(4 * g + j, 1), lo:hi],
                                                (ps_x, ps_z)[n % 2][:, 0:hi - lo].unsqueeze(1),
                                                gains[:, ds(4 * g + j, 1)], g_hi[:, ds(4 * g + j, 1), lo:hi],
                                                ALU.mult, ALU.subtract).then_inc(glo_ready, 1)

            each_group(dve, group)

        @block.gpsimd
        def _(pool):
            p_ = nc.gpsimd
            pool.wait_ge(small_loaded, 64)
            def group(g):
                for j in range(n_conv):
                    prompt, streams = sequences(pad[:, j % 2, :], 3)
                    row = n_conv * g + j
                    if j < 2:
                        wait_ge(pool, t_ready, 12 * g)
                    else:
                        wait_ge(pool, tap_done, 8 * (j - 1) + 8 * n_conv * g)
                    p_.tensor_copy(pad[:, j % 2, 0:3], hist[:, ds(row, 1), 0, :].rearrange("p a t -> p (a t)"))
                    p_.tensor_copy(streams(0, 3), hist[:, ds(row, 1), 1:1 + STREAMS, :]
                                   .rearrange("p a s t -> p (a s) t")).then_inc(hist_put, 1)
                    wait_ge(pool, pad_ready, 4 * (j + 1) + 4 * n_conv * g)
                    wait_ge(pool, hist_put, j + 1 + n_conv * g)
                    alone(pool)
                    p_.tensor_copy(hist[:, ds(row, 1), 0, :].rearrange("p a t -> p (a t)"),
                                   pad[:, j % 2, SEQ:SEQ + 3])
                    p_.tensor_copy(hist[:, ds(row, 1), 1:1 + STREAMS, :].rearrange("p a s t -> p (a s) t"),
                                   streams(STEP, 3)).then_inc(hist_kept, 1)
                for t in range(TT):
                    v = TT * g + t
                    if t:
                        wait_ge(pool, seg_ready, v)
                    else:
                        wait_ge(pool, yo_ready, v)
                    p_.tensor_tensor(seg_l, c.tri_strict.unsqueeze(1).to_broadcast([P, SHPG, P]),
                                     m.da[:, t, ds(SHPG * g, SHPG)].unsqueeze(2).to_broadcast([P, SHPG, P]),
                                     ALU.mult).then_inc(segl_ready, 1)
                    wait_ge(pool, x_copied, v + 1)
                    wait_ge(pool, yd_ready, v)
                    p_.tensor_tensor(heads(xdt), heads(x_tok),
                                     of_heads(t, m.dt[:, t, ds(SHPG * g, SHPG)]), ALU.mult).then_inc(xdt_ready, 1)
                    if t < LAST:
                        wait_ge(pool, h_ready, t + 1 + PER_H * g)
                        p_.tensor_tensor(heads(decayed), heads(state[:, 0, :]),
                                         of_heads(t, m.chunk_decay[:, t, ds(SHPG * g, SHPG)]), ALU.mult
                                         ).then_inc(dec_ready, 1)
                    wait_ge(pool, xdec_ready, v + 1)
                    wait_ge(pool, xdt_ready, v + 1)
                    alone(pool)
                    p_.tensor_tensor(heads(x_tok), heads(x_tok), of_heads(t, m.d[:, ds(SHPG * g, SHPG)]),
                                     ALU.mult).then_inc(xd_ready, 1)
                wait_ge(pool, seg_ready, TT + TT * g)
                alone(pool)
                p_.memset(seg_l, 0.0).then_inc(cm_zero, 1)
                wait_ge(pool, cm_zero, 1 + g)
                alone(pool)
                for k in range(STREAMS):
                    p_.tensor_copy(seg_l[:, k, k * STEP:(k + 1) * STEP],
                                   c.y[:, 5, SEQ + k * STEP:SEQ + (k + 1) * STEP]).then_inc(cm_ready, 1)
                wait_ge(pool, yd_ready, TT + TT * g)
                wait_ge(pool, b_ready, TT + TT * g)
                p_.tensor_tensor(e, b_tok.unsqueeze(1).to_broadcast([P, STREAMS, P]),
                                 c.stream_mask.unsqueeze(2).to_broadcast([P, STREAMS, P]), ALU.mult
                                 ).then_inc(bm_ready, 1)
                for k in range(STREAMS):
                    r = ring[k]
                    wait_ge(pool, state_loaded[r], 16 * (turn[k] + 1) + 16 * uses[r] * g)
                    wait_ge(pool, h_ready, LAST + 1 + k + PER_H * g)
                    p_.tensor_tensor(heads(decayed), heads(state[:, r, :]),
                                     of_heads(0, m.stream_decay[:, k, ds(SHPG * g, SHPG)]), ALU.mult
                                     ).then_inc(dec_ready, 1)

            each_group(pool, group)



MATRICES = ("ident", "ones", "swap", "tri_incl", "tri_strict", "tri_block", "block_ones")


def build(nc, a):
    c_ctx = ExitStack()
    with c_ctx as ctx:
        c = Core(nc, ctx, [(a["ab_w_in"], UNIT), (a["ab_w_out"], UNIT), (a["gate_up0"], UNIT),
                           (a["down0"], DOWN_K * P), (a["dt_w"], KD * SHEADS), (a["ssm_w"], UNIT),
                           (a["gate_up1"], UNIT), (a["down1"], DOWN_K * P)])
        starts = c.starts
        c.x_hi, c.x_lo = c.sbuf("x_hi", [P, KD, T], F16), c.sbuf("x_lo", [P, KD, T], F16)
        c.y = c.sbuf("y", [P, KD, T], F32)
        c.acc = c.sbuf("acc", [P, T], F32)
        c.eps = c.sbuf("eps", [P, 1], F32)
        c.consts = c.sbuf("consts", [P, len(MATRICES) * P + STREAMS], F32)
        c.gains = c.sbuf("gains", [P, 2 * 4 * KD], F32)
        (c.ident, c.ones, c.swap, c.tri_incl, c.tri_strict, c.tri_block, c.block_ones) = (
            c.consts[:, n * P:(n + 1) * P] for n in range(len(MATRICES)))
        c.stream_mask = c.consts[:, len(MATRICES) * P:]
        c.gain = lambda layer, which, j: c.gains[:, (layer * 4 + which) * KD + j:(layer * 4 + which) * KD + j + 1]
        x1, x2, x3 = a["x1"], a["x2"], a["x3"]

        stage_load(c, a)
        c.end_stage()
        with ExitStack() as mixer:
            c.cat_hi, c.cat_lo = (c.sbuf(n, [P, KD, T], F16, mixer) for n in ("cat_hi", "cat_lo"))
            with ExitStack() as heads:
                q = c.y[:, 0:4, :].rearrange("p j t -> p (j t)")
                c.q_prompt = q[:, 0:4 * SEQ].rearrange("p (n j q) -> p n j q", j=4, q=CHUNK)
                c.q_stream = q[:, 4 * SEQ:4 * T].rearrange("p (n j q) -> p n j q", j=4, q=STEP)
                c.k, c.v = c.y[:, 4, :], c.y[:, 5, :]
                stage_qkv(c, a, 0)
                c.end_stage()
                with ExitStack() as conv:
                    c.conv = c.sbuf("conv", [P, 4, T], F32, conv)
                    stage_conv(c, a, 6)
                    c.end_stage()
                    stage_gate_b(c, a, 14)
                    c.end_stage()
                stage_attention(c, a)
                c.end_stage()
            stage_project_y(c, "ao", starts[1], 1, KD, c.cat_hi, c.cat_lo)
            c.end_stage()
        stage_residual(c, "r0", 0, 1, a["x"], x1, False)
        c.end_stage()
        feed_forward(c, "f0", starts[2], 0, x1, x2, False)
        with ExitStack() as mixer:
            g_hi, g_lo = (c.sbuf(n, [P, 16, T], F16, mixer) for n in ("g_hi", "g_lo"))
            with ExitStack() as scan:
                m = SSM(c, scan)
                stage_dt(c, a, starts[4], m)
                c.end_stage()
                stage_ssm(c, a, starts[5], m, g_hi, g_lo)
                c.end_stage()
            stage_project_y(c, "so", starts[5] + 40, 2, KD, g_hi, g_lo)
            c.end_stage()
        stage_residual(c, "r1", 1, 1, x2, x3, False)
        c.end_stage()
        feed_forward(c, "f1", starts[6], 1, x3, a["y_out"], True)



def _units(w, k_tiles):
    k, n = w.shape
    w = w.reshape(k // (k_tiles * P), k_tiles, P, n // P, P)
    return w.transpose(3, 0, 2, 1, 4).reshape(-1, P, k_tiles * P)


def _features(x):
    t, f = x.shape
    return x.T.reshape(f // P, P, t).transpose(1, 0, 2)


def _constants():
    i = np.arange(P)
    same = (i[:, None] // STEP) == (i[None, :] // STEP)
    swap = np.zeros((P, P), np.float32)
    for r in range(P):
        d = r % HD
        if d < ROPE:
            swap[r - d + (d + ROPE // 2) % ROPE, r] = 1
    mats = [np.eye(P), np.ones((P, P)), swap, i[:, None] <= i[None, :], i[:, None] > i[None, :],
            (i[:, None] <= i[None, :]) & same, same, i[:, None] // STEP == np.arange(STREAMS)[None, :]]
    return np.concatenate([x.astype(np.float32) for x in mats], axis=1)


def _rope():
    half = ROPE // 2
    inv = np.power(np.float32(500000.0), -np.arange(half, dtype=np.float32) / np.float32(half)).astype(np.float32)
    pos = np.concatenate([np.arange(SEQ), np.tile(PAST + np.arange(STEP), STREAMS)]).astype(np.float32)
    ang = (inv[:, None] * pos[None, :]).astype(np.float32).astype(np.float64)
    cos, sin = np.ones((P, T)), np.zeros((P, T))
    for r in range(P):
        d = r % HD
        if d < ROPE:
            cos[r] = np.cos(ang[d % half])
            sin[r] = np.sin(ang[d % half]) * (-1 if d < half else 1)
    return np.stack([cos, sin], axis=1).astype(np.float32)


def _head_order(w, axis):
    w = np.moveaxis(w, axis, 0)
    w = w.reshape((2, GROUP, HD) + w.shape[1:]).swapaxes(0, 1).reshape((HEADS * HD,) + w.shape[1:])
    return np.moveaxis(w, 0, axis)


def _group_order(w):
    x, b, c = np.split(w, [SG * GW, SG * GW + SG * SN], axis=-1)
    lead = w.shape[:-1]
    parts = [y.reshape(lead + (SG, -1)) for y in (x, b, c)]
    return np.concatenate(parts, axis=-1)


def _arrays(i):
    f = np.ascontiguousarray
    out = {}
    tokens = np.concatenate([i["x_prompt"][0], i["x_sample"].reshape(STREAMS * STEP, D)])
    out["x"] = _features(tokens)
    out["consts"] = _constants()
    out["rope"] = _rope()
    out["norm_g"] = i["norm_g"].reshape(2 * 4 * KD, P).T
    w = i["ab_w_in"][0]
    q, rest = w[:, :HEADS * HD], w[:, HEADS * HD:]
    kv, gb, gc, hx = rest[:, :256], rest[:, 256:768], rest[:, 768:1280], rest[:, 1280:1792]
    pairs = np.stack([gc.reshape(D, 4, P), hx.reshape(D, 4, P)], axis=2).reshape(D, 1024)
    out["ab_w_in"] = _units(np.concatenate([_head_order(q, 1), kv, pairs, gb], axis=1), KD)
    w = i["ab_w_out"][0]
    out["ab_w_out"] = _units(np.concatenate([_head_order(w[:512], 0), w[512:]]), KD)
    out["sconv_w"] = i["sconv_w"][0].reshape(3, 4, P).transpose(2, 0, 1)
    out["sconv_hist"] = i["state_sconv"][0].reshape(STREAMS, 2, 4, P).transpose(3, 2, 0, 1)
    out["cache_k"] = i["cache_attn_k"][0].reshape(STREAMS, P, P).transpose(2, 0, 1)
    out["cache_v"] = i["cache_attn_v"][0].reshape(STREAMS, P, P).transpose(1, 0, 2)
    sinks = i["attn_sinks"][0].reshape(2, GROUP)
    prompt = np.repeat(sinks.reshape(4, 2), CHUNK, axis=1).T
    stream = np.concatenate([np.repeat(sinks, STEP, axis=1).T] * 2)
    both = np.zeros((P, 2, 8), np.float32)
    both[:, 0, :4], both[:, 1, :2] = prompt, stream
    out["sinks"] = both
    for layer in range(2):
        g, u = (i[n][layer].reshape(D, FT, 1, P) for n in ("ffn_w_gate", "ffn_w_up"))
        out[f"gate_up{layer}"] = _units(np.concatenate([g, u], axis=2).reshape(D, 2 * DFF), KD)
        out[f"down{layer}"] = _units(i["ffn_w_down"][layer], DOWN_K)
    w = i["ssm_w_in"][0]
    z, xbc, dt = np.split(w, [SG * GW, 2 * SG * GW + 2 * SG * SN], axis=1)
    out["dt_w"] = dt.reshape(KD, P, SHEADS).transpose(1, 0, 2).reshape(1, P, KD * SHEADS)
    grouped = np.concatenate([_group_order(xbc), z.reshape(D, SG, GW)], axis=-1).reshape(D, SG * 10 * P)
    out["ssm_w"] = np.concatenate([_units(grouped, KD), _units(i["ssm_w_out"][0], KD)])
    rows = np.stack([i["ssm_dt_bias"][0], i["ssm_a_log"][0], i["ssm_d"][0]])
    out["ssm_rows"] = np.repeat(rows[None], P, axis=0)
    out["ssm_taps"] = _group_order(i["ssm_conv_w"][0]).reshape(4, 24, P).transpose(2, 0, 1)
    out["ssm_bias"] = _group_order(i["ssm_conv_b"][0]).reshape(24, P).T
    hist = _group_order(i["state_ssm_conv"][0]).reshape(STREAMS, 3, 24, P).transpose(3, 2, 0, 1)
    out["ssm_hist"] = np.concatenate([np.zeros((P, 24, 1, 3), np.float32), hist], axis=2)
    out["ssm_gains"] = i["ssm_norm_g"][0].reshape(16, P).T
    out["state"] = i["state_ssm"][0].reshape(STREAMS, SHEADS * SHD, SN).transpose(0, 2, 1)
    return {k: f(v) for k, v in out.items()}


OUTS = {"y_out": (P, KD, T), "kv_prompt": (2, P, P), "kv_sample": (2, P, P), "new_sconv": (P, 4, 1 + STREAMS, 2),
        "new_ssm_hist": (P, 24, 1 + STREAMS, 3), "new_state_prompt": (P, SHEADS * SHD),
        "new_state": (STREAMS, P, SHEADS * SHD)}


def _results(r):
    y = r["y_out"].transpose(2, 1, 0).reshape(T, D)
    kvp = r["kv_prompt"].transpose(0, 2, 1).reshape(2, 1, 1, P, 2, HD)
    kvs = r["kv_sample"].transpose(0, 2, 1).reshape(2, 1, STREAMS, STEP, 2, HD)
    sc = r["new_sconv"].transpose(2, 3, 1, 0).reshape(1 + STREAMS, 2, 512)
    h = r["new_ssm_hist"].transpose(2, 3, 1, 0).reshape(1 + STREAMS, 3, SG, 6 * P)
    x, b, cc = (p.reshape(1 + STREAMS, 3, -1) for p in (h[..., :GW], h[..., GW:GW + SN], h[..., GW + SN:]))
    hist = np.concatenate([x, b, cc], axis=-1)
    sp = r["new_state_prompt"].T.reshape(1, 1, SHEADS, SHD, SN)
    ss = r["new_state"].transpose(0, 2, 1).reshape(1, STREAMS, SHEADS, SHD, SN)
    outs = (y[:SEQ].reshape(1, SEQ, D), y[SEQ:].reshape(STREAMS, STEP, D), kvp[0], kvp[1], sc[None, :1],
            hist[None, :1], sp, kvs[0], kvs[1], sc[None, 1:], hist[None, 1:], ss)
    return tuple(np.ascontiguousarray(o) for o in outs)


def kernel(**inputs):
    import concourse.bacc as bacc
    from concourse.bass_utils import run_bass_kernel_spmd

    arrays = _arrays({k: np.asarray(v) for k, v in inputs.items()})
    nc = bacc.Bacc("TRN2", target_bir_lowering=False, num_devices=1, dynamic_dma_scratch_size=1024)
    aps = {k: nc.dram_tensor("in_" + k, v.shape, F32, kind="ExternalInput").ap() for k, v in arrays.items()}
    aps |= {k: nc.dram_tensor("out_" + k, s, F32, kind="ExternalOutput").ap() for k, s in OUTS.items()}
    aps |= {k: nc.dram_tensor("mid_" + k, (P, KD, T), F32, kind="Internal").ap() for k in ("x1", "x2", "x3")}
    build(nc, aps)
    r = run_bass_kernel_spmd(nc, [{"in_" + k: v for k, v in arrays.items()}], core_ids=[0]).results[0]
    return _results({k: r["out_" + k] for k in OUTS})
```

```python
from contextlib import ExitStack

import numpy as np

import concourse.bass as bass
from concourse import mybir

F32, F16 = mybir.dt.float32, mybir.dt.float16
AF = mybir.ActivationFunctionType
ALU = mybir.AluOpType
AX_X = mybir.AxisListType.X
ds = bass.ds

P = 128
D, SEQ, STREAMS, STEP = 1024, 1024, 8, 16
T = SEQ + STREAMS * STEP
TT = T // P
BLOCKS, BW = 3, T // 3
KD = D // P
HEADS, GROUP, HD, CHUNK = 8, 4, 64, 64
PAST = 512
ROPE = HD // 4
DFF = 2816
FT = DFF // P
DOWN_K = FT // 2
SG, SHPG, SHD, SN = 4, 8, 64, 128
SHEADS = SG * SHPG
GW = SHPG * SHD
UNIT = KD * P
WSCALE = 64.0
EPS = 1e-6
MODEL_SCALE = 1.0 / D
XW = SEQ + 2 + STREAMS * (STEP + 2)
XW3 = SEQ + 3 + STREAMS * (STEP + 3)


def sizes(segment):
    return segment[0].shape[0], segment[1]


class Core:

    def __init__(self, nc, ctx, segments):
        self.nc, self.ctx = nc, ctx
        self.stage_sems = []
        self.segments = segments
        self.starts = [0]
        for w, _ in segments:
            self.starts.append(self.starts[-1] + w.shape[0])
        most = max(f for _, f in segments)
        self.w_raw = self.sbuf("w_raw", [P, 2, most], F32)
        self.w_hi = self.sbuf("w_hi", [P, 2, most], F16)
        self.w_lo = self.sbuf("w_lo", [P, 2, most], F16)
        self.w_loaded = [self.sem("w_loaded0"), self.sem("w_loaded1")]
        self.w_hi_ready = self.sem("w_hi_ready")
        self.w_lo_ready = self.sem("w_lo_ready")
        self.stage_sems = []

    def sbuf(self, name, shape, dtype, ctx=None):
        return (ctx or self.ctx).enter_context(self.nc.sbuf_tensor(name, shape, dtype))

    def psum(self, name, shape, ctx):
        return ctx.enter_context(self.nc.psum_tensor(name, shape, F32))

    def sem(self, name):
        self.stage_sems.append(self.nc.alloc_semaphore(name))
        return self.stage_sems[-1]

    def end_stage(self):
        self.nc.clear_and_free_semaphores(self.stage_sems)
        self.nc.all_engine_barrier()
        self.stage_sems = []

    def segment_of(self, u):
        n = max(k for k, s in enumerate(self.starts[:-1]) if s <= u)
        return self.segments[n], self.starts[n]


    def load_weights(self, sp, u, i=0):
        if u >= self.starts[-1]:
            return
        (w, cols), start = self.segment_of(u)
        if u >= 2:
            sp.wait_ge(self.w_hi_ready, u - 1 + 2 * i)
            sp.wait_ge(self.w_lo_ready, u - 1 + 2 * i)
        src = w[ds(u - start + 2 * i, 1), :, :].rearrange("a p c -> (a p) c") if not isinstance(i, int) \
            else w[u - start + 2 * i, :, :]
        sp.dma_start(self.w_raw[:, u % 2, 0:cols], src).then_inc(self.w_loaded[u % 2], 16)

    def split_hi(self, act, u, i=0, acc=None, acc_value=None):
        if u >= self.starts[-1]:
            return
        cols = self.segment_of(u)[0][1]
        act.wait_ge(self.w_loaded[u % 2], 16 * (u // 2 + 1) + 16 * i)
        if acc is not None:
            act.wait_ge(acc, acc_value)
        self.nc.scalar.activation(self.w_hi[:, u % 2, 0:cols], self.w_raw[:, u % 2, 0:cols], AF.Copy,
                                  scale=WSCALE).then_inc(self.w_hi_ready, 1)

    def split_lo(self, dve, u, i=0, acc=None, acc_value=None):
        if u >= self.starts[-1]:
            return
        cols = self.segment_of(u)[0][1]
        if acc is not None:
            dve.wait_ge(acc, acc_value)
        dve.wait_ge(self.w_hi_ready, u + 1 + 2 * i)
        self.nc.vector.scalar_tensor_tensor(self.w_lo[:, u % 2, 0:cols], self.w_raw[:, u % 2, 0:cols], WSCALE,
                                            self.w_hi[:, u % 2, 0:cols], ALU.mult, ALU.subtract
                                            ).then_inc(self.w_lo_ready, 1)

    def weights_split(self, pe, u, i=0):
        pe.wait_ge(self.w_hi_ready, u + 1 + 2 * i)
        pe.wait_ge(self.w_lo_ready, u + 1 + 2 * i)

    def multiply(self, out, u, k_tiles, x_hi, x_lo, k0, cols, first, last):
        for k in range(k_tiles):
            wh = self.w_hi[:, u % 2, k * P:(k + 1) * P]
            wl = self.w_lo[:, u % 2, k * P:(k + 1) * P]
            xh, xl = x_hi[:, k0 + k, cols], x_lo[:, k0 + k, cols]
            self.nc.tensor.matmul(out, wh, xh, start=(first and k == 0), stop=False)
            self.nc.tensor.matmul(out, wh, xl, start=False, stop=False)
            mm = self.nc.tensor.matmul(out, wl, xh, start=False, stop=(last and k == k_tiles - 1))
        return mm


def blk(b):
    return slice(b * BW, (b + 1) * BW)


def run(engine, n, body):
    body(0, True, n == 1)
    if n > 3:
        with engine.Fori(1, n - 1) as i:
            body(i, False, False)
    else:
        for i in range(1, n - 1):
            body(i, False, False)
    if n > 1:
        body(n - 1, False, True)


def load_ring(c, sp, s, e):
    own = max(0, e - s - 4) // 2
    if own > 0:
        with sp.Fori(0, own) as i:
            c.load_weights(sp, s + 4, i)
            c.load_weights(sp, s + 5, i)
    for u in range(s + 4 + 2 * own, e + 4):
        c.load_weights(sp, u)


def split_u(c, eng, split, s, u, i, last, acc, per=BLOCKS):
    if last:
        n = u + 2 + 2 * i
        split(eng, n, 0, acc, per * (u + 2 * i - s + 1))
    else:
        split(eng, u + 2, i, acc, per * (u - s + 1) + 2 * per * i)



class Norm:

    def __init__(self, c, ctx, tag, bank0):
        self.c = c
        self.acc_ready = c.sem(tag + "_acc_ready")
        self.sum_ready = c.sem(tag + "_sum_ready")
        self.root_ready = c.sem(tag + "_root_ready")
        self.inv_ready = c.sem(tag + "_inv_ready")
        self.spread_ready = c.sem(tag + "_spread_ready")
        self.ps_sum = bank0
        self.ps_spread = [c.psum(f"{tag}_spread{b}", [P, 512], ctx) for b in range(BLOCKS)]
        self.root = c.sbuf(tag + "_root", [P, TT], F32, ctx)
        self.inv = c.sbuf(tag + "_inv", [P, TT], F32, ctx)

    def tensor(self, pe, acc):
        pe.wait_ge(self.acc_ready, 1)
        for t in range(TT):
            mm = pe.matmul(self.ps_sum[:, t:t + 1], acc[:, t * P:(t + 1) * P], self.c.ones[:, 0:1],
                           start=True, stop=True)
        mm.then_inc(self.sum_ready, 1)
        pe.wait_ge(self.inv_ready, 1)
        for t in range(TT):
            mm = pe.matmul(self.ps_spread[t // 3][:, (t % 3) * P:(t % 3 + 1) * P],
                           self.inv[:, t:t + 1].to_broadcast([P, P]), self.c.ident, start=True, stop=True)
        mm.then_inc(self.spread_ready, 1)

    def scalar(self, act):
        act.wait_ge(self.sum_ready, 1)
        self.c.nc.scalar.activation(self.root[:, :], self.ps_sum[:, 0:TT], AF.Sqrt, bias=self.c.eps[:, 0:1],
                                    scale=MODEL_SCALE).then_inc(self.root_ready, 1)

    def vector(self, dve):
        dve.wait_ge(self.root_ready, 1)
        self.c.nc.vector.reciprocal(self.inv[:, :], self.root[:, :]).then_inc(self.inv_ready, 1)
        dve.wait_ge(self.spread_ready, 1)


def normalise(c, ctx, tag, block_fns, norm, src, gain, ready=None):
    tmp = c.sbuf(tag + "_h", [P, 2, T], F32, ctx)
    h_ready, hi_ready, lo_ready = (c.sem(f"{tag}_{n}") for n in ("h_ready", "hi_ready", "lo_ready"))
    nc = c.nc

    def vector(dve):
        for j in range(KD):
            if j >= 2:
                dve.wait_ge(lo_ready, j - 1)
            for b in range(BLOCKS):
                ins = nc.vector.scalar_tensor_tensor(tmp[:, j % 2, blk(b)], src[:, j, blk(b)], gain(j),
                                                     norm.ps_spread[b][:, 0:BW], ALU.mult, ALU.mult)
            ins.then_inc(h_ready, 1)

    def scalar(act):
        for j in range(KD):
            act.wait_ge(h_ready, j + 1)
            nc.scalar.copy(c.x_hi[:, j, :], tmp[:, j % 2, :]).then_inc(hi_ready, 1)

    def gpsimd(pool):
        for j in range(KD):
            pool.wait_ge(hi_ready, j + 1)
            nc.gpsimd.tensor_tensor(c.x_lo[:, j, :], tmp[:, j % 2, :], c.x_hi[:, j, :],
                                    ALU.subtract).then_inc(lo_ready, 1)

    return vector, scalar, gpsimd


def stage_load(c, a):
    nc = c.nc
    with ExitStack() as ctx:
        consts_loaded = c.sem("consts_loaded")
        x_loaded = [c.sem(f"x_loaded{q}") for q in range(4)]
        eps_set, sq_ready, sq_used = c.sem("eps_set"), c.sem("sq_ready"), c.sem("sq_used")
        sq = c.sbuf("sq0", [P, 2, T], F32, ctx)
        bank0 = c.psum("n0_sum", [P, 512], ctx)
        norm = Norm(c, ctx, "n0", bank0)
        h_vector, h_scalar, h_gpsimd = normalise(c, ctx, "n0", None, norm, c.y, lambda j: c.gain(0, 0, j))
        block = ctx.enter_context(nc.Block())

        @block.sync
        def _(sp):
            for q in range(4):
                sp.dma_start(c.y[:, 2 * q:2 * q + 2, :], a["x"][:, 2 * q:2 * q + 2, :]).then_inc(x_loaded[q], 16)
            sp.dma_start(c.consts[:, :], a["consts"]).then_inc(consts_loaded, 16)
            sp.dma_start(c.gains[:, :], a["norm_g"]).then_inc(consts_loaded, 16)
            load_ring(c, sp, -4, 0)

        @block.scalar
        def _(act):
            for j in range(KD):
                act.wait_ge(x_loaded[j // 2], 16)
                if j >= 2:
                    act.wait_ge(sq_used, j - 1)
                nc.scalar.activation(sq[:, j % 2, :], c.y[:, j, :], AF.Square).then_inc(sq_ready, 1)
            c.split_hi(act, 0)
            c.split_hi(act, 1)
            act.wait_ge(eps_set, 1)
            norm.scalar(act)
            h_scalar(act)

        @block.vector
        def _(dve):
            nc.vector.memset(c.eps[:, :], EPS).then_inc(eps_set, 1)
            for j in range(KD):
                dve.wait_ge(sq_ready, j + 1)
                if j == 0:
                    nc.vector.tensor_copy(c.acc[:, :], sq[:, 0, :]).then_inc(sq_used, 1)
                else:
                    dve.wait_ge(sq_used, j)
                    ins = nc.vector.tensor_tensor(c.acc[:, :], c.acc[:, :], sq[:, j % 2, :], ALU.add)
                    ins.then_inc(sq_used if j < KD - 1 else norm.acc_ready, 1)
            c.split_lo(dve, 0)
            c.split_lo(dve, 1)
            dve.wait_ge(consts_loaded, 32)
            norm.vector(dve)
            h_vector(dve)

        @block.gpsimd
        def _(pool):
            h_gpsimd(pool)

        @block.tensor
        def _(pe):
            pe.wait_ge(consts_loaded, 32)
            norm.tensor(pe, c.acc)



def stage_qkv(c, a, s):
    nc, n, rot = c.nc, 6, 5
    with ExitStack() as ctx:
        tables = c.sbuf("rope_tables", [P, 2, T], F32, ctx)
        raw = c.sbuf("qkv_raw", [P, 3, BW], F32, ctx)
        part = c.sbuf("rope_parts", [P, 2, 2, BW], F32, ctx)
        bank = [c.psum(f"qkv{b}", [P, 512], ctx) for b in range(3)]
        swapped = [c.psum(f"swapped{b}", [P, 512], ctx) for b in range(3)]
        tables_loaded, kv_stored = c.sem("tables_loaded"), c.sem("kv_stored")
        acc_ready, raw_ready, swap_ready, v_ready = (c.sem(x) for x in
                                                     ("qkv_acc", "qkv_raw_ready", "qkv_swapped", "v_ready"))
        cos_done, sin_done, rope_done = c.sem("rope_cos"), c.sem("rope_sin"), c.sem("rope_done")
        block = ctx.enter_context(nc.Block())

        def q_parts(j, b):
            lo, hi = b * BW // CHUNK, min((b + 1) * BW, SEQ) // CHUNK
            parts = [(c.q_prompt[:, lo:hi, j, :], 0, (hi - lo) * CHUNK)]
            if b == BLOCKS - 1:
                parts.append((c.q_stream[:, :, j, :], (hi - lo) * CHUNK, BW))
            return parts

        @block.sync
        def _(sp):
            sp.dma_start(tables[:, :, :], a["rope"]).then_inc(tables_loaded, 16)
            load_ring(c, sp, s, s + n)
            sp.wait_ge(rope_done, 3 * rot)
            sp.wait_ge(v_ready, 3)
            sp.dma_start(a["kv_prompt"][0], c.k[:, SEQ - P:SEQ]).then_inc(kv_stored, 16)
            sp.dma_start(a["kv_prompt"][1], c.v[:, SEQ - P:SEQ]).then_inc(kv_stored, 16)
            sp.dma_start(a["kv_sample"][0], c.k[:, SEQ:T]).then_inc(kv_stored, 16)
            sp.dma_start(a["kv_sample"][1], c.v[:, SEQ:T]).then_inc(kv_stored, 16)
            sp.wait_ge(kv_stored, 64)

        @block.tensor
        def _(pe):
            def swap(m):
                pe.wait_ge(raw_ready, m + 1)
                if m >= 3:
                    pe.wait_ge(sin_done, m - 2)
                pe.matmul(swapped[m % 3][:, 0:BW], c.swap, raw[:, m % 3, :], start=True,
                          stop=True).then_inc(swap_ready, 1)

            for j in range(n):
                c.weights_split(pe, s + j)
                for b in range(BLOCKS):
                    m = 3 * j + b
                    if m >= 3:
                        pe.wait_ge(raw_ready, m - 2)
                    c.multiply(bank[b][:, 0:BW], s + j, KD, c.x_hi, c.x_lo, 0, blk(b), True, True
                               ).then_inc(acc_ready, 1)
                    if 1 <= m <= 3 * rot:
                        swap(m - 1)

        @block.scalar
        def _(act):
            for j in range(n):
                for b in range(BLOCKS):
                    m = 3 * j + b
                    act.wait_ge(acc_ready, m + 1)
                    if j < rot:
                        if m >= 3:
                            act.wait_ge(swap_ready, m - 2)
                            act.wait_ge(cos_done, m - 2)
                        nc.scalar.mul(raw[:, b, :], bank[b][:, 0:BW], 1 / WSCALE).then_inc(raw_ready, 1)
                    else:
                        nc.scalar.mul(c.v[:, blk(b)], bank[b][:, 0:BW], 1 / WSCALE).then_inc(v_ready, 1)
                c.split_hi(act, s + j + 2, 0, acc_ready, 3 * (j + 1))

        @block.vector
        def _(dve):
            dve.wait_ge(tables_loaded, 16)
            for j in range(n):
                for b in range(BLOCKS if j < rot else 0):
                    m = 3 * j + b
                    parts = q_parts(j, b) if j < rot - 1 else [(c.k[:, blk(b)], 0, BW)]
                    dve.wait_ge(raw_ready, m + 1)
                    if m >= 2:
                        dve.wait_ge(rope_done, m - 1)
                    nc.vector.tensor_tensor(part[:, 0, m % 2, :], raw[:, b, :], tables[:, 0, blk(b)],
                                            ALU.mult).then_inc(cos_done, 1)
                    dve.wait_ge(swap_ready, m + 1)
                    nc.vector.tensor_tensor(part[:, 1, m % 2, :], swapped[b][:, 0:BW], tables[:, 1, blk(b)],
                                            ALU.mult).then_inc(sin_done, 1)
                    dve.wait_ge(cos_done, m + 1)
                    dve.wait_ge(sin_done, m + 1)
                    for out, lo, hi in parts:
                        x, y = (part[:, k, m % 2, lo:hi] for k in range(2))
                        if len(out.shape) == 3:
                            x, y = (z.rearrange("p (n t) -> p n t", n=out.shape[1]) for z in (x, y))
                        ins = nc.vector.tensor_tensor(out, x, y, ALU.add)
                    ins.then_inc(rope_done, 1)
                c.split_lo(dve, s + j + 2, 0, acc_ready, 3 * (j + 1))


def sequences(view, hist):
    def prompt(shift):
        return view[:, shift:shift + SEQ]

    def streams(shift, n=STEP):
        rest = view[:, SEQ + hist:SEQ + hist + STREAMS * (STEP + hist)]
        return rest.rearrange("p (s t) -> p s t", s=STREAMS)[:, :, shift:shift + n]

    return prompt, streams


def by_stream(view):
    return view[:, SEQ:T].rearrange("p (s t) -> p s t", s=STREAMS)


def stage_conv(c, a, s):
    nc, n = c.nc, 4
    with ExitStack() as ctx:
        gate = c.sbuf("gate_c", [P, T], F32, ctx)
        u = c.sbuf("conv_in", [P, n, XW], F32, ctx)
        bank = [c.psum(f"cv{b}", [P, 512], ctx) for b in range(6)]
        taps = c.sbuf("sconv_taps", [P, 3, n], F32, ctx)
        hist_loaded, zeroed, taps_loaded = c.sem("shist_loaded"), c.sem("shist_zeroed"), c.sem("staps_loaded")
        acc_ready, gate_ready, u_ready, tap_done = (c.sem(x) for x in ("cv_acc", "gate_ready", "u_ready", "tap_done"))
        hist_stored = c.sem("shist_stored")
        block = ctx.enter_context(nc.Block())

        @block.sync
        def _(sp):
            sp.dma_start(taps[:, :, :], a["sconv_w"]).then_inc(taps_loaded, 16)
            for j in range(n):
                rest = u[:, j, SEQ + 2:XW].rearrange("p (s t) -> p s t", s=STREAMS)
                sp.dma_start(rest[:, :, 0:2], a["sconv_hist"][:, j, :, :]).then_inc(hist_loaded, 16)
            load_ring(c, sp, s, s + 2 * n)
            sp.wait_ge(u_ready, 4 * n)
            sp.dma_start(a["new_sconv"][:, :, 0, :], u[:, :, SEQ:SEQ + 2]).then_inc(hist_stored, 16)
            for j in range(n):
                rest = u[:, j, SEQ + 2:XW].rearrange("p (s t) -> p s t", s=STREAMS)
                sp.dma_start(a["new_sconv"][:, j, 1:1 + STREAMS, :], rest[:, :, STEP:STEP + 2]
                             ).then_inc(hist_stored, 16)
            sp.wait_ge(hist_stored, 16 * (n + 1))

        @block.tensor
        def _(pe):
            for j in range(2 * n):
                c.weights_split(pe, s + j)
                for b in range(BLOCKS):
                    if j >= 2:
                        pe.wait_ge(gate_ready if j % 2 == 0 else u_ready,
                                   3 * (j // 2 - 1) + b + 1 if j % 2 == 0 else 4 * (j // 2 - 1) + b + 1)
                    c.multiply(bank[3 * (j % 2) + b][:, 0:BW], s + j, KD, c.x_hi, c.x_lo, 0, blk(b), True, True
                               ).then_inc(acc_ready, 1)

        @block.scalar
        def _(act):
            for j in range(n):
                for b in range(BLOCKS):
                    act.wait_ge(acc_ready, 6 * j + b + 1)
                    if j >= 1:
                        act.wait_ge(u_ready, 4 * (j - 1) + (b + 1 if b < 2 else 4))
                    nc.scalar.mul(gate[:, blk(b)], bank[b][:, 0:BW], 1 / WSCALE).then_inc(gate_ready, 1)
                for k in range(2):
                    c.split_hi(act, s + 2 * j + 2 + k, 0, acc_ready, 3 * (2 * j + k + 1))

        @block.vector
        def _(dve):
            nc.vector.memset(u[:, :, 0:2], 0.0).then_inc(zeroed, 1)
            dve.wait_ge(taps_loaded, 16)
            dve.wait_ge(hist_loaded, 16 * n)
            dve.wait_ge(zeroed, 1)
            for j in range(n):
                prompt, streams = sequences(u[:, j, :], 2)
                for b in range(BLOCKS):
                    dve.wait_ge(acc_ready, 6 * j + 3 + b + 1)
                    dve.wait_ge(gate_ready, 3 * j + b + 1)
                    lo, hi = b * BW, min((b + 1) * BW, SEQ)
                    nc.vector.scalar_tensor_tensor(u[:, j, 2 + lo:2 + hi], bank[3 + b][:, 0:hi - lo], 1 / WSCALE,
                                                   gate[:, lo:hi], ALU.mult, ALU.mult).then_inc(u_ready, 1)
                nc.vector.scalar_tensor_tensor(
                    streams(2), bank[5][:, SEQ - 2 * BW:BW].rearrange("p (s t) -> p s t", s=STREAMS), 1 / WSCALE,
                    by_stream(gate[:, :]), ALU.mult, ALU.mult).then_inc(u_ready, 1)
                dve.wait_ge(u_ready, 4 * (j + 1))
                outs = c.conv[:, j, 0:SEQ], by_stream(c.conv[:, j, :])
                for tap in range(3):
                    if tap:
                        dve.wait_ge(tap_done, 6 * j + 2 * tap)
                    for out, seq in zip(outs, (prompt, streams)):
                        if tap == 0:
                            ins = nc.vector.tensor_scalar(out, seq(0), taps[:, 0, j:j + 1], None, ALU.mult)
                        else:
                            ins = nc.vector.scalar_tensor_tensor(out, seq(tap), taps[:, tap, j:j + 1], out,
                                                                 ALU.mult, ALU.add)
                        ins.then_inc(tap_done, 1)
                for k in range(2):
                    c.split_lo(dve, s + 2 * j + 2 + k, 0, acc_ready, 3 * (2 * j + k + 1))
            dve.wait_ge(tap_done, 6 * n)


def stage_gate_b(c, a, s):
    nc, n = c.nc, 4
    with ExitStack() as ctx:
        prod = c.sbuf("gated", [P, 3, BW], F32, ctx)
        bank = [c.psum(f"gb{b}", [P, 512], ctx) for b in range(3)]
        acc_ready, prod_ready, hi_ready, lo_ready = (c.sem(x) for x in ("gb_acc", "gb_prod", "gb_hi", "gb_lo"))
        block = ctx.enter_context(nc.Block())

        @block.sync
        def _(sp):
            load_ring(c, sp, s, s + n)

        @block.tensor
        def _(pe):
            for j in range(n):
                c.weights_split(pe, s + j)
                for b in range(BLOCKS):
                    if j:
                        pe.wait_ge(prod_ready, 3 * (j - 1) + b + 1)
                    c.multiply(bank[b][:, 0:BW], s + j, KD, c.x_hi, c.x_lo, 0, blk(b), True, True
                               ).then_inc(acc_ready, 1)

        @block.vector
        def _(dve):
            for j in range(n):
                for b in range(BLOCKS):
                    m = 3 * j + b
                    dve.wait_ge(acc_ready, m + 1)
                    if m >= 3:
                        dve.wait_ge(lo_ready, m - 2)
                    nc.vector.scalar_tensor_tensor(prod[:, b, :], bank[b][:, 0:BW], 1 / WSCALE, c.conv[:, j, blk(b)],
                                                   ALU.mult, ALU.mult).then_inc(prod_ready, 1)
                c.split_lo(dve, s + j + 2, 0, acc_ready, 3 * (j + 1))

        @block.scalar
        def _(act):
            for j in range(n):
                for b in range(BLOCKS):
                    act.wait_ge(prod_ready, 3 * j + b + 1)
                    nc.scalar.copy(c.cat_hi[:, 4 + j, blk(b)], prod[:, b, :]).then_inc(hi_ready, 1)
                c.split_hi(act, s + j + 2, 0, acc_ready, 3 * (j + 1))

        @block.gpsimd
        def _(pool):
            for j in range(n):
                for b in range(BLOCKS):
                    pool.wait_ge(hi_ready, 3 * j + b + 1)
                    nc.gpsimd.tensor_tensor(c.cat_lo[:, 4 + j, blk(b)], prod[:, b, :], c.cat_hi[:, 4 + j, blk(b)],
                                            ALU.subtract).then_inc(lo_ready, 1)


def stage_attention(c, a):
    nc = c.nc
    scale = HD ** -0.5
    steps = [("prompt", n) for n in range(SEQ // CHUNK)] + [("stream", n) for n in range(STREAMS)]
    with ExitStack() as ctx:
        cache = c.sbuf("kv_cache", [P, 2, STREAMS, P], F32, ctx)
        sinks = c.sbuf("sinks", [P, 2, 8], F32, ctx)
        neg_sinks = c.sbuf("neg_sinks", [P, 2, 8], F32, ctx)
        prob = c.sbuf("prob", [P, 2, 4, 192], F32, ctx)
        prob_t = c.sbuf("prob_t", [P, 2, 2, 512], F32, ctx)
        vals = c.sbuf("vals", [P, 2, 2, P], F32, ctx)
        small = c.sbuf("softmax_small", [P, 2, 6, 4], F32, ctx)
        ps_s = [[c.psum(f"scores{p}{g}", [P, 512], ctx) for g in range(2)] for p in range(2)]
        ps_p = [c.psum(f"prob_t{n}", [P, 512], ctx) for n in range(2)]
        ps_v = c.psum("vals_t", [P, 512], ctx)
        ps_o = c.psum("attn_out", [P, 512], ctx)
        cache_loaded, sinks_loaded, neg_ready = c.sem("cache_loaded"), c.sem("sinks_loaded"), c.sem("neg_sinks_ready")
        s_ready, max_ready, cap_ready, negm_ready, sinkm_ready, exp_ready, sinke_ready = (
            c.sem("at_" + x) for x in ("scores", "max", "scaled", "negm", "sinkm", "exp", "sinke"))
        den_ready, inv_ready, prob_ready, pt_ready, pta_copied, ptb_copied = (
            c.sem("at_" + x) for x in ("den", "inv", "prob", "pt", "pta_copied", "ptb_copied"))
        v_ready, v_copied, o_ready, out_ready, hi_ready, lo_ready = (
            c.sem("at_" + x) for x in ("vt", "v_copied", "o", "out", "hi", "lo"))
        out = c.sbuf("attn_out_sb", [P, 2, 256], F32, ctx)
        block = ctx.enter_context(nc.Block())

        def shape(step):
            kind, n = step
            if kind == "stream":
                return STEP, 1, GROUP * STEP, P, STEP
            keys = CHUNK * min(n + 1, 3)
            return CHUNK, 2, 2 * CHUNK, min(keys, P), keys - min(keys, P)

        def token(step):
            kind, n = step
            return SEQ + STEP * n if kind == "stream" else CHUNK * n

        def first_key(step):
            return max(0, token(step) - 2 * CHUNK)

        @block.sync
        def _(sp):
            sp.dma_start(cache[:, 0], a["cache_k"]).then_inc(cache_loaded, 16)
            sp.dma_start(cache[:, 1], a["cache_v"]).then_inc(cache_loaded, 16)
            sp.dma_start(sinks[:, :, :], a["sinks"]).then_inc(sinks_loaded, 16)

        @block.tensor
        def _(pe):
            def front(i):
                step = steps[i]
                nq, units, rows, na, nb = shape(step)
                t0, k0 = token(step), first_key(step)
                if i >= 2:
                    pe.wait_ge(exp_ready, i - 1)
                if step == ("stream", 0):
                    pe.wait_ge(cache_loaded, 32)
                for g in range(2):
                    half = slice(64 * g, 64 * g + 64)
                    for w in range(units):
                        q = c.q_stream if step[0] == "stream" else c.q_prompt
                        lhs = q[half, step[1], w * 4 // units:(w + 1) * 4 // units, :].rearrange("p t q -> p (t q)")
                        o = ps_s[i % 2][g]
                        if step[0] == "stream":
                            pe.matmul(o[0:rows, 0:P], lhs, cache[half, 0, step[1], :], start=True, stop=True)
                            mm = pe.matmul(o[0:rows, P:P + nb], lhs, c.k[half, t0:t0 + nb], start=True, stop=True)
                        else:
                            mm = pe.matmul(o[0:rows, w * 192:w * 192 + na + nb], lhs, c.k[half, k0:k0 + na + nb],
                                           start=True, stop=True)
                mm.then_inc(s_ready, 1)
                if i >= 1:
                    pe.wait_ge(v_copied, i)
                if step[0] == "stream":
                    mm = pe.transpose(ps_v[0:nb, P:2 * P], c.v[:, t0:t0 + nb], c.ident)
                else:
                    mm = pe.transpose(ps_v[0:na, 0:P], c.v[:, k0:k0 + na], c.ident)
                    if nb:
                        mm = pe.transpose(ps_v[0:nb, P:2 * P], c.v[:, k0 + na:k0 + na + nb], c.ident)
                mm.then_inc(v_ready, 1)

            def back(i):
                step = steps[i]
                nq, units, rows, na, nb = shape(step)
                pe.wait_ge(prob_ready, i + 1)
                if i >= 1:
                    pe.wait_ge(pta_copied, i)
                    pe.wait_ge(ptb_copied, i)
                for n in range(2 * units):
                    mm = pe.transpose(ps_p[0][0:na, n * rows:(n + 1) * rows], prob[0:rows, i % 2, n, 0:na],
                                      c.ident[0:rows, 0:rows])
                    if nb:
                        mm = pe.transpose(ps_p[1][0:nb, n * rows:(n + 1) * rows], prob[0:rows, i % 2, n, na:na + nb],
                                          c.ident[0:rows, 0:rows])
                mm.then_inc(pt_ready, 1)
                pe.wait_ge(pta_copied, i + 1)
                pe.wait_ge(ptb_copied, i + 1)
                pe.wait_ge(v_copied, i + 1)
                if i >= 1:
                    pe.wait_ge(out_ready, i)
                for g in range(2):
                    half = slice(64 * g, 64 * g + 64)
                    for w in range(units):
                        n = g * units + w
                        o = ps_o[half, w * rows:(w + 1) * rows]
                        va = cache[:, 1, step[1], half] if step[0] == "stream" else vals[0:na, i % 2, 0, half]
                        mm = pe.matmul(o, va, prob_t[0:na, i % 2, 0, n * rows:(n + 1) * rows], start=True, stop=not nb)
                        if nb:
                            mm = pe.matmul(o, vals[0:nb, i % 2, 1, half],
                                           prob_t[0:nb, i % 2, 1, n * rows:(n + 1) * rows], start=False, stop=True)
                mm.then_inc(o_ready, 1)

            for i in range(len(steps) + 1):
                if i < len(steps):
                    front(i)
                if i >= 1:
                    back(i - 1)

        @block.vector
        def _(dve):
            dve.wait_ge(sinks_loaded, 16)
            nc.vector.tensor_scalar(neg_sinks[:, :, :], sinks[:, :, :], -1.0, None, ALU.mult).then_inc(neg_ready, 1)
            dve.wait_ge(neg_ready, 1)

            def front(i):
                step = steps[i]
                nq, units, rows, na, nb = shape(step)
                kind = 1 if step[0] == "stream" else 0
                nu, p = 2 * units, i % 2
                dve.wait_ge(s_ready, i + 1)
                if i >= 2:
                    dve.wait_ge(prob_ready, i - 1)
                for g in range(2):
                    src = ps_s[p][g][0:rows, 0:192 * units].rearrange("p (w k) -> p w k", w=units)[:, :, 0:na + nb]
                    ins = nc.vector.reduce_max(small[0:rows, p, 0, g * units:(g + 1) * units], src, AX_X)
                ins.then_inc(max_ready, 1)
                dve.wait_ge(max_ready, i + 1)
                nc.vector.tensor_scalar(small[0:rows, p, 1, 0:nu], small[0:rows, p, 0, 0:nu], -scale, None,
                                        ALU.mult).then_inc(cap_ready, 1)
                dve.wait_ge(cap_ready, i + 1)
                nc.vector.tensor_tensor(small[0:rows, p, 2, 0:nu], small[0:rows, p, 1, 0:nu],
                                        neg_sinks[0:rows, kind, 0:nu], ALU.min).then_inc(negm_ready, 1)
                dve.wait_ge(negm_ready, i + 1)
                nc.vector.tensor_tensor(small[0:rows, p, 3, 0:nu], small[0:rows, p, 2, 0:nu],
                                        sinks[0:rows, kind, 0:nu], ALU.add).then_inc(sinkm_ready, 1)
                dve.wait_ge(v_ready, i + 1)
                if i >= 2:
                    dve.wait_ge(o_ready, i - 1)
                if step[0] == "prompt":
                    ins = nc.vector.tensor_copy(vals[0:na, p, 0, :], ps_v[0:na, 0:P])
                if nb:
                    ins = nc.vector.tensor_copy(vals[0:nb, p, 1, :], ps_v[0:nb, P:2 * P])
                ins.then_inc(v_copied, 1)

            def back(i):
                step = steps[i]
                nq, units, rows, na, nb = shape(step)
                nu, p = 2 * units, i % 2
                dve.wait_ge(sinke_ready, i + 1)
                nc.vector.tensor_tensor(small[0:rows, p, 5, 0:nu], small[0:rows, p, 4, 0:nu], small[0:rows, p, 3, 0:nu],
                                        ALU.add).then_inc(den_ready, 1)
                dve.wait_ge(den_ready, i + 1)
                nc.vector.reciprocal(small[0:rows, p, 5, 0:nu], small[0:rows, p, 5, 0:nu]).then_inc(inv_ready, 1)
                dve.wait_ge(inv_ready, i + 1)
                nc.vector.tensor_tensor(prob[0:rows, p, 0:nu, 0:na + nb], prob[0:rows, p, 0:nu, 0:na + nb],
                                        small[0:rows, p, 5, 0:nu].unsqueeze(2).to_broadcast([rows, nu, na + nb]),
                                        ALU.mult).then_inc(prob_ready, 1)
                dve.wait_ge(pt_ready, i + 1)
                if nb:
                    nc.vector.tensor_copy(prob_t[0:nb, p, 1, 0:nu * rows], ps_p[1][0:nb, 0:nu * rows]
                                          ).then_inc(ptb_copied, 1)
                else:
                    nc.vector.sem_inc(ptb_copied, 1)
                dve.wait_ge(o_ready, i + 1)
                if i >= 2:
                    dve.wait_ge(lo_ready, i - 1)
                nc.vector.tensor_copy(out[:, p, 0:4 * nq], ps_o[:, 0:4 * nq]).then_inc(out_ready, 1)

            for i in range(len(steps) + 1):
                if i < len(steps):
                    front(i)
                if i >= 1:
                    back(i - 1)

        @block.scalar
        def _(act):
            def front(i):
                step = steps[i]
                nq, units, rows, na, nb = shape(step)
                nu, p = 2 * units, i % 2
                act.wait_ge(negm_ready, i + 1)
                if i >= 2:
                    act.wait_ge(pt_ready, i - 1)
                for n in range(nu):
                    w = n % units
                    ins = nc.scalar.activation(prob[0:rows, p, n, 0:na + nb],
                                               ps_s[p][n // units][0:rows, w * 192:w * 192 + na + nb],
                                               AF.Exp, bias=small[0:rows, p, 2, n:n + 1], scale=scale,
                                               accum_out=small[0:rows, p, 4, n:n + 1])
                ins.then_inc(exp_ready, 1)
                act.wait_ge(sinkm_ready, i + 1)
                nc.scalar.activation(small[0:rows, p, 3, 0:nu], small[0:rows, p, 3, 0:nu], AF.Exp
                                     ).then_inc(sinke_ready, 1)

            def back(i):
                step = steps[i]
                nq, units, rows, na, nb = shape(step)
                p, t0 = i % 2, token(step)
                act.wait_ge(pt_ready, i + 1)
                nc.scalar.copy(prob_t[0:na, p, 0, 0:2 * units * rows], ps_p[0][0:na, 0:2 * units * rows]
                               ).then_inc(pta_copied, 1)
                act.wait_ge(out_ready, i + 1)
                nc.scalar.copy(c.cat_hi[:, 0:4, t0:t0 + nq],
                               out[:, p, 0:4 * nq].rearrange("p (t q) -> p t q", t=4)).then_inc(hi_ready, 1)

            for i in range(len(steps) + 1):
                if i < len(steps):
                    front(i)
                if i >= 1:
                    back(i - 1)

        @block.gpsimd
        def _(pool):
            for i, step in enumerate(steps):
                nq, t0 = shape(step)[0], token(step)
                pool.wait_ge(hi_ready, i + 1)
                nc.gpsimd.tensor_tensor(c.cat_lo[:, 0:4, t0:t0 + nq],
                                        out[:, i % 2, 0:4 * nq].rearrange("p (t q) -> p t q", t=4),
                                        c.cat_hi[:, 0:4, t0:t0 + nq], ALU.subtract).then_inc(lo_ready, 1)



def stage_project_y(c, tag, s, per, k_tiles, x_hi, x_lo):
    nc = c.nc
    steps = KD * per // 2
    tiles = 2 // per
    with ExitStack() as ctx:
        sq = c.sbuf(tag + "_sq", [P, 3, BW], F32, ctx)
        bank = [c.psum(f"{tag}{b}", [P, 512], ctx) for b in range(3)]
        acc_ready, y_ready, sq_ready, sum_done = (c.sem(f"{tag}_{x}") for x in ("acc", "y", "sq", "sum"))
        block = ctx.enter_context(nc.Block())

        @block.sync
        def _(sp):
            load_ring(c, sp, s, s + KD * per)

        @block.tensor
        def _(pe):
            def body(i, first, last):
                for j in range(2):
                    begins = per == 1 or j == 0
                    c.weights_split(pe, s + j, i)
                    for b in range(BLOCKS):
                        m = (3 * (j if per == 1 else 0) + b) - 3
                        if begins and not (first and m < 0):
                            pe.wait_ge(sq_ready, m + 1 + 3 * tiles * i)
                        c.multiply(bank[b][:, 0:BW], s + j, k_tiles, x_hi, x_lo,
                                   0 if per == 1 else j * k_tiles, blk(b), begins, per == 1 or j == 1
                                   ).then_inc(acc_ready, 1)

            run(pe, steps, body)

        @block.scalar
        def _(act):
            def body(i, first, last):
                for j in range(2):
                    if per == 1 or j == 1:
                        t = j if per == 1 else 0
                        for b in range(BLOCKS):
                            m = 3 * t + b
                            act.wait_ge(acc_ready, 3 * j + b + 1 + 6 * i)
                            nc.scalar.mul(c.y[:, ds(tiles * i + t, 1), blk(b)], bank[b][:, 0:BW].unsqueeze(1),
                                          1 / WSCALE).then_inc(y_ready, 1)
                            if not (first and m < 3):
                                act.wait_ge(sum_done, m - 2 + 3 * tiles * i)
                            nc.scalar.activation(sq[:, b, :], bank[b][:, 0:BW], AF.Square, scale=1 / WSCALE
                                                 ).then_inc(sq_ready, 1)
                    split_u(c, act, c.split_hi, s, s + j, i, last, acc_ready)

            run(act, steps, body)

        @block.vector
        def _(dve):
            def body(i, first, last):
                for j in range(2):
                    if per == 1 or j == 1:
                        t = j if per == 1 else 0
                        for b in range(BLOCKS):
                            m = 3 * t + b
                            dve.wait_ge(sq_ready, m + 1 + 3 * tiles * i)
                            if first and t == 0:
                                nc.vector.tensor_copy(c.acc[:, blk(b)], sq[:, b, :]).then_inc(sum_done, 1)
                            else:
                                dve.wait_ge(sum_done, m - 2 + 3 * tiles * i)
                                nc.vector.tensor_tensor(c.acc[:, blk(b)], c.acc[:, blk(b)], sq[:, b, :], ALU.add
                                                        ).then_inc(sum_done, 1)
                    split_u(c, dve, c.split_lo, s, s + j, i, last, acc_ready)

            run(dve, steps, body)


def stage_residual(c, tag, layer, which, x_in, x_out, final):
    nc = c.nc
    with ExitStack() as ctx:
        xr = c.sbuf(tag + "_x", [P, 2, T], F32, ctx)
        sq = c.sbuf(tag + "_sq", [P, 2, T], F32, ctx)
        bank = c.psum(tag + "_sum", [P, 512], ctx)
        post = Norm(c, ctx, tag + "p", bank)
        x_loaded = [c.sem(f"{tag}_x_loaded{k}") for k in range(2)]
        scaled, x_ready, sq_ready, sum_done, x_stored = (
            c.sem(f"{tag}_{x}") for x in ("scaled", "x_ready", "sq_ready", "sum", "stored"))
        if not final:
            nxt = (layer, 2) if which == 1 else (layer + 1, 0)
            pre = NormReuse(c, ctx, tag + "n", post)
            h_vector, h_scalar, h_gpsimd = normalise(c, ctx, tag, None, pre, c.y, lambda j: c.gain(*nxt, j))
        block = ctx.enter_context(nc.Block())

        @block.sync
        def _(sp):
            for j in range(KD):
                if j >= 2:
                    sp.wait_ge(x_ready, j - 1)
                sp.dma_start(xr[:, j % 2, :], x_in[:, j, :]).then_inc(x_loaded[j % 2], 16)
            for j in range(KD):
                sp.wait_ge(x_ready, j + 1)
                sp.dma_start(x_out[:, j, :], c.y[:, j, :]).then_inc(x_stored, 16)
            sp.wait_ge(x_stored, 16 * KD)

        @block.tensor
        def _(pe):
            post.tensor(pe, c.acc)
            if not final:
                pre.tensor(pe, c.acc)

        @block.vector
        def _(dve):
            nc.vector.sem_inc(post.acc_ready, 1)
            post.vector(dve)
            for j in range(KD):
                for b in range(BLOCKS):
                    ins = nc.vector.tensor_tensor(c.y[:, j, blk(b)], c.y[:, j, blk(b)], post.ps_spread[b][:, 0:BW],
                                                  ALU.mult)
                ins.then_inc(scaled, 1)
                dve.wait_ge(scaled, j + 1)
                dve.wait_ge(x_loaded[j % 2], 16 * (j // 2 + 1))
                nc.vector.scalar_tensor_tensor(c.y[:, j, :], c.y[:, j, :], c.gain(layer, which, j), xr[:, j % 2, :],
                                               ALU.mult, ALU.add).then_inc(x_ready, 1)
            if not final:
                pre.vector(dve)
                h_vector(dve)

        @block.scalar
        def _(act):
            post.scalar(act)
            if not final:
                for j in range(KD):
                    act.wait_ge(x_ready, j + 1)
                    if j >= 2:
                        act.wait_ge(sum_done, j - 1)
                    nc.scalar.activation(sq[:, j % 2, :], c.y[:, j, :], AF.Square).then_inc(sq_ready, 1)
                pre.scalar(act)
                h_scalar(act)

        @block.gpsimd
        def _(pool):
            if final:
                return
            pool.wait_ge(post.sum_ready, 1)
            for j in range(KD):
                pool.wait_ge(sq_ready, j + 1)
                if j:
                    pool.wait_ge(sum_done, j)
                if j == 0:
                    nc.gpsimd.tensor_copy(c.acc[:, :], sq[:, 0, :]).then_inc(sum_done, 1)
                else:
                    nc.gpsimd.tensor_tensor(c.acc[:, :], c.acc[:, :], sq[:, j % 2, :], ALU.add
                                            ).then_inc(sum_done if j < KD - 1 else pre.acc_ready, 1)
            h_gpsimd(pool)


class NormReuse(Norm):

    def __init__(self, c, ctx, tag, other):
        self.c = c
        self.acc_ready, self.sum_ready, self.root_ready, self.inv_ready, self.spread_ready = (
            c.sem(f"{tag}_{x}") for x in ("acc_ready", "sum_ready", "root_ready", "inv_ready", "spread_ready"))
        self.ps_sum, self.ps_spread = other.ps_sum, other.ps_spread
        self.root, self.inv = c.sbuf(tag + "_root", [P, TT], F32, ctx), c.sbuf(tag + "_inv", [P, TT], F32, ctx)



def stage_gate_up(c, tag, s, mid_hi, mid_lo):
    nc = c.nc
    with ExitStack() as ctx:
        sil = c.sbuf(tag + "_silu", [P, 3, BW], F32, ctx)
        mid = c.sbuf(tag + "_mid", [P, 3, BW], F32, ctx)
        bank = [c.psum(f"{tag}{b}", [P, 512], ctx) for b in range(6)]
        acc_ready, sil_ready, mid_ready, hi_ready, lo_ready = (
            c.sem(f"{tag}_{x}") for x in ("acc", "sil", "mid", "hi", "lo"))
        block = ctx.enter_context(nc.Block())

        @block.sync
        def _(sp):
            load_ring(c, sp, s, s + 2 * FT)

        @block.tensor
        def _(pe):
            def body(i, first, last):
                for j, used in enumerate((sil_ready, mid_ready)):
                    c.weights_split(pe, s + j, i)
                    for b in range(BLOCKS):
                        if not first:
                            pe.wait_ge(used, b - 2 + 3 * i)
                        c.multiply(bank[3 * j + b][:, 0:BW], s + j, KD, c.x_hi, c.x_lo, 0, blk(b), True, True
                                   ).then_inc(acc_ready, 1)

            run(pe, FT, body)

        @block.scalar
        def _(act):
            def body(i, first, last):
                for b in range(BLOCKS):
                    act.wait_ge(acc_ready, b + 1 + 6 * i)
                    if not first:
                        act.wait_ge(mid_ready, b - 2 + 3 * i)
                    nc.scalar.activation(sil[:, b, :], bank[b][:, 0:BW], AF.Silu, scale=1 / WSCALE
                                         ).then_inc(sil_ready, 1)
                split_u(c, act, c.split_hi, s, s, i, last, acc_ready)
                for b in range(BLOCKS):
                    act.wait_ge(mid_ready, b + 1 + 3 * i)
                    nc.scalar.copy(mid_hi[:, ds(i, 1), blk(b)], mid[:, b, :].unsqueeze(1)).then_inc(hi_ready, 1)
                split_u(c, act, c.split_hi, s, s + 1, i, last, acc_ready)

            run(act, FT, body)

        @block.vector
        def _(dve):
            def body(i, first, last):
                split_u(c, dve, c.split_lo, s, s, i, last, acc_ready)
                for b in range(BLOCKS):
                    dve.wait_ge(acc_ready, 3 + b + 1 + 6 * i)
                    dve.wait_ge(sil_ready, b + 1 + 3 * i)
                    if not first:
                        dve.wait_ge(lo_ready, b - 2 + 3 * i)
                    nc.vector.scalar_tensor_tensor(mid[:, b, :], bank[3 + b][:, 0:BW], 1 / WSCALE, sil[:, b, :],
                                                   ALU.mult, ALU.mult).then_inc(mid_ready, 1)
                split_u(c, dve, c.split_lo, s, s + 1, i, last, acc_ready)

            run(dve, FT, body)

        @block.gpsimd
        def _(pool):
            with pool.Fori(0, FT) as i:
                for b in range(BLOCKS):
                    pool.wait_ge(hi_ready, b + 1 + 3 * i)
                    nc.gpsimd.tensor_tensor(mid_lo[:, ds(i, 1), blk(b)], mid[:, b, :].unsqueeze(1),
                                            mid_hi[:, ds(i, 1), blk(b)], ALU.subtract).then_inc(lo_ready, 1)


def feed_forward(c, tag, s, layer, x_in, x_out, final):
    with ExitStack() as ctx:
        mid_hi = c.sbuf(tag + "_mid_hi", [P, FT, T], F16, ctx)
        mid_lo = c.sbuf(tag + "_mid_lo", [P, FT, T], F16, ctx)
        stage_gate_up(c, tag + "_gu", s, mid_hi, mid_lo)
        c.end_stage()
        stage_project_y(c, tag + "_dn", s + 2 * FT, 2, DOWN_K, mid_hi, mid_lo)
        c.end_stage()
    stage_residual(c, tag + "_r", layer, 3, x_in, x_out, final)
    c.end_stage()



class SSM:

    def __init__(self, c, ctx):
        shape = [P, TT, SHEADS]
        self.dt, self.da, self.ea, self.dend = (c.sbuf("ssm_" + n, shape, F32, ctx) for n in ("dt", "da", "ea", "dend"))
        self.chunk_decay = c.sbuf("ssm_chunk_decay", [P, SEQ // P, SHEADS], F32, ctx)
        self.stream_decay = c.sbuf("ssm_stream_decay", [P, STREAMS, SHEADS], F32, ctx)
        self.d = c.sbuf("ssm_d", [P, SHEADS], F32, ctx)


def stage_dt(c, a, s, m):
    nc, n = c.nc, TT * SHEADS
    np_ = SEQ // P * SHEADS
    with ExitStack() as ctx:
        rows = c.sbuf("ssm_rows", [P, 3, SHEADS], F32, ctx)
        neg_a = c.sbuf("ssm_neg_a", [P, SHEADS], F32, ctx)
        work = c.sbuf("ssm_work", [P, 6, n], F32, ctx)
        by_s = c.sbuf("ssm_by_stream", [P, STREAMS, SHEADS], F32, ctx)
        ps_dt, ps_cum, ps_tot, ps_str = (c.psum("dt_" + x, [P, 512], ctx) for x in ("raw", "cum", "tot", "str"))
        rows_loaded, acc_ready, sums_ready = c.sem("ssm_rows_loaded"), c.sem("dt_acc"), c.sem("dt_sums")
        neg_abs, exp_done, u_ready, ln_done, da_ready, a_ready = (
            c.sem("dt_" + x) for x in ("neg_abs", "exp", "u", "ln", "da", "a"))
        step, diff_ready, decays = c.sem("dt_step"), c.sem("dt_diff"), c.sem("dt_decays")
        block = ctx.enter_context(nc.Block())

        def flat(t):
            return t[:, :, :].rearrange("p a b -> p (a b)")

        def w(k):
            return work[:, k, :]

        @block.sync
        def _(sp):
            sp.dma_start(rows[:, :, :], a["ssm_rows"]).then_inc(rows_loaded, 16)
            load_ring(c, sp, s, s + 1)

        @block.tensor
        def _(pe):
            c.weights_split(pe, s)
            wh = c.w_hi[:, s % 2, 0:KD * SHEADS].rearrange("p (k h) -> p k h", k=KD)
            wl = c.w_lo[:, s % 2, 0:KD * SHEADS].rearrange("p (k h) -> p k h", k=KD)
            for t in range(TT):
                out = ps_dt[:, t * SHEADS:(t + 1) * SHEADS]
                for k in range(KD):
                    xh, xl = (x[:, k, t * P:(t + 1) * P] for x in (c.x_hi, c.x_lo))
                    pe.matmul(out, xh, wh[:, k, :], start=(k == 0), stop=False)
                    pe.matmul(out, xl, wh[:, k, :], start=False, stop=False)
                    mm = pe.matmul(out, xh, wl[:, k, :], start=False, stop=(k == KD - 1))
                if t == TT - 1:
                    mm.then_inc(acc_ready, 1)
            pe.wait_ge(da_ready, 2)
            da = flat(m.da)
            pe.matmul(ps_cum[:, 0:np_], c.tri_incl, da[:, 0:np_], start=True, stop=True)
            pe.matmul(ps_cum[:, np_:n], c.tri_block, da[:, np_:n], start=True, stop=True)
            pe.matmul(ps_tot[:, 0:np_], c.ones, da[:, 0:np_], start=True, stop=True)
            pe.matmul(ps_tot[:, np_:n], c.block_ones, da[:, np_:n], start=True, stop=True)
            pe.matmul(ps_str[:, 0:STREAMS * SHEADS], c.ones, flat(by_s), start=True, stop=True
                      ).then_inc(sums_ready, 1)

        @block.vector
        def _(dve):
            v = nc.vector
            dve.wait_ge(rows_loaded, 16)
            dve.wait_ge(acc_ready, 1)
            bias = rows[:, 0, :].unsqueeze(1).to_broadcast([P, TT, SHEADS])
            v.scalar_tensor_tensor(w(0).rearrange("p (a b) -> p a b", a=TT),
                                   ps_dt[:, 0:n].rearrange("p (a b) -> p a b", a=TT), 1 / WSCALE, bias,
                                   ALU.mult, ALU.add).then_inc(step, 1)
            dve.wait_ge(step, 1)
            v.tensor_scalar(w(1), w(0), -1.0, None, ALU.mult).then_inc(step, 1)
            dve.wait_ge(step, 2)
            v.tensor_tensor(w(1), w(0), w(1), ALU.min).then_inc(neg_abs, 1)
            v.tensor_scalar(w(0), w(0), 0.0, None, ALU.max).then_inc(step, 1)
            dve.wait_ge(exp_done, 2)
            v.tensor_scalar(w(3), w(2), 1.0, None, ALU.add).then_inc(u_ready, 1)
            dve.wait_ge(u_ready, 1)
            v.tensor_scalar(w(4), w(3), -1.0, None, ALU.add).then_inc(step, 1)
            v.reciprocal(w(5), w(3)).then_inc(step, 1)
            dve.wait_ge(step, 5)
            v.tensor_tensor(w(4), w(2), w(4), ALU.subtract).then_inc(step, 1)
            dve.wait_ge(step, 6)
            v.tensor_tensor(w(4), w(4), w(5), ALU.mult).then_inc(step, 1)
            dve.wait_ge(step, 7)
            v.tensor_tensor(w(0), w(0), w(4), ALU.add).then_inc(step, 1)
            dve.wait_ge(step, 8)
            dve.wait_ge(ln_done, 1)
            v.tensor_tensor(flat(m.dt), w(0), w(1), ALU.add).then_inc(step, 1)
            v.tensor_scalar(neg_a[:, :], neg_a[:, :], -1.0, None, ALU.mult).then_inc(a_ready, 1)
            v.tensor_copy(m.d[:, :], rows[:, 2, :]).then_inc(step, 1)
            dve.wait_ge(step, 9)
            dve.wait_ge(a_ready, 1)
            v.tensor_tensor(m.da[:, :, :], m.dt[:, :, :], neg_a[:, :].unsqueeze(1).to_broadcast([P, TT, SHEADS]),
                            ALU.mult).then_inc(da_ready, 1)
            dve.wait_ge(da_ready, 1)
            v.tensor_tensor(by_s[:, :, :], m.da[:, TT - 1, :].unsqueeze(1).to_broadcast([P, STREAMS, SHEADS]),
                            c.stream_mask.unsqueeze(2).to_broadcast([P, STREAMS, SHEADS]), ALU.mult
                            ).then_inc(da_ready, 1)
            c.split_lo(dve, s + 2, 0, acc_ready, 1)
            dve.wait_ge(sums_ready, 1)
            v.tensor_copy(w(2), ps_cum[:, 0:n]).then_inc(step, 1)
            dve.wait_ge(step, 11)
            v.tensor_tensor(w(3), ps_tot[:, 0:n], w(2), ALU.subtract).then_inc(diff_ready, 1)

        @block.scalar
        def _(act):
            act.wait_ge(neg_abs, 1)
            nc.scalar.activation(w(2), w(1), AF.Exp).then_inc(exp_done, 1)
            nc.scalar.activation(neg_a[:, :], rows[:, 1, :], AF.Exp).then_inc(exp_done, 1)
            act.wait_ge(u_ready, 1)
            nc.scalar.activation(w(1), w(3), AF.Ln).then_inc(ln_done, 1)
            c.split_hi(act, s + 2, 0, acc_ready, 1)
            act.wait_ge(sums_ready, 1)
            nc.scalar.activation(flat(m.stream_decay), ps_str[:, 0:STREAMS * SHEADS], AF.Exp).then_inc(decays, 1)
            act.wait_ge(diff_ready, 1)
            nc.scalar.activation(flat(m.ea), ps_cum[:, 0:n], AF.Exp).then_inc(decays, 1)
            nc.scalar.activation(flat(m.chunk_decay), ps_tot[:, 0:np_], AF.Exp).then_inc(decays, 1)
            nc.scalar.activation(flat(m.dend), w(3), AF.Exp).then_inc(decays, 1)
            act.wait_ge(decays, 4)


def stage_ssm(c, a, s, m):
    nc = c.nc
    n_units, n_conv, n_z, n_out = 14, 6, 4, 4
    per_acc = BLOCKS * (n_conv + 2 * n_out)
    with ExitStack() as ctx:
        sb = lambda name, shape, dt=F32: c.sbuf("ss_" + name, shape, dt, ctx)
        xbc = sb("xbc", [P, n_conv, T])
        pad = sb("pad", [P, 2, XW3])
        hist = sb("hist", [P, SG * n_conv, 1 + STREAMS, 3])
        taps = sb("taps", [P, 4, SG * n_conv])
        bias = sb("bias", [P, SG * n_conv])
        gains = sb("gains", [P, SG * 4])
        wz_hi, wz_lo = sb("wz_hi", [P, KD, GW], F16), sb("wz_lo", [P, KD, GW], F16)
        g_hi, g_lo = sb("g_hi", [P, 4, T], F16), sb("g_lo", [P, 4, T], F16)
        x_tok, xdt, xdec = (sb(x, [P, 2, GW]) for x in ("x_tok", "xdt", "xdec"))
        seg_in, e = sb("seg_in", [P, 2, SHPG, P]), sb("e", [P, 2, SHPG, P])
        b_tok = sb("b_tok", [P, 2, P])
        flat = pad[:, :, :].rearrange("p a b -> p (a b)")
        decayed, junk = flat[:, 0:GW], flat[:, GW:GW + GW // 2].bitcast(F16)
        yt, zt, cbm = c.acc[:, 0:GW], c.acc[:, GW:2 * GW], c.acc[:, 2 * GW:2 * GW + P]
        sq = flat[:, 2 * GW:2 * GW + 3 * BW].rearrange("p (b n) -> p b n", b=3)
        state = sb("state", [P, 3, GW])
        ssq, root, inv = sb("ssq", [P, TT]), sb("root", [P, TT]), sb("inv", [P, TT])
        ps_yo, ps_yd, ps_st = (c.psum("ss_" + x, [P, 512], ctx) for x in ("yo", "yd", "st"))
        ps_x, ps_z, ps_bc = (c.psum("ss_" + x, [P, 512], ctx) for x in ("x", "zt", "bc"))
        ps_seg = [c.psum(f"ss_seg{k}", [P, 512], ctx) for k in range(2)]
        bank = [ps_yo, ps_yd, ps_st]

        sem = lambda name: c.sem("ss_" + name)
        small_loaded, acc_ready = sem("small_loaded"), sem("acc")
        pad_ready, hist_put, hist_kept, tap_done, xbc_ready = (
            sem(x) for x in ("pad", "hist_put", "hist_kept", "tap", "xbc"))
        xt_ready, x_copied, bc_ready, b_ready, cb_ready = (sem(x) for x in ("xt", "x_copied", "bcr", "b", "cb"))
        segin_ready, seg_ready, exp_ready, w_ready = (sem(x) for x in ("segin", "seg", "exp", "w"))
        xdt_ready, xd_ready, xdec_ready = (sem(x) for x in ("xdt_ready", "xd", "xdec"))
        z_ready, tanh_ready, zt_ready = (sem(x) for x in ("z_ready", "tanh", "zt_ready"))
        yo_ready, yo_used, yd_ready, yd_used, y_done, gated, sq_done = (
            sem(x) for x in ("yo_ready", "yo_used", "yd_ready", "yd_used", "y_done", "gated", "sq_done"))
        st_ready, dec_ready, h_ready = (sem(x) for x in ("st_ready", "dec", "h"))
        cm_zero, cm_ready, bm_ready = (sem(x) for x in ("cm_zero", "cm", "bm"))
        root_ready, inv_ready, yn_ready, t_ready, ghi_ready, glo_ready = (
            sem(x) for x in ("root_ready", "inv_ready", "yn", "t", "ghi", "glo"))
        y_ready, ysq_ready, ysum_done = (sem(x) for x in ("y", "ysq", "ysum"))
        state_loaded = [sem(f"state_loaded{r}") for r in range(3)]
        state_stored = [sem(f"state_stored{r}") for r in range(3)]
        hist_stored, waits_alone = sem("hist_stored"), sem("waits_alone")
        block = ctx.enter_context(nc.Block())

        def chunk(t):
            return slice(t * P, (t + 1) * P)

        def wait_ge(engine, semaphore, value):
            if not isinstance(value, int) or value > 0:
                engine.wait_ge(semaphore, value)

        def each_group(engine, body):
            body(0, False)
            with engine.Fori(1, SG - 1) as g:
                body(g, False)
            body(SG - 1, True)

        def alone(engine):
            engine.sem_inc(waits_alone, 1)

        LAST = TT - 1
        PER_H = LAST + 1 + STREAMS
        PER_ST = LAST + STREAMS
        ring = [(k + 1) % 3 for k in range(STREAMS)]
        uses = [ring.count(r) for r in range(3)]
        turn = [ring[:k].count(ring[k]) for k in range(STREAMS)]

        def of_heads(v):
            return v.unsqueeze(2).to_broadcast([P, SHPG, SHD])

        def heads(t):
            return t.rearrange("p (h d) -> p h d", h=SHPG)

        def head_cols(t, g):
            return t[:, ds(SHPG * g, SHPG)]

        @block.sync
        def _(sp):
            sp.dma_start(hist[:, :, :, :], a["ssm_hist"]).then_inc(small_loaded, 16)
            sp.dma_start(taps[:, :, :], a["ssm_taps"]).then_inc(small_loaded, 16)
            sp.dma_start(bias[:, :], a["ssm_bias"]).then_inc(small_loaded, 16)
            sp.dma_start(gains[:, :], a["ssm_gains"]).then_inc(small_loaded, 16)

            def load_state(g, k):
                sp.dma_start(state[:, ring[k], :], a["state"][k, :, ds(g * GW, GW)]
                             ).then_inc(state_loaded[ring[k]], 16)

            def load_unit(g, j):
                u = s + 4 + j
                wait_ge(sp, c.w_hi_ready, u - 1 + n_units * g)
                wait_ge(sp, c.w_lo_ready, u - 1 + n_units * g)
                src = a["ssm_w"][ds(4 + j + n_units * g, 1), :, :].rearrange("a p c -> (a p) c")
                sp.dma_start(c.w_raw[:, u % 2, 0:UNIT], src).then_inc(c.w_loaded[u % 2], 16)

            def group(g, last):
                for j in range(n_units - 4):
                    load_unit(g, j)
                load_state(g, 0)
                load_state(g, 1)
                wait_ge(sp, h_ready, (LAST + 1) + PER_H * g)
                sp.dma_start(a["new_state_prompt"][:, ds(g * GW, GW)], state[:, 0, :]
                             ).then_inc(state_stored[0], 16)
                for k in range(STREAMS):
                    if k == 2:
                        wait_ge(sp, state_stored[0], 16 + 16 * (uses[0] + 1) * g)
                        load_state(g, 2)
                    wait_ge(sp, h_ready, (LAST + 2 + k) + PER_H * g)
                    r, extra = ring[k], 1 if ring[k] == 0 else 0
                    sp.dma_start(a["new_state"][k, :, ds(g * GW, GW)], state[:, r, :]).then_inc(state_stored[r], 16)
                    wait_ge(sp, state_stored[r], 16 * (turn[k] + 1 + extra) + 16 * (uses[r] + extra) * g)
                    alone(sp)
                    if k + 3 < STREAMS:
                        load_state(g, k + 3)
                for j in range(n_units - 4, n_units):
                    if last:
                        c.load_weights(sp, s + 4 + j + n_units * g)
                    else:
                        load_unit(g, j)

            each_group(sp, group)
            wait_ge(sp, hist_kept, SG * n_conv)
            sp.dma_start(a["new_ssm_hist"], hist[:, :, :, :]).then_inc(hist_stored, 16)
            sp.wait_ge(hist_stored, 16)

        @block.tensor
        def _(pe):
            def weights(u, g):
                wait_ge(pe, c.w_hi_ready, s + u + 1 + n_units * g)
                wait_ge(pe, c.w_lo_ready, s + u + 1 + n_units * g)

            def project(g):
                for j in range(n_conv):
                    weights(j, g)
                    for b in range(BLOCKS):
                        if j == 0:
                            wait_ge(pe, y_ready, 3 * (2 * n_out - 1) + b + 1 + 6 * n_out * (g - 1)
                                    if not (isinstance(g, int) and g == 0) else 0)
                        else:
                            wait_ge(pe, pad_ready, 4 * (j - 1) + (b + 1 if b < 2 else 4) + 4 * n_conv * g)
                        c.multiply(bank[b][:, 0:BW], s + j, KD, c.x_hi, c.x_lo, 0, blk(b), True, True
                                   ).then_inc(acc_ready, 1)

            def inputs(g, t):
                v = TT * g + t
                cols = chunk(t)
                wait_ge(pe, x_copied, v)
                wait_ge(pe, glo_ready, max(0, t - 2) + TT * g)
                for j in range(4):
                    mm = pe.transpose(ps_x[:, j * P:(j + 1) * P], xbc[:, j, cols], c.ident)
                mm.then_inc(xt_ready, 1)
                wait_ge(pe, b_ready, v)
                wait_ge(pe, cb_ready, v)
                pe.transpose(ps_bc[:, 0:P], xbc[:, 4, cols], c.ident)
                pe.matmul(ps_bc[:, P:2 * P], xbc[:, 4, cols], xbc[:, 5, cols], start=True, stop=True
                          ).then_inc(bc_ready, 1)
                wait_ge(pe, segin_ready, v + 1)
                wait_ge(pe, exp_ready, v)
                for h in range(SHPG):
                    mm = pe.matmul(ps_seg[h // 4][:, (h % 4) * P:(h % 4 + 1) * P], seg_in[:, t % 2, h, :], c.tri_incl,
                                   start=True, stop=True)
                mm.then_inc(seg_ready, 1)

            def project_z(g, t):
                if t == 0:
                    weights(n_conv + n_z - 1, g)
                wait_ge(pe, zt_ready, TT * g + t)
                for k in range(KD):
                    xh, xl = c.x_hi[:, k, chunk(t)], c.x_lo[:, k, chunk(t)]
                    pe.matmul(ps_z[:, :], xh, wz_hi[:, k, :], start=(k == 0), stop=False)
                    pe.matmul(ps_z[:, :], xl, wz_hi[:, k, :], start=False, stop=False)
                    mm = pe.matmul(ps_z[:, :], xh, wz_lo[:, k, :], start=False, stop=(k == KD - 1))
                mm.then_inc(z_ready, 1)

            def outputs(g, t):
                v, p = TT * g + t, t % 2
                cols = chunk(t)
                wait_ge(pe, w_ready, v + 1)
                wait_ge(pe, xdt_ready, v + 1)
                wait_ge(pe, yd_used, v)
                for h in range(SHPG):
                    mm = pe.matmul(ps_yd[:, h * SHD:(h + 1) * SHD], e[:, p, h, :], xdt[:, p, h * SHD:(h + 1) * SHD],
                                   start=True, stop=True)
                mm.then_inc(yd_ready, 1)
                wait_ge(pe, yo_used, v)
                wait_ge(pe, xdec_ready, v + 1)
                if t < LAST:
                    wait_ge(pe, h_ready, t + 1 + PER_H * g)
                    pe.matmul(ps_yo[:, :], xbc[:, 5, cols], state[:, 0, :], start=True, stop=True
                              ).then_inc(yo_ready, 1)
                    wait_ge(pe, b_ready, v + 1)
                    pe.matmul(ps_st[:, :], b_tok[:, p, :], xdec[:, p, :], start=True, stop=True
                              ).then_inc(st_ready, 1)
                    return
                wait_ge(pe, cm_ready, STREAMS + STREAMS * g)
                wait_ge(pe, bm_ready, 1 + g)
                for k in range(STREAMS):
                    r = ring[k]
                    wait_ge(pe, state_loaded[r], 16 * (turn[k] + 1) + 16 * uses[r] * g)
                    mm = pe.matmul(ps_yo[:, :], seg_in[:, 1 - p, k, :], state[:, r, :], start=(k == 0),
                                   stop=(k == STREAMS - 1))
                    if k == STREAMS - 1:
                        mm.then_inc(yo_ready, 1)
                    wait_ge(pe, h_ready, LAST + 1 + k + PER_H * g)
                    pe.matmul(ps_st[:, :], e[:, 1 - p, k, :], xdec[:, p, :], start=True, stop=True
                              ).then_inc(st_ready, 1)

            def turn_back(g, t):
                wait_ge(pe, yn_ready, t + 1 + TT * g)
                wait_ge(pe, x_copied, min(t + 3, TT) + TT * g)
                wait_ge(pe, glo_ready, t + TT * g)
                for j in range(4):
                    mm = pe.transpose(ps_x[:, j * P:(j + 1) * P], xbc[:, j, chunk(t)], c.ident)
                mm.then_inc(t_ready, 1)

            def project_out(g):
                for q in range(n_out):
                    u = n_conv + n_z + q
                    weights(u, g)
                    for n in range(2):
                        for b in range(BLOCKS):
                            if q == 0 and n == 0:
                                wait_ge(pe, (yo_used, yd_used, h_ready)[b], (TT, TT, PER_H)[b] * (g + 1))
                                wait_ge(pe, glo_ready, 3 * (b + 1) + TT * g)
                            else:
                                wait_ge(pe, y_ready, 3 * (2 * q + n - 1) + b + 1 + 6 * n_out * g)
                            for k in range(4):
                                lo = (2 * k + n) * P
                                wh, wl = (w[:, u % 2 ^ s % 2, lo:lo + P] for w in (c.w_hi, c.w_lo))
                                pe.matmul(bank[b][:, 0:BW], wh, g_hi[:, k, blk(b)], start=(k == 0), stop=False)
                                pe.matmul(bank[b][:, 0:BW], wh, g_lo[:, k, blk(b)], start=False, stop=False)
                                mm = pe.matmul(bank[b][:, 0:BW], wl, g_hi[:, k, blk(b)], start=False, stop=(k == 3))
                            mm.then_inc(acc_ready, 1)

            def group(g, last):
                project(g)
                wait_ge(pe, xbc_ready, n_conv + n_conv * g)
                for i in range(TT + 2):
                    if i < TT:
                        inputs(g, i)
                    if 1 <= i <= TT:
                        outputs(g, i - 1)
                    if i >= 2:
                        turn_back(g, i - 2)
                    if i < TT:
                        project_z(g, i)
                project_out(g)

            each_group(pe, group)

        @block.scalar
        def _(act):
            act.wait_ge(small_loaded, 64)

            def split(g, j, last=False):
                u = s + j
                if last and j >= n_units:
                    wait_ge(act, acc_ready, per_acc * g + 3 * n_conv + 6 * (j - n_units + 3))
                    c.split_hi(act, u + n_units * g)
                    return
                wait_ge(act, c.w_loaded[u % 2], 16 * (u // 2 + 1) + 16 * (n_units // 2) * g)
                if n_conv <= j < n_conv + n_z:
                    wait_ge(act, z_ready, TT * g)
                    q = 2 * (j - n_conv)
                    out = wz_hi[:, q:q + 2, :].rearrange("p a b -> p (a b)")
                else:
                    out = c.w_hi[:, u % 2, 0:UNIT]
                nc.scalar.activation(out, c.w_raw[:, u % 2, 0:UNIT], AF.Copy, scale=WSCALE
                                     ).then_inc(c.w_hi_ready, 1)

            def conv_input(g, j):
                for b in range(BLOCKS):
                    wait_ge(act, acc_ready, 3 * j + b + 1 + per_acc * g)
                    if b == 0 and j >= 2:
                        wait_ge(act, tap_done, 8 * (j - 1) + 8 * n_conv * g)
                        wait_ge(act, hist_kept, j - 1 + n_conv * g)
                    elif b == 0:
                        wait_ge(act, t_ready, TT * g)
                    lo, hi = b * BW, min((b + 1) * BW, SEQ)
                    nc.scalar.mul(pad[:, j % 2, 3 + lo:3 + hi], bank[b][:, 0:hi - lo], 1 / WSCALE
                                  ).then_inc(pad_ready, 1)
                _, streams = sequences(pad[:, j % 2, :], 3)
                nc.scalar.mul(streams(3), bank[2][:, SEQ - 2 * BW:BW].rearrange("p (s t) -> p s t", s=STREAMS),
                              1 / WSCALE).then_inc(pad_ready, 1)

            def silu(g, j):
                wait_ge(act, tap_done, 8 * (j + 1) + 8 * n_conv * g)
                nc.scalar.activation(xbc[:, j, :], xbc[:, j, :], AF.Silu, bias=bias[:, ds(n_conv * g + j, 1)]
                                     ).then_inc(xbc_ready, 1)

            def tanh(g, t):
                v = TT * g + t
                wait_ge(act, z_ready, v + 1)
                wait_ge(act, gated, v)
                nc.scalar.activation(zt, ps_z[:, :], AF.Tanh, scale=0.5 / WSCALE).then_inc(tanh_ready, 1)

            def inputs(g, t):
                v, p = TT * g + t, t % 2
                wait_ge(act, xt_ready, v + 1)
                wait_ge(act, y_done, (v - 1 if t >= 2 else TT * g))
                nc.scalar.copy(x_tok[:, p, :], ps_x[:, :]).then_inc(x_copied, 1)
                wait_ge(act, seg_ready, v + 1)
                if t == 1:
                    wait_ge(act, st_ready, PER_ST * g)
                else:
                    wait_ge(act, yd_ready, v - 1 if t else v)
                for q in range(2):
                    ins = nc.scalar.activation(e[:, p, 4 * q:4 * q + 4, :],
                                               ps_seg[q][:, :].rearrange("p (h k) -> p h k", h=4), AF.Exp)
                ins.then_inc(exp_ready, 1)

            def mean(g, t):
                v = TT * g + t
                wait_ge(act, gated, v + 1)
                nc.scalar.activation(junk.rearrange("p (j k) -> p j k", j=4), xbc[:, 0:4, chunk(t)],
                                     AF.Square, accum_out=ssq[:, t:t + 1]).then_inc(sq_done, 1)
                wait_ge(act, sq_done, v + 1)
                nc.scalar.activation(root[:, t:t + 1], ssq[:, t:t + 1], AF.Sqrt, bias=c.eps[:, 0:1], scale=1.0 / GW
                                     ).then_inc(root_ready, 1)

            def result_hi(g, t):
                wait_ge(act, t_ready, t + 1 + TT * g)
                if t == 0:
                    wait_ge(act, acc_ready, per_acc * g)
                alone(act)
                for j in range(4):
                    ins = nc.scalar.activation(g_hi[:, j, chunk(t)], ps_x[:, j * P:(j + 1) * P], AF.Copy,
                                               scale=gains[:, ds(4 * g + j, 1)])
                ins.then_inc(ghi_ready, 1)

            def group(g, last):
                for j in range(n_conv):
                    conv_input(g, j)
                    if j:
                        silu(g, j - 1)
                    split(g, j + 2)
                silu(g, n_conv - 1)
                for j in range(n_conv + 2, n_conv + n_z + 2):
                    split(g, j)
                wait_ge(act, hist_kept, n_conv + n_conv * g)
                for i in range(TT + 2):
                    if 1 <= i <= TT:
                        tanh(g, i - 1)
                    if i < TT:
                        inputs(g, i)
                    if i >= 2:
                        result_hi(g, i - 2)
                    if 1 <= i <= TT:
                        mean(g, i - 1)
                for q in range(n_out):
                    if last:
                        for n in range(2):
                            for b in range(BLOCKS):
                                y_n = 6 * q + 3 * n + b
                                wait_ge(act, y_ready, y_n + 1 + 6 * n_out * g)
                                wait_ge(act, ysum_done, max(0, y_n - 2))
                                nc.scalar.activation(sq[:, b, :], c.y[:, 2 * q + n, blk(b)], AF.Square
                                                     ).then_inc(ysq_ready, 1)
                    wait_ge(act, acc_ready, 3 * n_conv + 6 * (q + 1) + per_acc * g)
                    split(g, n_conv + n_z + 2 + q, last)

            each_group(act, group)

        @block.vector
        def _(dve):
            v_ = nc.vector
            dve.wait_ge(small_loaded, 64)

            def split(g, j, last=False):
                u = s + j
                if last and j >= n_units:
                    wait_ge(dve, acc_ready, per_acc * g + 3 * n_conv + 6 * (j - n_units + 3))
                    c.split_lo(dve, u + n_units * g)
                    return
                wait_ge(dve, c.w_hi_ready, u + 1 + n_units * g)
                if n_conv <= j < n_conv + n_z:
                    q = 2 * (j - n_conv)
                    hi, lo = (w[:, q:q + 2, :].rearrange("p a b -> p (a b)") for w in (wz_hi, wz_lo))
                    wait_ge(dve, z_ready, TT * g)
                else:
                    hi, lo = c.w_hi[:, u % 2, 0:UNIT], c.w_lo[:, u % 2, 0:UNIT]
                v_.scalar_tensor_tensor(lo, c.w_raw[:, u % 2, 0:UNIT], WSCALE, hi, ALU.mult, ALU.subtract
                                        ).then_inc(c.w_lo_ready, 1)

            def convolve(g, j):
                wait_ge(dve, pad_ready, 4 * (j + 1) + 4 * n_conv * g)
                wait_ge(dve, hist_put, j + 1 + n_conv * g)
                seqs = sequences(pad[:, j % 2, :], 3)
                outs = xbc[:, j, 0:SEQ], by_stream(xbc[:, j, :])
                for tap in range(4):
                    wt = taps[:, tap, ds(n_conv * g + j, 1)]
                    if tap:
                        wait_ge(dve, tap_done, 8 * j + 2 * tap + 8 * n_conv * g)
                    for out, seq in zip(outs, seqs):
                        if tap == 0:
                            ins = v_.tensor_scalar(out, seq(0), wt, None, ALU.mult)
                        else:
                            ins = v_.scalar_tensor_tensor(out, seq(tap), wt, out, ALU.mult, ALU.add)
                        ins.then_inc(tap_done, 1)

            def silu_z(g, t):
                v = TT * g + t
                wait_ge(dve, tanh_ready, v + 1)
                v_.scalar_tensor_tensor(zt, zt, 1.0, ps_z[:, :], ALU.add, ALU.mult).then_inc(zt_ready, 1)

            def inputs(g, t):
                v, p = TT * g + t, t % 2
                wait_ge(dve, bc_ready, v + 1)
                wait_ge(dve, st_ready, max(0, t - 1) + PER_ST * g)
                if t < 2:
                    wait_ge(dve, bm_ready, g)
                v_.tensor_copy(b_tok[:, p, :], ps_bc[:, 0:P]).then_inc(b_ready, 1)
                wait_ge(dve, w_ready, v)
                v_.tensor_tensor(cbm, ps_bc[:, P:2 * P], c.tri_incl if t < LAST else c.tri_block, ALU.mult
                                 ).then_inc(cb_ready, 1)
                wait_ge(dve, cb_ready, v + 1)
                wait_ge(dve, exp_ready, v + 1)
                v_.tensor_tensor(e[:, p], e[:, p], cbm.unsqueeze(1).to_broadcast([P, SHPG, P]), ALU.mult
                                 ).then_inc(w_ready, 1)
                wait_ge(dve, xdt_ready, v + 1)
                v_.tensor_tensor(heads(xdec[:, p, :]), heads(xdt[:, p, :]), of_heads(head_cols(m.dend[:, t, :], g)),
                                 ALU.mult).then_inc(xdec_ready, 1)

            def outputs(g, t):
                v, p = TT * g + t, t % 2
                for k in range(STREAMS if t == LAST else 1):
                    wait_ge(dve, st_ready, t + 1 + k + PER_ST * g)
                    wait_ge(dve, dec_ready, t + 1 + k + PER_ST * g)
                    v_.tensor_tensor(state[:, ring[k] if t == LAST else 0, :], decayed, ps_st[:, :], ALU.add
                                     ).then_inc(h_ready, 1)
                wait_ge(dve, yo_ready, v + 1)
                wait_ge(dve, gated, v)
                v_.tensor_tensor(heads(yt), heads(ps_yo[:, :]), of_heads(head_cols(m.ea[:, t, :], g)), ALU.mult
                                 ).then_inc(yo_used, 1)
                wait_ge(dve, yo_used, v + 1)
                wait_ge(dve, yd_ready, v + 1)
                v_.tensor_tensor(yt, ps_yd[:, :], yt, ALU.add).then_inc(yd_used, 1)
                wait_ge(dve, yd_used, v + 1)
                wait_ge(dve, xd_ready, v + 1)
                v_.tensor_tensor(yt, yt, x_tok[:, p, :], ALU.add).then_inc(y_done, 1)
                wait_ge(dve, y_done, v + 1)
                wait_ge(dve, zt_ready, v + 1)
                v_.scalar_tensor_tensor(xbc[:, 0:4, chunk(t)], yt.rearrange("p (j k) -> p j k", j=4), 0.5 / WSCALE,
                                        zt.rearrange("p (j k) -> p j k", j=4), ALU.mult, ALU.mult
                                        ).then_inc(gated, 1)

            def normed(g, t):
                v = TT * g + t
                wait_ge(dve, root_ready, v + 1)
                v_.reciprocal(inv[:, t:t + 1], root[:, t:t + 1]).then_inc(inv_ready, 1)
                wait_ge(dve, inv_ready, v + 1)
                yc = xbc[:, 0:4, chunk(t)]
                v_.tensor_scalar(yc, yc, inv[:, t:t + 1], None, ALU.mult).then_inc(yn_ready, 1)

            def result_lo(g, t):
                wait_ge(dve, ghi_ready, t + 1 + TT * g)
                for j in range(4):
                    ins = v_.scalar_tensor_tensor(g_lo[:, j, chunk(t)], ps_x[:, j * P:(j + 1) * P],
                                                  gains[:, ds(4 * g + j, 1)], g_hi[:, j, chunk(t)],
                                                  ALU.mult, ALU.subtract)
                ins.then_inc(glo_ready, 1)

            def group(g, last):
                wait_ge(dve, t_ready, TT * g)
                for j in range(n_conv):
                    convolve(g, j)
                    wait_ge(dve, acc_ready, 3 * (j + 1) + per_acc * g)
                    split(g, j + 2)
                for j in range(n_conv + 2, n_conv + n_z + 2):
                    split(g, j)
                for r in range(3):
                    wait_ge(dve, state_stored[r], 16 * (uses[r] + (r == 0)) * g)
                v_.memset(state[:, 0, :], 0.0).then_inc(h_ready, 1)
                for i in range(TT + 2):
                    if i >= 2:
                        normed(g, i - 2)
                    if 1 <= i <= TT:
                        silu_z(g, i - 1)
                    if i < TT:
                        inputs(g, i)
                    if 1 <= i <= TT:
                        outputs(g, i - 1)
                    if i >= 2:
                        result_lo(g, i - 2)
                first = isinstance(g, int) and g == 0
                for q in range(n_out):
                    for n in range(2):
                        for b in range(BLOCKS):
                            y_n = 6 * q + 3 * n + b
                            wait_ge(dve, acc_ready, 3 * n_conv + y_n + 1 + per_acc * g)
                            y = c.y[:, 2 * q + n, blk(b)]
                            if first:
                                ins = v_.tensor_scalar(y, bank[b][:, 0:BW], 1 / WSCALE, None, ALU.mult)
                            else:
                                ins = v_.scalar_tensor_tensor(y, bank[b][:, 0:BW], 1 / WSCALE, y, ALU.mult, ALU.add)
                            ins.then_inc(y_ready, 1)
                            if last:
                                if y_n:
                                    add_square(y_n - 1)
                    wait_ge(dve, acc_ready, 3 * n_conv + 6 * (q + 1) + per_acc * g)
                    split(g, n_conv + n_z + 2 + q, last)
                if last:
                    add_square(6 * n_out - 1)

            def add_square(n):
                b = n % 3
                dve.wait_ge(ysq_ready, n + 1)
                if n < 3:
                    ins = v_.tensor_copy(c.acc[:, blk(b)], sq[:, b, :])
                else:
                    dve.wait_ge(ysum_done, n - 2)
                    ins = v_.tensor_tensor(c.acc[:, blk(b)], c.acc[:, blk(b)], sq[:, b, :], ALU.add)
                ins.then_inc(ysum_done, 1)

            each_group(dve, group)

        @block.gpsimd
        def _(pool):
            p_ = nc.gpsimd
            pool.wait_ge(small_loaded, 64)

            def keep_history(g, j):
                _, streams = sequences(pad[:, j % 2, :], 3)
                row = n_conv * g + j
                old = hist[:, ds(row, 1), 0, :].rearrange("p a t -> p (a t)")
                olds = hist[:, ds(row, 1), 1:1 + STREAMS, :].rearrange("p a s t -> p (a s) t")
                if j < 2:
                    wait_ge(pool, t_ready, TT * g)
                else:
                    wait_ge(pool, tap_done, 8 * (j - 1) + 8 * n_conv * g)
                p_.tensor_copy(pad[:, j % 2, 0:3], old)
                p_.tensor_copy(streams(0, 3), olds).then_inc(hist_put, 1)
                wait_ge(pool, pad_ready, 4 * (j + 1) + 4 * n_conv * g)
                wait_ge(pool, hist_put, j + 1 + n_conv * g)
                alone(pool)
                p_.tensor_copy(old, pad[:, j % 2, SEQ:SEQ + 3])
                p_.tensor_copy(olds, streams(STEP, 3)).then_inc(hist_kept, 1)

            def seg_input(g, t):
                v, p = TT * g + t, t % 2
                if t == 1:
                    wait_ge(pool, yo_ready, TT * g)
                else:
                    wait_ge(pool, seg_ready, v - 1 if t else v)
                p_.tensor_tensor(seg_in[:, p], c.tri_strict.unsqueeze(1).to_broadcast([P, SHPG, P]),
                                 head_cols(m.da[:, t, :], g).unsqueeze(2).to_broadcast([P, SHPG, P]),
                                 ALU.mult).then_inc(segin_ready, 1)

            def inputs(g, t):
                v, p = TT * g + t, t % 2
                wait_ge(pool, x_copied, v + 1)
                wait_ge(pool, yd_ready, v - 1 if t >= 2 else TT * g)
                wait_ge(pool, xdec_ready, v - 1 if t >= 2 else TT * g)
                p_.tensor_tensor(heads(xdt[:, p, :]), heads(x_tok[:, p, :]), of_heads(head_cols(m.dt[:, t, :], g)),
                                 ALU.mult).then_inc(xdt_ready, 1)
                if t < LAST:
                    wait_ge(pool, h_ready, t + 1 + PER_H * g)
                    p_.tensor_tensor(heads(decayed), heads(state[:, 0, :]),
                                     of_heads(head_cols(m.chunk_decay[:, t, :], g)), ALU.mult).then_inc(dec_ready, 1)
                wait_ge(pool, xdt_ready, v + 1)
                alone(pool)
                p_.tensor_tensor(heads(x_tok[:, p, :]), heads(x_tok[:, p, :]), of_heads(head_cols(m.d, g)),
                                 ALU.mult).then_inc(xd_ready, 1)

            def streams_inputs(g):
                q = 1 - LAST % 2
                wait_ge(pool, seg_ready, TT - 1 + TT * g)
                alone(pool)
                p_.memset(seg_in[:, q], 0.0).then_inc(cm_zero, 1)
                wait_ge(pool, cm_zero, 1 + g)
                alone(pool)
                for k in range(STREAMS):
                    p_.tensor_copy(seg_in[:, q, k, k * STEP:(k + 1) * STEP],
                                   xbc[:, 5, SEQ + k * STEP:SEQ + (k + 1) * STEP]).then_inc(cm_ready, 1)
                wait_ge(pool, yd_ready, TT - 1 + TT * g)
                wait_ge(pool, b_ready, TT + TT * g)
                p_.tensor_tensor(e[:, q], b_tok[:, LAST % 2, :].unsqueeze(1).to_broadcast([P, STREAMS, P]),
                                 c.stream_mask.unsqueeze(2).to_broadcast([P, STREAMS, P]), ALU.mult
                                 ).then_inc(bm_ready, 1)

            def stream_decays(g):
                for k in range(STREAMS):
                    r = ring[k]
                    wait_ge(pool, state_loaded[r], 16 * (turn[k] + 1) + 16 * uses[r] * g)
                    wait_ge(pool, h_ready, LAST + 1 + k + PER_H * g)
                    p_.tensor_tensor(heads(decayed), heads(state[:, r, :]),
                                     of_heads(head_cols(m.stream_decay[:, k, :], g)), ALU.mult
                                     ).then_inc(dec_ready, 1)

            def group(g, last):
                for j in range(n_conv):
                    keep_history(g, j)
                seg_input(g, 0)
                for t in range(TT):
                    if t < LAST:
                        seg_input(g, t + 1)
                    inputs(g, t)
                streams_inputs(g)
                stream_decays(g)

            each_group(pool, group)



MATRICES = ("ident", "ones", "swap", "tri_incl", "tri_strict", "tri_block", "block_ones")


def build(nc, a):
    c_ctx = ExitStack()
    with c_ctx as ctx:
        c = Core(nc, ctx, [(a["ab_w_in"], UNIT), (a["ab_w_out"], UNIT), (a["gate_up0"], UNIT),
                           (a["down0"], DOWN_K * P), (a["dt_w"], KD * SHEADS), (a["ssm_w"], UNIT),
                           (a["gate_up1"], UNIT), (a["down1"], DOWN_K * P)])
        starts = c.starts
        c.x_hi, c.x_lo = c.sbuf("x_hi", [P, KD, T], F16), c.sbuf("x_lo", [P, KD, T], F16)
        c.y = c.sbuf("y", [P, KD, T], F32)
        c.acc = c.sbuf("acc", [P, T], F32)
        c.eps = c.sbuf("eps", [P, 1], F32)
        c.consts = c.sbuf("consts", [P, len(MATRICES) * P + STREAMS], F32)
        c.gains = c.sbuf("gains", [P, 2 * 4 * KD], F32)
        (c.ident, c.ones, c.swap, c.tri_incl, c.tri_strict, c.tri_block, c.block_ones) = (
            c.consts[:, n * P:(n + 1) * P] for n in range(len(MATRICES)))
        c.stream_mask = c.consts[:, len(MATRICES) * P:]
        c.gain = lambda layer, which, j: c.gains[:, (layer * 4 + which) * KD + j:(layer * 4 + which) * KD + j + 1]
        x1, x2, x3 = a["x1"], a["x2"], a["x3"]

        stage_load(c, a)
        c.end_stage()
        with ExitStack() as mixer:
            c.cat_hi, c.cat_lo = (c.sbuf(n, [P, KD, T], F16, mixer) for n in ("cat_hi", "cat_lo"))
            with ExitStack() as heads:
                q = c.y[:, 0:4, :].rearrange("p j t -> p (j t)")
                c.q_prompt = q[:, 0:4 * SEQ].rearrange("p (n j q) -> p n j q", j=4, q=CHUNK)
                c.q_stream = q[:, 4 * SEQ:4 * T].rearrange("p (n j q) -> p n j q", j=4, q=STEP)
                c.k, c.v = c.y[:, 4, :], c.y[:, 5, :]
                stage_qkv(c, a, 0)
                c.end_stage()
                with ExitStack() as conv:
                    c.conv = c.sbuf("conv", [P, 4, T], F32, conv)
                    stage_conv(c, a, 6)
                    c.end_stage()
                    stage_gate_b(c, a, 14)
                    c.end_stage()
                stage_attention(c, a)
                c.end_stage()
            stage_project_y(c, "ao", starts[1], 1, KD, c.cat_hi, c.cat_lo)
            c.end_stage()
        stage_residual(c, "r0", 0, 1, a["x"], x1, False)
        c.end_stage()
        feed_forward(c, "f0", starts[2], 0, x1, x2, False)
        with ExitStack() as mixer:
            m = SSM(c, mixer)
            stage_dt(c, a, starts[4], m)
            c.end_stage()
            stage_ssm(c, a, starts[5], m)
            c.end_stage()
        stage_residual(c, "r1", 1, 1, x2, x3, False)
        c.end_stage()
        feed_forward(c, "f1", starts[6], 1, x3, a["y_out"], True)



def _units(w, k_tiles):
    k, n = w.shape
    w = w.reshape(k // (k_tiles * P), k_tiles, P, n // P, P)
    return w.transpose(3, 0, 2, 1, 4).reshape(-1, P, k_tiles * P)


def _features(x):
    t, f = x.shape
    return x.T.reshape(f // P, P, t).transpose(1, 0, 2)


def _constants():
    i = np.arange(P)
    same = (i[:, None] // STEP) == (i[None, :] // STEP)
    swap = np.zeros((P, P), np.float32)
    for r in range(P):
        d = r % HD
        if d < ROPE:
            swap[r - d + (d + ROPE // 2) % ROPE, r] = 1
    mats = [np.eye(P), np.ones((P, P)), swap, i[:, None] <= i[None, :], i[:, None] > i[None, :],
            (i[:, None] <= i[None, :]) & same, same, i[:, None] // STEP == np.arange(STREAMS)[None, :]]
    return np.concatenate([x.astype(np.float32) for x in mats], axis=1)


def _rope():
    half = ROPE // 2
    inv = np.power(np.float32(500000.0), -np.arange(half, dtype=np.float32) / np.float32(half)).astype(np.float32)
    pos = np.concatenate([np.arange(SEQ), np.tile(PAST + np.arange(STEP), STREAMS)]).astype(np.float32)
    ang = (inv[:, None] * pos[None, :]).astype(np.float32).astype(np.float64)
    cos, sin = np.ones((P, T)), np.zeros((P, T))
    for r in range(P):
        d = r % HD
        if d < ROPE:
            cos[r] = np.cos(ang[d % half])
            sin[r] = np.sin(ang[d % half]) * (-1 if d < half else 1)
    return np.stack([cos, sin], axis=1).astype(np.float32)


def _head_order(w, axis):
    w = np.moveaxis(w, axis, 0)
    w = w.reshape((2, GROUP, HD) + w.shape[1:]).swapaxes(0, 1).reshape((HEADS * HD,) + w.shape[1:])
    return np.moveaxis(w, 0, axis)


def _group_order(w):
    x, b, c = np.split(w, [SG * GW, SG * GW + SG * SN], axis=-1)
    lead = w.shape[:-1]
    parts = [y.reshape(lead + (SG, -1)) for y in (x, b, c)]
    return np.concatenate(parts, axis=-1)


def _arrays(i):
    f = np.ascontiguousarray
    out = {}
    tokens = np.concatenate([i["x_prompt"][0], i["x_sample"].reshape(STREAMS * STEP, D)])
    out["x"] = _features(tokens)
    out["consts"] = _constants()
    out["rope"] = _rope()
    out["norm_g"] = i["norm_g"].reshape(2 * 4 * KD, P).T
    w = i["ab_w_in"][0]
    q, rest = w[:, :HEADS * HD], w[:, HEADS * HD:]
    kv, gb, gc, hx = rest[:, :256], rest[:, 256:768], rest[:, 768:1280], rest[:, 1280:1792]
    pairs = np.stack([gc.reshape(D, 4, P), hx.reshape(D, 4, P)], axis=2).reshape(D, 1024)
    out["ab_w_in"] = _units(np.concatenate([_head_order(q, 1), kv, pairs, gb], axis=1), KD)
    w = i["ab_w_out"][0]
    out["ab_w_out"] = _units(np.concatenate([_head_order(w[:512], 0), w[512:]]), KD)
    out["sconv_w"] = i["sconv_w"][0].reshape(3, 4, P).transpose(2, 0, 1)
    out["sconv_hist"] = i["state_sconv"][0].reshape(STREAMS, 2, 4, P).transpose(3, 2, 0, 1)
    out["cache_k"] = i["cache_attn_k"][0].reshape(STREAMS, P, P).transpose(2, 0, 1)
    out["cache_v"] = i["cache_attn_v"][0].reshape(STREAMS, P, P).transpose(1, 0, 2)
    sinks = i["attn_sinks"][0].reshape(2, GROUP)
    prompt = np.repeat(sinks.reshape(4, 2), CHUNK, axis=1).T
    stream = np.concatenate([np.repeat(sinks, STEP, axis=1).T] * 2)
    both = np.zeros((P, 2, 8), np.float32)
    both[:, 0, :4], both[:, 1, :2] = prompt, stream
    out["sinks"] = both
    for layer in range(2):
        g, u = (i[n][layer].reshape(D, FT, 1, P) for n in ("ffn_w_gate", "ffn_w_up"))
        out[f"gate_up{layer}"] = _units(np.concatenate([g, u], axis=2).reshape(D, 2 * DFF), KD)
        out[f"down{layer}"] = _units(i["ffn_w_down"][layer], DOWN_K)
    w = i["ssm_w_in"][0]
    z, xbc, dt = np.split(w, [SG * GW, 2 * SG * GW + 2 * SG * SN], axis=1)
    out["dt_w"] = dt.reshape(KD, P, SHEADS).transpose(1, 0, 2).reshape(1, P, KD * SHEADS)
    grouped = _group_order(xbc)
    units = []
    for n in range(SG):
        z_n = z[:, n * GW:(n + 1) * GW].reshape(KD // 2, 2, P, GW).transpose(0, 2, 1, 3).reshape(-1, P, UNIT)
        o_n = i["ssm_w_out"][0][n * GW:(n + 1) * GW].reshape(4, P, 4, 2 * P).transpose(2, 1, 0, 3).reshape(-1, P, UNIT)
        units += [_units(grouped[:, n], KD), z_n, o_n]
    out["ssm_w"] = np.concatenate(units)
    rows = np.stack([i["ssm_dt_bias"][0], i["ssm_a_log"][0], i["ssm_d"][0]])
    out["ssm_rows"] = np.repeat(rows[None], P, axis=0)
    out["ssm_taps"] = _group_order(i["ssm_conv_w"][0]).reshape(4, 24, P).transpose(2, 0, 1)
    out["ssm_bias"] = _group_order(i["ssm_conv_b"][0]).reshape(24, P).T
    hist = _group_order(i["state_ssm_conv"][0]).reshape(STREAMS, 3, 24, P).transpose(3, 2, 0, 1)
    out["ssm_hist"] = np.concatenate([np.zeros((P, 24, 1, 3), np.float32), hist], axis=2)
    out["ssm_gains"] = i["ssm_norm_g"][0].reshape(16, P).T
    out["state"] = i["state_ssm"][0].reshape(STREAMS, SHEADS * SHD, SN).transpose(0, 2, 1)
    return {k: f(v) for k, v in out.items()}


OUTS = {"y_out": (P, KD, T), "kv_prompt": (2, P, P), "kv_sample": (2, P, P), "new_sconv": (P, 4, 1 + STREAMS, 2),
        "new_ssm_hist": (P, 24, 1 + STREAMS, 3), "new_state_prompt": (P, SHEADS * SHD),
        "new_state": (STREAMS, P, SHEADS * SHD)}


def _results(r):
    y = r["y_out"].transpose(2, 1, 0).reshape(T, D)
    kvp = r["kv_prompt"].transpose(0, 2, 1).reshape(2, 1, 1, P, 2, HD)
    kvs = r["kv_sample"].transpose(0, 2, 1).reshape(2, 1, STREAMS, STEP, 2, HD)
    sc = r["new_sconv"].transpose(2, 3, 1, 0).reshape(1 + STREAMS, 2, 512)
    h = r["new_ssm_hist"].transpose(2, 3, 1, 0).reshape(1 + STREAMS, 3, SG, 6 * P)
    x, b, cc = (p.reshape(1 + STREAMS, 3, -1) for p in (h[..., :GW], h[..., GW:GW + SN], h[..., GW + SN:]))
    hist = np.concatenate([x, b, cc], axis=-1)
    sp = r["new_state_prompt"].T.reshape(1, 1, SHEADS, SHD, SN)
    ss = r["new_state"].transpose(0, 2, 1).reshape(1, STREAMS, SHEADS, SHD, SN)
    outs = (y[:SEQ].reshape(1, SEQ, D), y[SEQ:].reshape(STREAMS, STEP, D), kvp[0], kvp[1], sc[None, :1],
            hist[None, :1], sp, kvs[0], kvs[1], sc[None, 1:], hist[None, 1:], ss)
    return tuple(np.ascontiguousarray(o) for o in outs)


def kernel(**inputs):
    import concourse.bacc as bacc
    from concourse.bass_utils import run_bass_kernel_spmd

    arrays = _arrays({k: np.asarray(v) for k, v in inputs.items()})
    nc = bacc.Bacc("TRN2", target_bir_lowering=False, num_devices=1, dynamic_dma_scratch_size=1024)
    aps = {k: nc.dram_tensor("in_" + k, v.shape, F32, kind="ExternalInput").ap() for k, v in arrays.items()}
    aps |= {k: nc.dram_tensor("out_" + k, s, F32, kind="ExternalOutput").ap() for k, s in OUTS.items()}
    aps |= {k: nc.dram_tensor("mid_" + k, (P, KD, T), F32, kind="Internal").ap() for k in ("x1", "x2", "x3")}
    build(nc, aps)
    r = run_bass_kernel_spmd(nc, [{"in_" + k: v for k, v in arrays.items()}], core_ids=[0]).results[0]
    return _results({k: r["out_" + k] for k in OUTS})
```

```python
from contextlib import ExitStack

import numpy as np

import concourse.bass as bass
from concourse import mybir

F32, F16 = mybir.dt.float32, mybir.dt.float16
AF = mybir.ActivationFunctionType
ALU = mybir.AluOpType
AX_X = mybir.AxisListType.X
ds = bass.ds

P = 128
D, SEQ, STREAMS, STEP = 1024, 1024, 8, 16
T = SEQ + STREAMS * STEP
TT = T // P
BLOCKS, BW = 3, T // 3
BT = TT // BLOCKS
KD = D // P
HEADS, GROUP, HD, CHUNK = 8, 4, 64, 64
PAST = 512
ROPE = HD // 4
DFF = 2816
FT = DFF // P
DOWN_K = FT // 2
SG, SHPG, SHD, SN = 4, 8, 64, 128
SHEADS = SG * SHPG
GW = SHPG * SHD
UNIT = KD * P
WSCALE = 64.0
EPS = 1e-6
MODEL_SCALE = 1.0 / D
XW = SEQ + 2 + STREAMS * (STEP + 2)
XW3 = SEQ + 3 + STREAMS * (STEP + 3)


def sizes(segment):
    return segment[0].shape[0], segment[1]


class Core:

    def __init__(self, nc, ctx, segments):
        self.nc, self.ctx = nc, ctx
        self.stage_sems = []
        self.segments = segments
        self.starts = [0]
        for w, _ in segments:
            self.starts.append(self.starts[-1] + w.shape[0])
        most = max(f for _, f in segments)
        self.w_raw = self.sbuf("w_raw", [P, 2, most], F32)
        self.w_hi = self.sbuf("w_hi", [P, 2, most], F16)
        self.w_lo = self.sbuf("w_lo", [P, 2, most], F16)
        self.w_loaded = [self.sem("w_loaded0"), self.sem("w_loaded1")]
        self.w_hi_ready = self.sem("w_hi_ready")
        self.w_lo_ready = self.sem("w_lo_ready")
        self.x_stored = self.sem("x_stored")
        self.x_stores = 0
        self.stage_sems = []

    def sbuf(self, name, shape, dtype, ctx=None):
        return (ctx or self.ctx).enter_context(self.nc.sbuf_tensor(name, shape, dtype))

    def psum(self, name, shape, ctx):
        return ctx.enter_context(self.nc.psum_tensor(name, shape, F32))

    def sem(self, name):
        self.stage_sems.append(self.nc.alloc_semaphore(name))
        return self.stage_sems[-1]

    def end_stage(self):
        self.nc.clear_and_free_semaphores(self.stage_sems)
        self.nc.all_engine_barrier()
        self.stage_sems = []

    def segment_of(self, u):
        n = max(k for k, s in enumerate(self.starts[:-1]) if s <= u)
        return self.segments[n], self.starts[n]


    def load_weights(self, sp, u, i=0):
        if u >= self.starts[-1]:
            return
        (w, cols), start = self.segment_of(u)
        if u >= 2:
            sp.wait_ge(self.w_hi_ready, u - 1 + 2 * i)
            sp.wait_ge(self.w_lo_ready, u - 1 + 2 * i)
        src = w[ds(u - start + 2 * i, 1), :, :].rearrange("a p c -> (a p) c") if not isinstance(i, int) \
            else w[u - start + 2 * i, :, :]
        sp.dma_start(self.w_raw[:, u % 2, 0:cols], src).then_inc(self.w_loaded[u % 2], 16)

    def split_hi(self, act, u, i=0, acc=None, acc_value=None):
        if u >= self.starts[-1]:
            return
        cols = self.segment_of(u)[0][1]
        act.wait_ge(self.w_loaded[u % 2], 16 * (u // 2 + 1) + 16 * i)
        if acc is not None:
            act.wait_ge(acc, acc_value)
        self.nc.scalar.activation(self.w_hi[:, u % 2, 0:cols], self.w_raw[:, u % 2, 0:cols], AF.Copy,
                                  scale=WSCALE).then_inc(self.w_hi_ready, 1)

    def split_lo(self, dve, u, i=0, acc=None, acc_value=None):
        if u >= self.starts[-1]:
            return
        cols = self.segment_of(u)[0][1]
        if acc is not None:
            dve.wait_ge(acc, acc_value)
        dve.wait_ge(self.w_hi_ready, u + 1 + 2 * i)
        self.nc.vector.scalar_tensor_tensor(self.w_lo[:, u % 2, 0:cols], self.w_raw[:, u % 2, 0:cols], WSCALE,
                                            self.w_hi[:, u % 2, 0:cols], ALU.mult, ALU.subtract
                                            ).then_inc(self.w_lo_ready, 1)

    def weights_split(self, pe, u, i=0):
        pe.wait_ge(self.w_hi_ready, u + 1 + 2 * i)
        pe.wait_ge(self.w_lo_ready, u + 1 + 2 * i)

    def multiply(self, out, u, k_tiles, x_hi, x_lo, k0, cols, first, last, tile_ready=None):
        for k in range(k_tiles):
            if tile_ready is not None:
                tile_ready(k)
            wh = self.w_hi[:, u % 2, k * P:(k + 1) * P]
            wl = self.w_lo[:, u % 2, k * P:(k + 1) * P]
            xh, xl = x_hi[:, k0 + k, cols], x_lo[:, k0 + k, cols]
            self.nc.tensor.matmul(out, wh, xh, start=(first and k == 0), stop=False)
            self.nc.tensor.matmul(out, wh, xl, start=False, stop=False)
            mm = self.nc.tensor.matmul(out, wl, xh, start=False, stop=(last and k == k_tiles - 1))
        return mm


def blk(b):
    return slice(b * BW, (b + 1) * BW)


def run(engine, n, body):
    body(0, True, n == 1)
    if n > 3:
        with engine.Fori(1, n - 1) as i:
            body(i, False, False)
    else:
        for i in range(1, n - 1):
            body(i, False, False)
    if n > 1:
        body(n - 1, False, True)


def load_ring(c, sp, s, e):
    own = max(0, e - s - 4) // 2
    if own > 0:
        with sp.Fori(0, own) as i:
            c.load_weights(sp, s + 4, i)
            c.load_weights(sp, s + 5, i)
    for u in range(s + 4 + 2 * own, e + 4):
        c.load_weights(sp, u)


def split_u(c, eng, split, s, u, i, last, acc, per=BLOCKS):
    if last:
        n = u + 2 + 2 * i
        split(eng, n, 0, acc, per * (u + 2 * i - s + 1))
    else:
        split(eng, u + 2, i, acc, per * (u - s + 1) + 2 * per * i)



class Rms:

    def __init__(self, c, ctx, tag, banks, blocks):
        self.c, self.banks = c, banks
        self.nth = {b: n + 1 for n, b in enumerate(blocks)}
        self.sum_ready, self.root_ready, self.inv_ready, self.spread_ready = (
            c.sem(f"{tag}_{x}") for x in ("sum_ready", "root_ready", "inv_ready", "spread_ready"))
        self.root = c.sbuf(tag + "_root", [P, TT], F32, ctx)
        self.inv = c.sbuf(tag + "_inv", [P, TT], F32, ctx)

    def sums(self, pe, b):
        for k, t in enumerate(tiles_of(b)):
            mm = pe.matmul(self.banks[b][:, BW + k:BW + k + 1], self.c.acc[:, t * P:(t + 1) * P],
                           self.c.ones[:, 0:1], start=True, stop=True)
        mm.then_inc(self.sum_ready, 1)

    def roots(self, act, b):
        act.wait_ge(self.sum_ready, self.nth[b])
        self.c.nc.scalar.activation(self.root[:, BT * b:BT * (b + 1)], self.banks[b][:, BW:BW + BT], AF.Sqrt,
                                    bias=self.c.eps[:, 0:1], scale=MODEL_SCALE).then_inc(self.root_ready, 1)

    def inverses(self, dve, b):
        dve.wait_ge(self.root_ready, self.nth[b])
        cols = slice(BT * b, BT * (b + 1))
        self.c.nc.vector.reciprocal(self.inv[:, cols], self.root[:, cols]).then_inc(self.inv_ready, 1)

    def spread(self, pe, b):
        pe.wait_ge(self.inv_ready, self.nth[b])
        for k in range(BT):
            mm = pe.matmul(self.banks[b][:, k * P:(k + 1) * P],
                           self.inv[:, BT * b + k:BT * b + k + 1].to_broadcast([P, P]), self.c.ident,
                           start=True, stop=True)
        mm.then_inc(self.spread_ready, 1)


def tiles_of(b):
    return range(BT * b, BT * (b + 1))


class Lead:

    def __init__(self, c, ctx, tag, post, pre, x_in, x_out, banks, bufs, pool_lo=5, early=False, tail=False):
        self.c, self.post, self.pre, self.x_in, self.x_out, self.pool_lo = c, post, pre, x_in, x_out, pool_lo
        self.early, self.tail = early, tail
        blocks = list(range(BLOCKS))
        self.res = [] if not post else RES_EARLY if tail else blocks[len(RES_EARLY):] if early else blocks
        self.squares = SQ_EARLY if tail else [] if not pre else blocks[len(SQ_EARLY):] if early else blocks
        self.pool_x = not pre
        self.xr, self.sq, self.h = bufs
        self.slots = self.xr.shape[1] if post else 0
        self.ring = self.sq.shape[1]
        self.x_loaded = [[c.sem(f"{tag}_x_loaded{b}{k}") for k in range(2)] for b in range(BLOCKS)]
        if post:
            self.rms_y = Rms(c, ctx, tag + "_post", banks, self.res)
            self.scaled, self.x_ready = c.sem(tag + "_scaled"), c.sem(tag + "_x_ready")
            self.x_pool = c.sem(tag + "_x_pool")
        if self.squares:
            self.sq_ready, self.sum_done = c.sem(tag + "_sq"), c.sem(tag + "_sum")
        if pre:
            self.rms_x = Rms(c, ctx, tag + "_pre", banks, blocks)
            self.h_ready, self.hi_ready, self.lo_pool, self.lo_dve = (
                c.sem(f"{tag}_{x}") for x in ("h", "hi", "lo_pool", "lo_dve"))

    def x_done(self, engine, tiles):
        if self.pool_x:
            engine.wait_ge(self.x_ready, (tiles + 1) // 2)
            if tiles > 1:
                engine.wait_ge(self.x_pool, tiles // 2)
        else:
            engine.wait_ge(self.x_ready, tiles)


    def load_x(self, sp, n):
        b, half = self.res[n], KD // 2
        for k in range(2):
            if n >= self.slots:
                self.x_done(sp, KD * (n - self.slots) + half * (k + 1))
            rows = slice(k * half, (k + 1) * half)
            sp.dma_start(self.xr[:, n % self.slots, rows], self.x_in[:, rows, blk(b)]).then_inc(self.x_loaded[b][k], 16)

    def store_x(self, sp, n):
        half = KD // 2
        for k in range(2):
            self.x_done(sp, KD * n + half * (k + 1))
            rows, cols = slice(k * half, (k + 1) * half), blk(self.res[n])
            sp.dma_start(self.x_out[:, rows, cols], self.c.y[:, rows, cols]).then_inc(self.c.x_stored, 16)
            self.c.x_stores += 1

    def sync(self, sp, between=None):
        if not self.post:
            half = KD // 2
            for b in range(BLOCKS):
                for k in range(2):
                    rows = slice(k * half, (k + 1) * half)
                    sp.dma_start(self.c.y[:, rows, blk(b)], self.x_in[:, rows, blk(b)]
                                 ).then_inc(self.x_loaded[b][k], 16)
                between(b)
            return
        for n in range(len(self.res)):
            self.load_x(sp, n)
        for n in range(len(self.res)):
            self.store_x(sp, n)

    def sync_end(self, sp):
        if self.post:
            sp.wait_ge(self.c.x_stored, 16 * self.c.x_stores)


    def tensor(self, pe, work=None):
        if self.early and self.pre:
            self.rms_x.sums(pe, 0)
            self.rms_y.sums(pe, self.res[0])
            self.rms_x.spread(pe, 0)
            self.rms_y.spread(pe, self.res[0])
        elif self.post:
            for n in range(min(2, len(self.res))):
                self.rms_y.sums(pe, self.res[n])
            for n, b in enumerate(self.res):
                self.rms_y.spread(pe, b)
                if n + 2 < len(self.res):
                    self.rms_y.sums(pe, self.res[n + 2])
        if not self.pre:
            return
        if not self.early:
            self.sums(pe, 0)
            self.rms_x.spread(pe, 0)
        for b in range(BLOCKS):
            work(b, 0, self.tile_ready(pe, b))
            if b + 1 == BLOCKS:
                work(b, 1, None)
                return
            self.sums(pe, b + 1)
            spread_done = []

            def between(k):
                if k == KD // 2:
                    self.rms_x.spread(pe, b + 1)
                    spread_done.append(b)

            work(b, 1, between)
            if not spread_done:
                self.rms_x.spread(pe, b + 1)

    def sums(self, pe, b):
        if b in self.squares:
            pe.wait_ge(self.sum_done, (KD - 1) * (self.squares.index(b) + 1))
        self.rms_x.sums(pe, b)

    def tile_ready(self, pe, b):
        def wait(k):
            if k < self.pool_lo:
                pe.wait_ge(self.lo_pool, self.pool_lo * b + k + 1)
            else:
                pe.wait_ge(self.lo_dve, (KD - self.pool_lo) * b + k - self.pool_lo + 1)
        return wait


    def in_turn(self, begin, root, finish, between=None):
        begin(0, range(KD))
        if between is not None:
            between()
        for b in range(BLOCKS):
            if b + 1 < BLOCKS:
                begin(b + 1, range(0, 3))
            if b or not self.early:
                root(b)
            if b + 1 < BLOCKS:
                begin(b + 1, range(3, 4))
            finish(b)
            if b + 1 < BLOCKS:
                begin(b + 1, range(4, KD))

    def residual(self, dve, b, tiles):
        if b not in self.res:
            return
        v, c, n = self.c.nc.vector, self.c, self.res.index(b)

        def scale(j):
            y = c.y[:, j, blk(b)]
            v.scalar_tensor_tensor(y, y, c.gain(*self.post, j), self.rms_y.banks[b][:, 0:BW],
                                   ALU.mult, ALU.mult).then_inc(self.scaled, 1)

        def add_x(j):
            if self.pool_x and j % 2:
                return
            y = c.y[:, j, blk(b)]
            dve.wait_ge(self.x_loaded[b][2 * j // KD], 16)
            dve.wait_ge(self.scaled, KD * n + j + 1)
            v.tensor_tensor(y, y, self.xr[:, n % self.slots, j], ALU.add).then_inc(self.x_ready, 1)

        dve.wait_ge(self.rms_y.spread_ready, self.rms_y.nth[b])
        for j in tiles:
            scale(j)
            if j > tiles[0]:
                add_x(j - 1)
        add_x(tiles[-1])

    def vector(self, dve, between=None):
        v, c = self.c.nc.vector, self.c

        def begin(b, tiles):
            if len(self.res) > 2 and b == 0:
                self.rms_y.inverses(dve, self.res[2])
            self.residual(dve, b, tiles)

        def root(b):
            self.rms_x.inverses(dve, b)

        def finish(b):
            dve.wait_ge(self.rms_x.spread_ready, b + 1)
            for j in range(KD):
                if b:
                    if j < self.pool_lo:
                        dve.wait_ge(self.lo_pool, self.pool_lo * (b - 1) + j + 1)
                    else:
                        dve.wait_ge(self.lo_dve, (KD - self.pool_lo) * (b - 1) + j - self.pool_lo + 1)
                v.scalar_tensor_tensor(self.h[:, j], c.y[:, j, blk(b)], c.gain(*self.pre, j),
                                       self.rms_x.banks[b][:, 0:BW], ALU.mult, ALU.mult
                                       ).then_inc(self.h_ready, 1)
            for j in range(self.pool_lo, KD):
                dve.wait_ge(self.hi_ready, KD * b + j + 1)
                v.tensor_tensor(c.x_lo[:, j, blk(b)], self.h[:, j], c.x_hi[:, j, blk(b)], ALU.subtract
                                ).then_inc(self.lo_dve, 1)

        if self.early and self.pre:
            root(0)
        for b in self.res[:2]:
            self.rms_y.inverses(dve, b)
        if self.pre:
            self.in_turn(begin, root, finish, between)
        else:
            for b in self.res:
                begin(b, range(KD))

    def square(self, act, b, tiles):
        if b not in self.squares:
            return
        c = self.c
        for j in tiles:
            if self.post and b in self.res:
                self.x_done(act, KD * self.res.index(b) + j + 1)
            elif not self.post:
                act.wait_ge(self.x_loaded[b][2 * j // KD], 16)
            n = (KD - 1) * self.squares.index(b) + j - 1
            if j and n >= self.ring:
                act.wait_ge(self.sum_done, n - self.ring + 1)
            out = self.sq[:, n % self.ring] if j else c.acc[:, blk(b)]
            self.c.nc.scalar.activation(out, c.y[:, j, blk(b)], AF.Square).then_inc(self.sq_ready, 1)

    def scalar(self, act, between=None):
        a, c = self.c.nc.scalar, self.c

        def root(b):
            self.rms_x.roots(act, b)

        def finish(b):
            for j in range(KD):
                act.wait_ge(self.h_ready, KD * b + j + 1)
                a.copy(c.x_hi[:, j, blk(b)], self.h[:, j]).then_inc(self.hi_ready, 1)

        if self.early and self.pre:
            root(0)
        for b in self.res:
            self.rms_y.roots(act, b)
        if self.pre:
            self.in_turn(lambda b, tiles: self.square(act, b, tiles), root, finish, between)

    def add_x_pool(self, pool, b):
        n, c = self.res.index(b), self.c
        for j in range(1, KD, 2):
            pool.wait_ge(self.x_loaded[b][2 * j // KD], 16)
            pool.wait_ge(self.scaled, KD * n + j + 1)
            y = c.y[:, j, blk(b)]
            c.nc.gpsimd.tensor_tensor(y, y, self.xr[:, n % self.slots, j], ALU.add).then_inc(self.x_pool, 1)

    def add_squares(self, pool, b, tiles):
        for j in tiles if b in self.squares else ():
            if j:
                i = self.squares.index(b)
                n = (KD - 1) * i + j - 1
                pool.wait_ge(self.sq_ready, KD * i + j + 1)
                if n:
                    pool.wait_ge(self.sum_done, n)
                acc = self.c.acc[:, blk(b)]
                self.c.nc.gpsimd.tensor_tensor(acc, acc, self.sq[:, n % self.ring], ALU.add).then_inc(self.sum_done, 1)

    def gpsimd(self, pool):
        g, c = self.c.nc.gpsimd, self.c

        def finish(b):
            for j in range(self.pool_lo):
                pool.wait_ge(self.hi_ready, KD * b + j + 1)
                g.tensor_tensor(c.x_lo[:, j, blk(b)], self.h[:, j], c.x_hi[:, j, blk(b)], ALU.subtract
                                ).then_inc(self.lo_pool, 1)

        if self.pre:
            self.in_turn(lambda b, tiles: self.add_squares(pool, b, tiles), lambda b: None, finish)
            return
        for b in self.res:
            self.add_x_pool(pool, b)


RES_EARLY, SQ_EARLY = [0, 1], [0]


def lead_buffers(c, ctx, tag, slots=2, ring=4, h=True):
    xr = c.sbuf(tag + "_xr", [P, slots, KD, BW], F32, ctx) if slots else None
    return xr, c.sbuf(tag + "_sq", [P, ring, BW], F32, ctx), c.sbuf(tag + "_h", [P, KD, BW], F32, ctx) if h else None



def stage_qkv(c, a, s):
    nc, n, rot = c.nc, 6, 5
    with ExitStack() as ctx:
        tables = c.sbuf("rope_tables", [P, 2, T], F32, ctx)
        raw = c.sbuf("qkv_raw", [P, 3, BW], F32, ctx)
        part = c.sbuf("rope_parts", [P, 2, 2, BW], F32, ctx)
        bank = [c.psum(f"qkv{b}", [P, 512], ctx) for b in range(3)]
        swapped = [c.psum(f"swapped{b}", [P, 512], ctx) for b in range(3)]
        lead = Lead(c, ctx, "n0_lead", None, (0, 0), a["x"], None, swapped,
                    lead_buffers(c, ctx, "n0", 0), pool_lo=2)
        tables_loaded, kv_stored = c.sem("tables_loaded"), c.sem("kv_stored")
        consts_loaded, eps_set = c.sem("consts_loaded"), c.sem("eps_set")
        acc_ready, raw_ready, swap_ready, v_ready = (c.sem(x) for x in
                                                     ("qkv_acc", "qkv_raw_ready", "qkv_swapped", "v_ready"))
        cos_done, sin_done, rope_done = c.sem("rope_cos"), c.sem("rope_sin"), c.sem("rope_done")
        block = ctx.enter_context(nc.Block())

        def q_parts(j, b):
            lo, hi = b * BW // CHUNK, min((b + 1) * BW, SEQ) // CHUNK
            parts = [(c.q_prompt[:, lo:hi, j, :], 0, (hi - lo) * CHUNK)]
            if b == BLOCKS - 1:
                parts.append((c.q_stream[:, :, j, :], (hi - lo) * CHUNK, BW))
            return parts

        @block.sync
        def _(sp):
            def constants_and_weights(b):
                if b == 0:
                    sp.dma_start(c.consts[:, :], a["consts"]).then_inc(consts_loaded, 16)
                    sp.dma_start(c.gains[:, :], a["norm_g"]).then_inc(consts_loaded, 16)
                    c.load_weights(sp, 0)
                if b == 1:
                    c.load_weights(sp, 1)

            lead.sync(sp, constants_and_weights)
            c.load_weights(sp, 2)
            c.load_weights(sp, 3)
            sp.dma_start(tables[:, :, :], a["rope"]).then_inc(tables_loaded, 16)
            load_ring(c, sp, s, s + n)
            sp.wait_ge(rope_done, 3 * rot)
            sp.wait_ge(v_ready, 3)
            sp.dma_start(a["kv_prompt"][0], c.k[:, SEQ - P:SEQ]).then_inc(kv_stored, 16)
            sp.dma_start(a["kv_prompt"][1], c.v[:, SEQ - P:SEQ]).then_inc(kv_stored, 16)
            sp.dma_start(a["kv_sample"][0], c.k[:, SEQ:T]).then_inc(kv_stored, 16)
            sp.dma_start(a["kv_sample"][1], c.v[:, SEQ:T]).then_inc(kv_stored, 16)
            sp.wait_ge(kv_stored, 64)

        @block.tensor
        def _(pe):
            def swap(m):
                pe.wait_ge(raw_ready, m + 1)
                if m >= 3:
                    pe.wait_ge(sin_done, m - 2)
                pe.matmul(swapped[m % 3][:, 0:BW], c.swap, raw[:, m % 3, :], start=True,
                          stop=True).then_inc(swap_ready, 1)

            def first_unit(b, part, hook):
                if part == 0:
                    c.multiply(bank[b][:, 0:BW], s, KD, c.x_hi, c.x_lo, 0, blk(b), True, True, hook
                               ).then_inc(acc_ready, 1)

            pe.wait_ge(consts_loaded, 32)
            c.weights_split(pe, s)
            lead.tensor(pe, first_unit)
            swap(0)
            swap(1)
            for j in range(1, n):
                c.weights_split(pe, s + j)
                for b in range(BLOCKS):
                    m = 3 * j + b
                    pe.wait_ge(raw_ready, m - 2)
                    c.multiply(bank[b][:, 0:BW], s + j, KD, c.x_hi, c.x_lo, 0, blk(b), True, True
                               ).then_inc(acc_ready, 1)
                    if m <= 3 * rot:
                        swap(m - 1)

        @block.scalar
        def _(act):
            act.wait_ge(eps_set, 1)
            lead.scalar(act, lambda: (c.split_hi(act, 0), c.split_hi(act, 1)))
            for j in range(n):
                for b in range(BLOCKS):
                    m = 3 * j + b
                    act.wait_ge(acc_ready, m + 1)
                    if j < rot:
                        if m >= 3:
                            act.wait_ge(swap_ready, m - 2)
                            act.wait_ge(cos_done, m - 2)
                        nc.scalar.mul(raw[:, b, :], bank[b][:, 0:BW], 1 / WSCALE).then_inc(raw_ready, 1)
                    else:
                        nc.scalar.mul(c.v[:, blk(b)], bank[b][:, 0:BW], 1 / WSCALE).then_inc(v_ready, 1)
                c.split_hi(act, s + j + 2, 0, acc_ready, 3 * (j + 1))

        @block.vector
        def _(dve):
            nc.vector.memset(c.eps[:, :], EPS).then_inc(eps_set, 1)
            dve.wait_ge(consts_loaded, 32)
            lead.vector(dve, lambda: (c.split_lo(dve, 0), c.split_lo(dve, 1)))
            dve.wait_ge(tables_loaded, 16)
            for j in range(n):
                for b in range(BLOCKS if j < rot else 0):
                    m = 3 * j + b
                    parts = q_parts(j, b) if j < rot - 1 else [(c.k[:, blk(b)], 0, BW)]
                    dve.wait_ge(raw_ready, m + 1)
                    if m >= 2:
                        dve.wait_ge(rope_done, m - 1)
                    nc.vector.tensor_tensor(part[:, 0, m % 2, :], raw[:, b, :], tables[:, 0, blk(b)],
                                            ALU.mult).then_inc(cos_done, 1)
                    dve.wait_ge(swap_ready, m + 1)
                    nc.vector.tensor_tensor(part[:, 1, m % 2, :], swapped[b][:, 0:BW], tables[:, 1, blk(b)],
                                            ALU.mult).then_inc(sin_done, 1)
                    dve.wait_ge(cos_done, m + 1)
                    dve.wait_ge(sin_done, m + 1)
                    for out, lo, hi in parts:
                        x, y = (part[:, k, m % 2, lo:hi] for k in range(2))
                        if len(out.shape) == 3:
                            x, y = (z.rearrange("p (n t) -> p n t", n=out.shape[1]) for z in (x, y))
                        ins = nc.vector.tensor_tensor(out, x, y, ALU.add)
                    ins.then_inc(rope_done, 1)
                c.split_lo(dve, s + j + 2, 0, acc_ready, 3 * (j + 1))

        @block.gpsimd
        def _(pool):
            lead.gpsimd(pool)


def sequences(view, hist):
    def prompt(shift):
        return view[:, shift:shift + SEQ]

    def streams(shift, n=STEP):
        rest = view[:, SEQ + hist:SEQ + hist + STREAMS * (STEP + hist)]
        return rest.rearrange("p (s t) -> p s t", s=STREAMS)[:, :, shift:shift + n]

    return prompt, streams


def by_stream(view):
    return view[:, SEQ:T].rearrange("p (s t) -> p s t", s=STREAMS)


def stage_mixer(c, a, s):
    nc = c.nc
    scale = HD ** -0.5
    n, kinds = 4, 3
    products = [(j, kind, b) for j in range(n) for kind in range(kinds) for b in range(BLOCKS)]
    steps = [("prompt", n) for n in range(SEQ // CHUNK)] + [("stream", n) for n in range(STREAMS)]
    with ExitStack() as ctx:
        cache = c.sbuf("kv_cache", [P, 2, STREAMS, P], F32, ctx)
        sinks = c.sbuf("sinks", [P, 2, 8], F32, ctx)
        neg_sinks = c.sbuf("neg_sinks", [P, 2, 8], F32, ctx)
        prob = c.sbuf("prob", [P, 2, 4, 192], F32, ctx)
        prob_t = c.sbuf("prob_t", [P, 2, 2, 512], F32, ctx)
        vals = c.sbuf("vals", [P, 2, 2, P], F32, ctx)
        small = c.sbuf("softmax_small", [P, 2, 6, 4], F32, ctx)
        ps_s = [c.psum(f"scores{g}", [P, 512], ctx) for g in range(2)]
        ps_p = [c.psum(f"prob_t{n}", [P, 512], ctx) for n in range(2)]
        ps_v = c.psum("vals_t", [P, 512], ctx)
        ps_o = c.psum("attn_out", [P, 512], ctx)
        cache_loaded, sinks_loaded, neg_ready = c.sem("cache_loaded"), c.sem("sinks_loaded"), c.sem("neg_sinks_ready")
        s_ready, max_ready, cap_ready, negm_ready, sinkm_ready, exp_ready, sinke_ready = (
            c.sem("at_" + x) for x in ("scores", "max", "scaled", "negm", "sinkm", "exp", "sinke"))
        den_ready, inv_ready, prob_ready, pt_ready, pta_copied, ptb_copied = (
            c.sem("at_" + x) for x in ("den", "inv", "prob", "pt", "pta_copied", "ptb_copied"))
        v_ready, v_copied, o_ready, out_ready, hi_ready, lo_ready = (
            c.sem("at_" + x) for x in ("vt", "v_copied", "o", "out", "hi", "lo"))
        out = c.sbuf("attn_out_sb", [P, 2, 256], F32, ctx)

        conv = c.sbuf("conv", [P, 2, T], F32, ctx)
        gate = c.sbuf("gate_c", [P, T], F32, ctx)
        u = c.sbuf("conv_in", [P, n, XW], F32, ctx)
        taps = c.sbuf("sconv_taps", [P, 3, n], F32, ctx)
        gated = c.sbuf("gated", [P, 3, BW], F32, ctx)
        bank = [c.psum(f"cv{b}", [P, 512], ctx) for b in range(2)]
        hist_loaded, zeroed, taps_loaded = c.sem("shist_loaded"), c.sem("shist_zeroed"), c.sem("staps_loaded")
        acc_ready, gate_ready, u_ready, tap_done, gated_ready, gated_hi, gated_lo = (
            c.sem("cv_" + x) for x in ("acc", "gate", "u", "tap", "gated", "hi", "lo"))
        hist_stored = c.sem("shist_stored")
        block = ctx.enter_context(nc.Block())

        def now(i):
            ms = list(range(len(products) * i // (len(steps) + 1), len(products) * (i + 1) // (len(steps) + 1)))
            return ms[:1], ms[1:]

        def split_behind(eng, split, m):
            if m % BLOCKS == BLOCKS - 1:
                split(eng, s + m // BLOCKS + 2, 0, acc_ready, m + 1)

        def shape(step):
            kind, n = step
            if kind == "stream":
                return STEP, 1, GROUP * STEP, P, STEP
            keys = CHUNK * min(n + 1, 3)
            return CHUNK, 2, 2 * CHUNK, min(keys, P), keys - min(keys, P)

        def token(step):
            kind, n = step
            return SEQ + STEP * n if kind == "stream" else CHUNK * n

        def first_key(step):
            return max(0, token(step) - 2 * CHUNK)

        @block.sync
        def _(sp):
            sp.dma_start(cache[:, 0], a["cache_k"]).then_inc(cache_loaded, 16)
            sp.dma_start(cache[:, 1], a["cache_v"]).then_inc(cache_loaded, 16)
            sp.dma_start(sinks[:, :, :], a["sinks"]).then_inc(sinks_loaded, 16)
            sp.dma_start(taps[:, :, :], a["sconv_w"]).then_inc(taps_loaded, 16)
            for j in range(n):
                rest = u[:, j, SEQ + 2:XW].rearrange("p (s t) -> p s t", s=STREAMS)
                sp.dma_start(rest[:, :, 0:2], a["sconv_hist"][:, j, :, :]).then_inc(hist_loaded, 16)
            load_ring(c, sp, s, s + kinds * n)
            sp.wait_ge(u_ready, 4 * n)
            sp.dma_start(a["new_sconv"][:, :, 0, :], u[:, :, SEQ:SEQ + 2]).then_inc(hist_stored, 16)
            for j in range(n):
                rest = u[:, j, SEQ + 2:XW].rearrange("p (s t) -> p s t", s=STREAMS)
                sp.dma_start(a["new_sconv"][:, j, 1:1 + STREAMS, :], rest[:, :, STEP:STEP + 2]
                             ).then_inc(hist_stored, 16)
            sp.wait_ge(hist_stored, 16 * (n + 1))

        @block.tensor
        def _(pe):
            def front(i):
                step = steps[i]
                nq, units, rows, na, nb = shape(step)
                t0, k0 = token(step), first_key(step)
                if i >= 1:
                    pe.wait_ge(exp_ready, i)
                if step == ("stream", 0):
                    pe.wait_ge(cache_loaded, 32)
                for g in range(2):
                    half = slice(64 * g, 64 * g + 64)
                    for w in range(units):
                        q = c.q_stream if step[0] == "stream" else c.q_prompt
                        lhs = q[half, step[1], w * 4 // units:(w + 1) * 4 // units, :].rearrange("p t q -> p (t q)")
                        o = ps_s[g]
                        if step[0] == "stream":
                            pe.matmul(o[0:rows, 0:P], lhs, cache[half, 0, step[1], :], start=True, stop=True)
                            mm = pe.matmul(o[0:rows, P:P + nb], lhs, c.k[half, t0:t0 + nb], start=True, stop=True)
                        else:
                            mm = pe.matmul(o[0:rows, w * 192:w * 192 + na + nb], lhs, c.k[half, k0:k0 + na + nb],
                                           start=True, stop=True)
                mm.then_inc(s_ready, 1)
                if i >= 1:
                    pe.wait_ge(v_copied, i)
                if step[0] == "stream":
                    mm = pe.transpose(ps_v[0:nb, P:2 * P], c.v[:, t0:t0 + nb], c.ident)
                else:
                    mm = pe.transpose(ps_v[0:na, 0:P], c.v[:, k0:k0 + na], c.ident)
                    if nb:
                        mm = pe.transpose(ps_v[0:nb, P:2 * P], c.v[:, k0 + na:k0 + na + nb], c.ident)
                mm.then_inc(v_ready, 1)

            def transposes(i):
                step = steps[i]
                nq, units, rows, na, nb = shape(step)
                pe.wait_ge(prob_ready, i + 1)
                if i >= 1:
                    pe.wait_ge(pta_copied, i)
                    pe.wait_ge(ptb_copied, i)
                for n in range(2 * units):
                    mm = pe.transpose(ps_p[0][0:na, n * rows:(n + 1) * rows], prob[0:rows, i % 2, n, 0:na],
                                      c.ident[0:rows, 0:rows])
                    if nb:
                        mm = pe.transpose(ps_p[1][0:nb, n * rows:(n + 1) * rows], prob[0:rows, i % 2, n, na:na + nb],
                                          c.ident[0:rows, 0:rows])
                mm.then_inc(pt_ready, 1)

            def times_values(i):
                step = steps[i]
                nq, units, rows, na, nb = shape(step)
                pe.wait_ge(pta_copied, i + 1)
                pe.wait_ge(ptb_copied, i + 1)
                pe.wait_ge(v_copied, i + 1)
                if i >= 1:
                    pe.wait_ge(out_ready, i)
                for g in range(2):
                    half = slice(64 * g, 64 * g + 64)
                    for w in range(units):
                        n = g * units + w
                        o = ps_o[half, w * rows:(w + 1) * rows]
                        va = cache[:, 1, step[1], half] if step[0] == "stream" else vals[0:na, i % 2, 0, half]
                        mm = pe.matmul(o, va, prob_t[0:na, i % 2, 0, n * rows:(n + 1) * rows], start=True, stop=not nb)
                        if nb:
                            mm = pe.matmul(o, vals[0:nb, i % 2, 1, half],
                                           prob_t[0:nb, i % 2, 1, n * rows:(n + 1) * rows], start=False, stop=True)
                mm.then_inc(o_ready, 1)

            def project(ms):
                for m in ms:
                    c.weights_split(pe, s + m // BLOCKS)
                    if m >= 2:
                        j, kind, b = products[m - 2]
                        if kind == 1:
                            pe.wait_ge(u_ready, 4 * j + (b + 1 if b < BLOCKS - 1 else 4))
                        else:
                            pe.wait_ge((gate_ready, None, gated_ready)[kind], BLOCKS * j + b + 1)
                    c.multiply(bank[m % 2][:, 0:BW], s + m // BLOCKS, KD, c.x_hi, c.x_lo, 0, blk(m % BLOCKS),
                               True, True).then_inc(acc_ready, 1)

            for i in range(len(steps) + 1):
                if i < len(steps):
                    front(i)
                if i >= 1:
                    transposes(i - 1)
                project(now(i)[0])
                if i >= 1:
                    times_values(i - 1)
                project(now(i)[1])

        @block.vector
        def _(dve):
            dve.wait_ge(sinks_loaded, 16)
            nc.vector.tensor_scalar(neg_sinks[:, :, :], sinks[:, :, :], -1.0, None, ALU.mult).then_inc(neg_ready, 1)
            dve.wait_ge(neg_ready, 1)

            def front(i):
                step = steps[i]
                nq, units, rows, na, nb = shape(step)
                kind = 1 if step[0] == "stream" else 0
                nu, p = 2 * units, i % 2
                dve.wait_ge(s_ready, i + 1)
                for g in range(2):
                    src = ps_s[g][0:rows, 0:192 * units].rearrange("p (w k) -> p w k", w=units)[:, :, 0:na + nb]
                    ins = nc.vector.reduce_max(small[0:rows, p, 0, g * units:(g + 1) * units], src, AX_X)
                ins.then_inc(max_ready, 1)
                dve.wait_ge(max_ready, i + 1)
                nc.vector.tensor_scalar(small[0:rows, p, 1, 0:nu], small[0:rows, p, 0, 0:nu], -scale, None,
                                        ALU.mult).then_inc(cap_ready, 1)
                dve.wait_ge(cap_ready, i + 1)
                nc.vector.tensor_tensor(small[0:rows, p, 2, 0:nu], small[0:rows, p, 1, 0:nu],
                                        neg_sinks[0:rows, kind, 0:nu], ALU.min).then_inc(negm_ready, 1)
                dve.wait_ge(negm_ready, i + 1)
                nc.vector.tensor_tensor(small[0:rows, p, 3, 0:nu], small[0:rows, p, 2, 0:nu],
                                        sinks[0:rows, kind, 0:nu], ALU.add).then_inc(sinkm_ready, 1)
                dve.wait_ge(v_ready, i + 1)
                if i >= 2:
                    dve.wait_ge(o_ready, i - 1)
                if step[0] == "prompt":
                    ins = nc.vector.tensor_copy(vals[0:na, p, 0, :], ps_v[0:na, 0:P])
                if nb:
                    ins = nc.vector.tensor_copy(vals[0:nb, p, 1, :], ps_v[0:nb, P:2 * P])
                ins.then_inc(v_copied, 1)

            def probabilities(i):
                step = steps[i]
                nq, units, rows, na, nb = shape(step)
                nu, p = 2 * units, i % 2
                dve.wait_ge(sinke_ready, i + 1)
                nc.vector.tensor_tensor(small[0:rows, p, 5, 0:nu], small[0:rows, p, 4, 0:nu], small[0:rows, p, 3, 0:nu],
                                        ALU.add).then_inc(den_ready, 1)
                dve.wait_ge(den_ready, i + 1)
                nc.vector.reciprocal(small[0:rows, p, 5, 0:nu], small[0:rows, p, 5, 0:nu]).then_inc(inv_ready, 1)
                dve.wait_ge(inv_ready, i + 1)
                nc.vector.tensor_tensor(prob[0:rows, p, 0:nu, 0:na + nb], prob[0:rows, p, 0:nu, 0:na + nb],
                                        small[0:rows, p, 5, 0:nu].unsqueeze(2).to_broadcast([rows, nu, na + nb]),
                                        ALU.mult).then_inc(prob_ready, 1)

            def copy_transposed(i):
                step = steps[i]
                nq, units, rows, na, nb = shape(step)
                nu, p = 2 * units, i % 2
                dve.wait_ge(pt_ready, i + 1)
                if nb:
                    nc.vector.tensor_copy(prob_t[0:nb, p, 1, 0:nu * rows], ps_p[1][0:nb, 0:nu * rows]
                                          ).then_inc(ptb_copied, 1)
                else:
                    nc.vector.sem_inc(ptb_copied, 1)

            def copy_out(i):
                nq = shape(steps[i])[0]
                dve.wait_ge(o_ready, i + 1)
                if i >= 2:
                    dve.wait_ge(lo_ready, i - 1)
                nc.vector.tensor_copy(out[:, i % 2, 0:4 * nq], ps_o[:, 0:4 * nq]).then_inc(out_ready, 1)

            def convolve(j):
                prompt, streams = sequences(u[:, j, :], 2)
                dve.wait_ge(u_ready, 4 * (j + 1))
                if j >= 2:
                    dve.wait_ge(gated_ready, BLOCKS * (j - 1))
                outs = conv[:, j % 2, 0:SEQ], by_stream(conv[:, j % 2, :])
                for tap in range(3):
                    if tap:
                        dve.wait_ge(tap_done, 6 * j + 2 * tap)
                    for dst, seq in zip(outs, (prompt, streams)):
                        if tap == 0:
                            ins = nc.vector.tensor_scalar(dst, seq(0), taps[:, 0, j:j + 1], None, ALU.mult)
                        else:
                            ins = nc.vector.scalar_tensor_tensor(dst, seq(tap), taps[:, tap, j:j + 1], dst,
                                                                 ALU.mult, ALU.add)
                        ins.then_inc(tap_done, 1)

            def products_read(ms):
                for m in ms:
                    j, kind, b = products[m]
                    src = bank[m % 2]
                    lo, hi = b * BW, min((b + 1) * BW, SEQ)
                    if kind:
                        dve.wait_ge(acc_ready, m + 1)
                    if kind == 1:
                        dve.wait_ge(gate_ready, BLOCKS * j + b + 1)
                        nc.vector.scalar_tensor_tensor(u[:, j, 2 + lo:2 + hi], src[:, 0:hi - lo], 1 / WSCALE,
                                                       gate[:, lo:hi], ALU.mult, ALU.mult).then_inc(u_ready, 1)
                        if b == BLOCKS - 1:
                            nc.vector.scalar_tensor_tensor(
                                sequences(u[:, j, :], 2)[1](2),
                                src[:, SEQ - 2 * BW:BW].rearrange("p (s t) -> p s t", s=STREAMS), 1 / WSCALE,
                                by_stream(gate[:, :]), ALU.mult, ALU.mult).then_inc(u_ready, 1)
                            convolve(j)
                    if kind == 2:
                        dve.wait_ge(tap_done, 6 * (j + 1))
                        n_th = BLOCKS * j + b
                        if j:
                            dve.wait_ge(gated_lo, n_th - 2)
                        nc.vector.scalar_tensor_tensor(gated[:, b, :], src[:, 0:BW], 1 / WSCALE,
                                                       conv[:, j % 2, blk(b)], ALU.mult, ALU.mult
                                                       ).then_inc(gated_ready, 1)
                    split_behind(dve, c.split_lo, m)

            nc.vector.memset(u[:, :, 0:2], 0.0).then_inc(zeroed, 1)
            dve.wait_ge(taps_loaded, 16)
            dve.wait_ge(hist_loaded, 16 * n)
            dve.wait_ge(zeroed, 1)
            for i in range(len(steps) + 1):
                if i < len(steps):
                    front(i)
                if i >= 1:
                    copy_transposed(i - 1)
                if i < len(steps):
                    probabilities(i)
                products_read(now(i)[0])
                if i >= 1:
                    copy_out(i - 1)
                products_read(now(i)[1])

        @block.scalar
        def _(act):
            def front(i):
                step = steps[i]
                nq, units, rows, na, nb = shape(step)
                nu, p = 2 * units, i % 2
                act.wait_ge(negm_ready, i + 1)
                if i >= 2:
                    act.wait_ge(pt_ready, i - 1)
                for n in range(nu):
                    w = n % units
                    ins = nc.scalar.activation(prob[0:rows, p, n, 0:na + nb],
                                               ps_s[n // units][0:rows, w * 192:w * 192 + na + nb],
                                               AF.Exp, bias=small[0:rows, p, 2, n:n + 1], scale=scale,
                                               accum_out=small[0:rows, p, 4, n:n + 1])
                ins.then_inc(exp_ready, 1)
                act.wait_ge(sinkm_ready, i + 1)
                nc.scalar.activation(small[0:rows, p, 3, 0:nu], small[0:rows, p, 3, 0:nu], AF.Exp
                                     ).then_inc(sinke_ready, 1)

            def copy_transposed(i):
                step = steps[i]
                nq, units, rows, na, nb = shape(step)
                p, t0 = i % 2, token(step)
                act.wait_ge(pt_ready, i + 1)
                nc.scalar.copy(prob_t[0:na, p, 0, 0:2 * units * rows], ps_p[0][0:na, 0:2 * units * rows]
                               ).then_inc(pta_copied, 1)

            def split_out(i):
                nq, t0, p = shape(steps[i])[0], token(steps[i]), i % 2
                act.wait_ge(out_ready, i + 1)
                nc.scalar.copy(c.cat_hi[:, 0:4, t0:t0 + nq],
                               out[:, p, 0:4 * nq].rearrange("p (t q) -> p t q", t=4)).then_inc(hi_ready, 1)

            def products_read(ms):
                for m in ms:
                    j, kind, b = products[m]
                    if kind == 0:
                        act.wait_ge(acc_ready, m + 1)
                        if j >= 1:
                            act.wait_ge(u_ready, 4 * (j - 1) + (b + 1 if b < 2 else 4))
                        nc.scalar.mul(gate[:, blk(b)], bank[m % 2][:, 0:BW], 1 / WSCALE).then_inc(gate_ready, 1)
                    if kind == 2:
                        act.wait_ge(gated_ready, BLOCKS * j + b + 1)
                        nc.scalar.copy(c.cat_hi[:, 4 + j, blk(b)], gated[:, b, :]).then_inc(gated_hi, 1)
                    split_behind(act, c.split_hi, m)

            for i in range(len(steps) + 1):
                if i < len(steps):
                    front(i)
                if i >= 1:
                    copy_transposed(i - 1)
                products_read(now(i)[0])
                if i >= 1:
                    split_out(i - 1)
                products_read(now(i)[1])

        @block.gpsimd
        def _(pool):
            def attention(i):
                nq, t0 = shape(steps[i])[0], token(steps[i])
                pool.wait_ge(hi_ready, i + 1)
                nc.gpsimd.tensor_tensor(c.cat_lo[:, 0:4, t0:t0 + nq],
                                        out[:, i % 2, 0:4 * nq].rearrange("p (t q) -> p t q", t=4),
                                        c.cat_hi[:, 0:4, t0:t0 + nq], ALU.subtract).then_inc(lo_ready, 1)

            def convolution(ms):
                for j, kind, b in (products[m] for m in ms):
                    if kind == 2:
                        pool.wait_ge(gated_hi, BLOCKS * j + b + 1)
                        nc.gpsimd.tensor_tensor(c.cat_lo[:, 4 + j, blk(b)], gated[:, b, :],
                                                c.cat_hi[:, 4 + j, blk(b)], ALU.subtract).then_inc(gated_lo, 1)

            for i in range(len(steps) + 1):
                convolution(now(i)[0])
                if i >= 1:
                    attention(i - 1)
                convolution(now(i)[1])



def stage_project_y(c, tag, s, per, k_tiles, x_hi, x_lo, post, x_in, x_out):
    nc = c.nc
    steps = KD * per // 2
    tiles = 2 // per
    end = s + KD * per
    with ExitStack() as ctx:
        sq = c.sbuf(tag + "_sq", [P, 3, BW], F32, ctx)
        bank = [c.psum(f"{tag}{b}", [P, 512], ctx) for b in range(3)]
        last_bank = bank if per == 2 else [c.psum(f"{tag}_last{b}", [P, 512], ctx) for b in range(3)]
        early = Lead(c, ctx, tag + "_tail", post, None, x_in, x_out,
                     [c.psum(f"{tag}_tail{b}", [P, 512], ctx) for b in RES_EARLY],
                     lead_buffers(c, ctx, tag + "_tail", 1, 2, False), tail=True)
        acc_ready, y_ready, sq_ready, sum_done = (c.sem(f"{tag}_{x}") for x in ("acc", "y", "sq", "sum"))
        block = ctx.enter_context(nc.Block())

        @block.sync
        def _(sp):
            load_ring(c, sp, s, end - 2)
            early.load_x(sp, 0)
            early.load_x(sp, 1)
            early.store_x(sp, 0)
            early.store_x(sp, 1)
            c.load_weights(sp, end + 2)
            c.load_weights(sp, end + 3)

        @block.tensor
        def _(pe):
            def last_step(i):
                n = 3 * tiles * i
                for b in range(BLOCKS):
                    for j in range(2):
                        begins = per == 1 or j == 0

                        def midway(k):
                            if b and j == 0 and k == k_tiles // 2:
                                pe.wait_ge(sum_done, n + tiles * b)
                                early.rms_y.sums(pe, b - 1)

                        if b and j:
                            early.rms_y.spread(pe, b - 1)
                        c.weights_split(pe, s + j + 2 * i)
                        if j == 0:
                            pe.wait_ge(sq_ready, n - 2 + b)
                        c.multiply((last_bank if j else bank)[b][:, 0:BW], s + j + 2 * i, k_tiles, x_hi, x_lo,
                                   0 if per == 1 else j * k_tiles, blk(b), begins, per == 1 or j == 1, midway
                                   ).then_inc(acc_ready, 1)

            def body(i, first, last):
                if last:
                    last_step(i)
                    return
                for j in range(2):
                    begins = per == 1 or j == 0
                    c.weights_split(pe, s + j, i)
                    for b in range(BLOCKS):
                        m = (3 * (j if per == 1 else 0) + b) - 3
                        if begins and not (first and m < 0):
                            pe.wait_ge(sq_ready, m + 1 + 3 * tiles * i)
                        c.multiply(bank[b][:, 0:BW], s + j, k_tiles, x_hi, x_lo,
                                   0 if per == 1 else j * k_tiles, blk(b), begins, per == 1 or j == 1
                                   ).then_inc(acc_ready, 1)

            run(pe, steps, body)

        @block.scalar
        def _(act):
            def last_step(i):
                for b in range(BLOCKS):
                    for t in range(tiles):
                        n = 3 * tiles * i + tiles * b + t
                        src = last_bank[b] if t or per == 2 else bank[b]
                        act.wait_ge(acc_ready, 6 * i + 2 * b + (2 if per == 2 else t + 1))
                        nc.scalar.mul(c.y[:, tiles * i + t, blk(b)], src[:, 0:BW], 1 / WSCALE).then_inc(y_ready, 1)
                        act.wait_ge(sum_done, n - 2)
                        nc.scalar.activation(sq[:, n % 3, :], src[:, 0:BW], AF.Square, scale=1 / WSCALE
                                             ).then_inc(sq_ready, 1)
                    if b in early.res:
                        early.rms_y.roots(act, b)
                    if b == 1:
                        early.square(act, 0, range(KD))
                    if b == BLOCKS - 1:
                        c.split_hi(act, end, 0, acc_ready, 6 * i + 5)
                        c.split_hi(act, end + 1, 0, acc_ready, 6 * i + 6)

            def body(i, first, last):
                if last:
                    last_step(i)
                    return
                for j in range(2):
                    if per == 1 or j == 1:
                        t = j if per == 1 else 0
                        for b in range(BLOCKS):
                            m = 3 * t + b
                            act.wait_ge(acc_ready, 3 * j + b + 1 + 6 * i)
                            nc.scalar.mul(c.y[:, ds(tiles * i + t, 1), blk(b)], bank[b][:, 0:BW].unsqueeze(1),
                                          1 / WSCALE).then_inc(y_ready, 1)
                            if not (first and m < 3):
                                act.wait_ge(sum_done, m - 2 + 3 * tiles * i)
                            nc.scalar.activation(sq[:, b, :], bank[b][:, 0:BW], AF.Square, scale=1 / WSCALE
                                                 ).then_inc(sq_ready, 1)
                    split_u(c, act, c.split_hi, s, s + j, i, False, acc_ready)

            run(act, steps, body)

        @block.vector
        def _(dve):
            def last_step(i):
                def add(b):
                    for t in range(tiles):
                        n = 3 * tiles * i + tiles * b + t
                        dve.wait_ge(sq_ready, n + 1)
                        dve.wait_ge(sum_done, n)
                        nc.vector.tensor_tensor(c.acc[:, blk(b)], c.acc[:, blk(b)], sq[:, n % 3, :], ALU.add
                                                ).then_inc(sum_done, 1)

                add(0)
                early.rms_y.inverses(dve, 0)
                dve.wait_ge(y_ready, 3 * tiles * i + tiles)
                early.residual(dve, 0, range(0, 4))
                add(1)
                early.residual(dve, 0, range(4, KD))
                early.rms_y.inverses(dve, 1)
                early.residual(dve, 1, range(0, KD))
                c.split_lo(dve, end, 0, acc_ready, 6 * i + 5)
                add(2)
                c.split_lo(dve, end + 1, 0, acc_ready, 6 * i + 6)

            def body(i, first, last):
                if last:
                    last_step(i)
                    return
                for j in range(2):
                    if per == 1 or j == 1:
                        t = j if per == 1 else 0
                        for b in range(BLOCKS):
                            m = 3 * t + b
                            dve.wait_ge(sq_ready, m + 1 + 3 * tiles * i)
                            if first and t == 0:
                                nc.vector.tensor_copy(c.acc[:, blk(b)], sq[:, b, :]).then_inc(sum_done, 1)
                            else:
                                dve.wait_ge(sum_done, m - 2 + 3 * tiles * i)
                                nc.vector.tensor_tensor(c.acc[:, blk(b)], c.acc[:, blk(b)], sq[:, b, :], ALU.add
                                                        ).then_inc(sum_done, 1)
                    split_u(c, dve, c.split_lo, s, s + j, i, False, acc_ready)

            run(dve, steps, body)

        @block.gpsimd
        def _(pool):
            early.add_x_pool(pool, 0)
            early.add_squares(pool, 0, range(KD))
            early.add_x_pool(pool, 1)


def stage_final(c, a, x_in):
    with ExitStack() as ctx:
        banks = [c.psum(f"end_spread{b}", [P, 512], ctx) for b in range(BLOCKS)]
        lead = Lead(c, ctx, "end", (1, 3), None, x_in, a["y_out"], banks, lead_buffers(c, ctx, "end", 1), early=True)
        block = ctx.enter_context(c.nc.Block())

        @block.sync
        def _(sp):
            lead.sync(sp)
            lead.sync_end(sp)

        @block.tensor
        def _(pe):
            lead.tensor(pe)

        @block.scalar
        def _(act):
            lead.scalar(act)

        @block.vector
        def _(dve):
            lead.vector(dve)

        @block.gpsimd
        def _(pool):
            lead.gpsimd(pool)



def stage_gate_up(c, tag, s, mid_hi, mid_lo, post, pre, x_in, x_out, early):
    nc = c.nc
    with ExitStack() as ctx:
        sil = c.sbuf(tag + "_silu", [P, 3, BW], F32, ctx)
        mid = c.sbuf(tag + "_mid", [P, 3, BW], F32, ctx)
        bank = [c.psum(f"{tag}{b}", [P, 512], ctx) for b in range(6)]
        late_hi, late_lo = (x[:, FT - 18:FT, :].rearrange("p j t -> p (j t)").bitcast(F32) for x in (mid_hi, mid_lo))
        xr = late_hi[:, 0:2 * KD * BW].rearrange("p (a j t) -> p a j t", a=2, j=KD)
        sq = late_lo[:, 0:4 * BW].rearrange("p (k t) -> p k t", k=4)
        h = late_lo[:, 4 * BW:(4 + KD) * BW].rearrange("p (j t) -> p j t", j=KD)
        lead = Lead(c, ctx, tag + "_lead", post, pre, x_in, x_out, bank[3:6], (xr, sq, h), 4 if early else 5,
                    early)
        acc_ready, sil_ready, mid_ready, hi_ready, lo_ready = (
            c.sem(f"{tag}_{x}") for x in ("acc", "sil", "mid", "hi", "lo"))
        block = ctx.enter_context(nc.Block())

        def acc_at(first, j, b):
            return 2 * b + j + 1 if first else 3 * j + b + 1

        def split_next(eng, split, j, i, first, last):
            if first:
                split(eng, s + j + 2, 0, acc_ready, 5 + j)
            else:
                split_u(c, eng, split, s, s + j, i, last, acc_ready)

        @block.sync
        def _(sp):
            lead.sync(sp)
            load_ring(c, sp, s, s + 2 * FT)
            lead.sync_end(sp)

        @block.tensor
        def _(pe):
            def first_step(b, j, hook):
                c.weights_split(pe, s + j)
                c.multiply(bank[3 * j + b][:, 0:BW], s + j, KD, c.x_hi, c.x_lo, 0, blk(b), True, True, hook
                           ).then_inc(acc_ready, 1)

            def body(i, first, last):
                if first:
                    lead.tensor(pe, first_step)
                    return
                for j, used in enumerate((sil_ready, mid_ready)):
                    c.weights_split(pe, s + j, i)
                    for b in range(BLOCKS):
                        pe.wait_ge(used, b - 2 + 3 * i)
                        c.multiply(bank[3 * j + b][:, 0:BW], s + j, KD, c.x_hi, c.x_lo, 0, blk(b), True, True
                                   ).then_inc(acc_ready, 1)

            run(pe, FT, body)

        @block.scalar
        def _(act):
            lead.scalar(act)

            def body(i, first, last):
                for b in range(BLOCKS):
                    act.wait_ge(acc_ready, acc_at(first, 0, b) + 6 * i)
                    if not first:
                        act.wait_ge(mid_ready, b - 2 + 3 * i)
                    nc.scalar.activation(sil[:, b, :], bank[b][:, 0:BW], AF.Silu, scale=1 / WSCALE
                                         ).then_inc(sil_ready, 1)
                split_next(act, c.split_hi, 0, i, first, last)
                for b in range(BLOCKS):
                    act.wait_ge(mid_ready, b + 1 + 3 * i)
                    nc.scalar.copy(mid_hi[:, ds(i, 1), blk(b)], mid[:, b, :].unsqueeze(1)).then_inc(hi_ready, 1)
                split_next(act, c.split_hi, 1, i, first, last)

            run(act, FT, body)

        @block.vector
        def _(dve):
            lead.vector(dve)

            def body(i, first, last):
                split_next(dve, c.split_lo, 0, i, first, last)
                for b in range(BLOCKS):
                    dve.wait_ge(acc_ready, acc_at(first, 1, b) + 6 * i)
                    dve.wait_ge(sil_ready, b + 1 + 3 * i)
                    if not first:
                        dve.wait_ge(lo_ready, b - 2 + 3 * i)
                    nc.vector.scalar_tensor_tensor(mid[:, b, :], bank[3 + b][:, 0:BW], 1 / WSCALE, sil[:, b, :],
                                                   ALU.mult, ALU.mult).then_inc(mid_ready, 1)
                split_next(dve, c.split_lo, 1, i, first, last)

            run(dve, FT, body)

        @block.gpsimd
        def _(pool):
            lead.gpsimd(pool)
            with pool.Fori(0, FT) as i:
                for b in range(BLOCKS):
                    pool.wait_ge(hi_ready, b + 1 + 3 * i)
                    nc.gpsimd.tensor_tensor(mid_lo[:, ds(i, 1), blk(b)], mid[:, b, :].unsqueeze(1),
                                            mid_hi[:, ds(i, 1), blk(b)], ALU.subtract).then_inc(lo_ready, 1)


def feed_forward(c, tag, s, layer, x_in, x_mid, x_out, early):
    with ExitStack() as ctx:
        mid_hi = c.sbuf(tag + "_mid_hi", [P, FT, T], F16, ctx)
        mid_lo = c.sbuf(tag + "_mid_lo", [P, FT, T], F16, ctx)
        stage_gate_up(c, tag + "_gu", s, mid_hi, mid_lo, (layer, 1), (layer, 2), x_in, x_mid, early)
        c.end_stage()
        stage_project_y(c, tag + "_dn", s + 2 * FT, 2, DOWN_K, mid_hi, mid_lo, (layer, 3), x_mid, x_out)
        c.end_stage()



class SSM:

    def __init__(self, c, ctx):
        shape = [P, TT, SHEADS]
        self.dt, self.ea, self.dend = (c.sbuf("ssm_" + n, shape, F32, ctx) for n in ("dt", "ea", "dend"))
        self.chunk_decay = c.sbuf("ssm_chunk_decay", [P, SEQ // P, SHEADS], F32, ctx)
        self.stream_decay = c.sbuf("ssm_stream_decay", [P, STREAMS, SHEADS], F32, ctx)
        self.d = c.sbuf("ssm_d", [P, SHEADS], F32, ctx)
        self.da_hi, self.da_lo = (c.sbuf("ssm_" + n, shape, F16, ctx) for n in ("da_hi", "da_lo"))
        self.tri_strict = c.sbuf("ssm_tri_strict", [P, P], F16, ctx)


def stage_dt(c, a, s, m, x_in, x_out):
    nc, n = c.nc, TT * SHEADS
    np_ = SEQ // P * SHEADS
    with ExitStack() as ctx:
        rows = c.sbuf("ssm_rows", [P, 3, SHEADS], F32, ctx)
        neg_a = c.sbuf("ssm_neg_a", [P, SHEADS], F32, ctx)
        work = c.sbuf("ssm_work", [P, 6, n], F32, ctx)
        dta = c.sbuf("ssm_dta", [P, TT, SHEADS], F32, ctx)
        by_s = c.sbuf("ssm_by_stream", [P, STREAMS, SHEADS], F32, ctx)
        ps_dt, ps_cum, ps_tot, ps_str = (c.psum("dt_" + x, [P, 512], ctx) for x in ("raw", "cum", "tot", "str"))
        rows_loaded, acc_ready, sums_ready = c.sem("ssm_rows_loaded"), c.sem("dt_acc"), c.sem("dt_sums")
        neg_abs, exp_done, u_ready, ln_done, da_ready, a_ready = (
            c.sem("dt_" + x) for x in ("neg_abs", "exp", "u", "ln", "da", "a"))
        da_split = c.sem("dt_da_split")
        step, diff_ready, decays = c.sem("dt_step"), c.sem("dt_diff"), c.sem("dt_decays")
        lead = Lead(c, ctx, "dt_lead", (0, 3), (1, 0), x_in, x_out,
                    [ps_cum, ps_tot, ps_str], lead_buffers(c, ctx, "dt"), 4, True)
        block = ctx.enter_context(nc.Block())

        def flat(t):
            return t[:, :, :].rearrange("p a b -> p (a b)")

        def w(k):
            return work[:, k, :]

        @block.sync
        def _(sp):
            sp.dma_start(rows[:, :, :], a["ssm_rows"]).then_inc(rows_loaded, 16)
            lead.sync(sp)
            load_ring(c, sp, s, s + 1)
            lead.sync_end(sp)

        @block.tensor
        def _(pe):
            c.weights_split(pe, s)
            wh = c.w_hi[:, s % 2, 0:KD * SHEADS].rearrange("p (k h) -> p k h", k=KD)
            wl = c.w_lo[:, s % 2, 0:KD * SHEADS].rearrange("p (k h) -> p k h", k=KD)

            def project(b, part, ready):
                for t in tiles_of(b) if part == 0 else ():
                    out = ps_dt[:, t * SHEADS:(t + 1) * SHEADS]
                    for k in range(KD):
                        ready(k)
                        xh, xl = (x[:, k, t * P:(t + 1) * P] for x in (c.x_hi, c.x_lo))
                        pe.matmul(out, xh, wh[:, k, :], start=(k == 0), stop=False)
                        pe.matmul(out, xl, wh[:, k, :], start=False, stop=False)
                        mm = pe.matmul(out, xh, wl[:, k, :], start=False, stop=(k == KD - 1))
                    if t == TT - 1:
                        mm.then_inc(acc_ready, 1)

            lead.tensor(pe, project)
            pe.wait_ge(da_ready, 2)
            da = flat(dta)
            pe.matmul(ps_cum[:, 0:np_], c.tri_incl, da[:, 0:np_], start=True, stop=True)
            pe.matmul(ps_cum[:, np_:n], c.tri_block, da[:, np_:n], start=True, stop=True)
            pe.matmul(ps_tot[:, 0:np_], c.ones, da[:, 0:np_], start=True, stop=True)
            pe.matmul(ps_tot[:, np_:n], c.block_ones, da[:, np_:n], start=True, stop=True)
            pe.matmul(ps_str[:, 0:STREAMS * SHEADS], c.ones, flat(by_s), start=True, stop=True
                      ).then_inc(sums_ready, 1)

        @block.vector
        def _(dve):
            v = nc.vector
            lead.vector(dve)
            dve.wait_ge(rows_loaded, 16)
            dve.wait_ge(acc_ready, 1)
            bias = rows[:, 0, :].unsqueeze(1).to_broadcast([P, TT, SHEADS])
            v.scalar_tensor_tensor(w(0).rearrange("p (a b) -> p a b", a=TT),
                                   ps_dt[:, 0:n].rearrange("p (a b) -> p a b", a=TT), 1 / WSCALE, bias,
                                   ALU.mult, ALU.add).then_inc(step, 1)
            dve.wait_ge(step, 1)
            v.tensor_scalar(w(1), w(0), -1.0, None, ALU.mult).then_inc(step, 1)
            dve.wait_ge(step, 2)
            v.tensor_tensor(w(1), w(0), w(1), ALU.min).then_inc(neg_abs, 1)
            v.tensor_scalar(w(0), w(0), 0.0, None, ALU.max).then_inc(step, 1)
            dve.wait_ge(exp_done, 2)
            v.tensor_scalar(w(3), w(2), 1.0, None, ALU.add).then_inc(u_ready, 1)
            dve.wait_ge(u_ready, 1)
            v.tensor_scalar(w(4), w(3), -1.0, None, ALU.add).then_inc(step, 1)
            v.reciprocal(w(5), w(3)).then_inc(step, 1)
            dve.wait_ge(step, 5)
            v.tensor_tensor(w(4), w(2), w(4), ALU.subtract).then_inc(step, 1)
            dve.wait_ge(step, 6)
            v.tensor_tensor(w(4), w(4), w(5), ALU.mult).then_inc(step, 1)
            dve.wait_ge(step, 7)
            v.tensor_tensor(w(0), w(0), w(4), ALU.add).then_inc(step, 1)
            dve.wait_ge(step, 8)
            dve.wait_ge(ln_done, 1)
            v.tensor_tensor(flat(m.dt), w(0), w(1), ALU.add).then_inc(step, 1)
            v.tensor_scalar(neg_a[:, :], neg_a[:, :], -1.0, None, ALU.mult).then_inc(a_ready, 1)
            v.tensor_copy(m.d[:, :], rows[:, 2, :]).then_inc(step, 1)
            dve.wait_ge(step, 9)
            dve.wait_ge(a_ready, 1)
            v.tensor_tensor(dta[:, :, :], m.dt[:, :, :], neg_a[:, :].unsqueeze(1).to_broadcast([P, TT, SHEADS]),
                            ALU.mult).then_inc(da_ready, 1)
            dve.wait_ge(da_ready, 1)
            v.tensor_tensor(by_s[:, :, :], dta[:, TT - 1, :].unsqueeze(1).to_broadcast([P, STREAMS, SHEADS]),
                            c.stream_mask.unsqueeze(2).to_broadcast([P, STREAMS, SHEADS]), ALU.mult
                            ).then_inc(da_ready, 1)
            v.tensor_copy(m.tri_strict[:, :], c.tri_strict).then_inc(da_split, 1)
            v.tensor_copy(flat(m.da_hi), flat(dta)).then_inc(da_split, 1)
            dve.wait_ge(da_split, 2)
            v.tensor_tensor(flat(m.da_lo), flat(dta), flat(m.da_hi), ALU.subtract).then_inc(da_split, 1)
            c.split_lo(dve, s + 2, 0, acc_ready, 1)
            dve.wait_ge(da_split, 3)
            dve.wait_ge(sums_ready, 1)
            v.tensor_copy(w(2), ps_cum[:, 0:n]).then_inc(step, 1)
            dve.wait_ge(step, 11)
            v.tensor_tensor(w(3), ps_tot[:, 0:n], w(2), ALU.subtract).then_inc(diff_ready, 1)

        @block.scalar
        def _(act):
            lead.scalar(act)
            act.wait_ge(neg_abs, 1)
            nc.scalar.activation(w(2), w(1), AF.Exp).then_inc(exp_done, 1)
            nc.scalar.activation(neg_a[:, :], rows[:, 1, :], AF.Exp).then_inc(exp_done, 1)
            act.wait_ge(u_ready, 1)
            nc.scalar.activation(w(1), w(3), AF.Ln).then_inc(ln_done, 1)
            c.split_hi(act, s + 2, 0, acc_ready, 1)
            act.wait_ge(sums_ready, 1)
            nc.scalar.activation(flat(m.stream_decay), ps_str[:, 0:STREAMS * SHEADS], AF.Exp).then_inc(decays, 1)
            act.wait_ge(diff_ready, 1)
            nc.scalar.activation(flat(m.ea), ps_cum[:, 0:n], AF.Exp).then_inc(decays, 1)
            nc.scalar.activation(flat(m.chunk_decay), ps_tot[:, 0:np_], AF.Exp).then_inc(decays, 1)
            nc.scalar.activation(flat(m.dend), w(3), AF.Exp).then_inc(decays, 1)
            act.wait_ge(decays, 4)

        @block.gpsimd
        def _(pool):
            lead.gpsimd(pool)


def stage_ssm(c, a, s, m):
    nc = c.nc
    n_units, n_conv, n_z, n_out = 14, 6, 4, 4
    per_conv, per_out = BLOCKS * n_conv, 2 * BLOCKS * n_out
    with ExitStack() as ctx:
        sb = lambda name, shape, dt=F32: c.sbuf("ss_" + name, shape, dt, ctx)
        xbc = sb("xbc", [P, n_conv, T])
        pad = sb("pad", [P, 2, XW3])
        hist = sb("hist", [P, SG * n_conv, 1 + STREAMS, 3])
        taps = sb("taps", [P, 4, SG * n_conv])
        bias = sb("bias", [P, SG * n_conv])
        gains = sb("gains", [P, SG * 4])
        wz_hi, wz_lo = sb("wz_hi", [P, KD, GW], F16), sb("wz_lo", [P, KD, GW], F16)
        g_hi, g_lo = sb("g_hi", [P, 4, T], F16), sb("g_lo", [P, 4, T], F16)
        x_tok, xdt, xdec = (sb(x, [P, 2, GW]) for x in ("x_tok", "xdt", "xdec"))
        seg_in, e = sb("seg_in", [P, 2, SHPG, P]), sb("e", [P, 2, SHPG, P])
        b_tok = sb("b_tok", [P, 2, P])
        decayed, junk = sb("decayed", [P, GW])[:, :], sb("junk", [P, GW], F16)[:, :]
        flat = pad[:, :, :].rearrange("p a b -> p (a b)")
        yt, zt, cbm = c.acc[:, 0:GW], c.acc[:, GW:2 * GW], c.acc[:, 2 * GW:2 * GW + P]
        sq = flat[:, 0:3 * BW].rearrange("p (b n) -> p b n", b=3)
        SLOTS = 4
        state = sb("state", [P, SLOTS, GW])
        ssq, root, inv = sb("ssq", [P, TT]), sb("root", [P, TT]), sb("inv", [P, TT])
        ps_yo, ps_yd, ps_st = (c.psum("ss_" + x, [P, 512], ctx) for x in ("yo", "yd", "st"))
        ps_x, ps_z, ps_bc = (c.psum("ss_" + x, [P, 512], ctx) for x in ("x", "zt", "bc"))
        ps_seg = [c.psum(f"ss_seg{k}", [P, 512], ctx) for k in range(2)]
        conv_bank = [ps_z, *ps_seg]
        out_bank = [ps_yo, ps_yd, ps_st]

        sem = lambda name: c.sem("ss_" + name)
        small_loaded, conv_acc, out_acc, y_zeroed = (sem(x) for x in ("small_loaded", "conv_acc", "out_acc", "y_zeroed"))
        pad_ready, hist_put, hist_kept, tap_done, xbc_ready = (
            sem(x) for x in ("pad", "hist_put", "hist_kept", "tap", "xbc"))
        xt_ready, x_copied, bc_ready, b_ready, cb_ready = (sem(x) for x in ("xt", "x_copied", "bcr", "b", "cb"))
        segin_ready, seg_ready, exp_ready, w_ready = (sem(x) for x in ("segin", "seg", "exp", "w"))
        xdt_ready, xd_ready, xdec_ready = (sem(x) for x in ("xdt_ready", "xd", "xdec"))
        z_ready, tanh_ready, zt_ready = (sem(x) for x in ("z_ready", "tanh", "zt_ready"))
        yo_ready, yo_used, yd_ready, yd_used, y_done, gated, sq_done = (
            sem(x) for x in ("yo_ready", "yo_used", "yd_ready", "yd_used", "y_done", "gated", "sq_done"))
        st_ready, dec_ready, h_ready = (sem(x) for x in ("st_ready", "dec", "h"))
        cm_zero, cm_ready, bm_ready = (sem(x) for x in ("cm_zero", "cm", "bm"))
        root_ready, inv_ready, yn_ready, t_ready, ghi_ready, glo_ready = (
            sem(x) for x in ("root_ready", "inv_ready", "yn", "t", "ghi", "glo"))
        y_ready, ysq_ready, ysum_done = (sem(x) for x in ("y", "ysq", "ysum"))
        state_loaded = [sem(f"state_loaded{r}") for r in range(SLOTS)]
        state_stored = [sem(f"state_stored{r}") for r in range(SLOTS)]
        hist_stored, waits_alone = sem("hist_stored"), sem("waits_alone")
        block = ctx.enter_context(nc.Block())

        def chunk(t):
            return slice(t * P, (t + 1) * P)

        def wait_ge(engine, semaphore, value):
            if not isinstance(value, int) or value > 0:
                engine.wait_ge(semaphore, value)

        def each_group(engine, body, end=None):
            body(0, True, False)
            with engine.Fori(1, SG - 1) as g:
                body(g, False, False)
            body(SG - 1, False, True)
            if end is not None:
                end()

        def z_unit(first, q):
            return n_conv + (0 if first else n_out) + q

        def turn_base(g):
            return s if isinstance(g, int) and g == 0 else s - n_out

        END = n_units

        def alone(engine):
            engine.sem_inc(waits_alone, 1)

        LAST = TT - 1
        PER_H = LAST + 1 + STREAMS
        PER_ST = LAST + STREAMS
        ring = [(k + 1) % SLOTS for k in range(STREAMS)]
        uses = [ring.count(r) for r in range(SLOTS)]
        turn = [ring[:k].count(ring[k]) for k in range(STREAMS)]

        def of_heads(v):
            return v.unsqueeze(2).to_broadcast([P, SHPG, SHD])

        def heads(t):
            return t.rearrange("p (h d) -> p h d", h=SHPG)

        def seg_part(t, part):
            both = seg_in[:, t % 2].rearrange("p h t -> p (h t)").bitcast(F16)
            return both[:, part * SHPG * P:(part + 1) * SHPG * P].rearrange("p (h t) -> p h t", h=SHPG)

        def head_cols(t, g):
            return t[:, ds(SHPG * g, SHPG)]

        @block.sync
        def _(sp):
            sp.dma_start(hist[:, :, :, :], a["ssm_hist"]).then_inc(small_loaded, 16)
            sp.dma_start(taps[:, :, :], a["ssm_taps"]).then_inc(small_loaded, 16)
            sp.dma_start(bias[:, :], a["ssm_bias"]).then_inc(small_loaded, 16)
            sp.dma_start(gains[:, :], a["ssm_gains"]).then_inc(small_loaded, 16)

            def load_state(g, k):
                sp.dma_start(state[:, ring[k], :], a["state"][k, :, ds(g * GW, GW)]
                             ).then_inc(state_loaded[ring[k]], 16)

            def load_unit(g, j):
                u = turn_base(g) + 4 + j
                wait_ge(sp, c.w_hi_ready, u - 1 + n_units * g)
                wait_ge(sp, c.w_lo_ready, u - 1 + n_units * g)
                src = a["ssm_w"][ds(u - s + n_units * g, 1), :, :].rearrange("a p c -> (a p) c")
                sp.dma_start(c.w_raw[:, u % 2, 0:UNIT], src).then_inc(c.w_loaded[u % 2], 16)

            def group(g, first, last):
                for j in range(n_units - (n_out if first else 0)):
                    load_unit(g, j)
                for k in range(SLOTS - 1):
                    load_state(g, k)
                wait_ge(sp, h_ready, (LAST + 1) + PER_H * g)
                sp.dma_start(a["new_state_prompt"][:, ds(g * GW, GW)], state[:, 0, :]
                             ).then_inc(state_stored[0], 16)
                wait_ge(sp, state_stored[0], 16 + 16 * (uses[0] + 1) * g)
                alone(sp)
                load_state(g, SLOTS - 1)
                for k in range(STREAMS):
                    wait_ge(sp, h_ready, (LAST + 2 + k) + PER_H * g)
                    sp.dma_start(a["new_state"][k, :, ds(g * GW, GW)], state[:, ring[k], :]
                                 ).then_inc(state_stored[ring[k]], 16)
                    if k:
                        r, extra = ring[k - 1], 1 if ring[k - 1] == 0 else 0
                        wait_ge(sp, state_stored[r], 16 * (turn[k - 1] + 1 + extra) + 16 * (uses[r] + extra) * g)
                        alone(sp)
                        if k - 1 + SLOTS < STREAMS:
                            load_state(g, k - 1 + SLOTS)
                for r in range(SLOTS):
                    wait_ge(sp, state_stored[r], 16 * (uses[r] + (r == 0)) * (g + 1))
                    alone(sp)

            def end():
                for j in range(4):
                    c.load_weights(sp, turn_base(SG - 1) + n_units * (SG - 1) + END + n_out + j)

            each_group(sp, group, end)
            wait_ge(sp, hist_kept, SG * n_conv)
            sp.dma_start(a["new_ssm_hist"], hist[:, :, :, :]).then_inc(hist_stored, 16)
            sp.wait_ge(hist_stored, 16)

        @block.tensor
        def _(pe):
            def weights(u, g):
                wait_ge(pe, c.w_hi_ready, turn_base(g) + u + 1 + n_units * g)
                wait_ge(pe, c.w_lo_ready, turn_base(g) + u + 1 + n_units * g)

            def project(g, j, blocks=range(BLOCKS)):
                for b in blocks:
                    wait_ge(pe, pad_ready, 4 * (j - 1) + (b + 1 if b < 2 else 4) + 4 * n_conv * g)
                    c.multiply(conv_bank[b][:, 0:BW], s + j, KD, c.x_hi, c.x_lo, 0, blk(b), True, True
                               ).then_inc(conv_acc, 1)

            def project_first(b):
                c.multiply(conv_bank[b][:, 0:BW], s, KD, c.x_hi, c.x_lo, 0, blk(b), True, True
                           ).then_inc(conv_acc, 1)

            def inputs(g, t):
                v = TT * g + t
                cols = chunk(t)
                wait_ge(pe, x_copied, v)
                wait_ge(pe, glo_ready, max(0, t - 2) + TT * g)
                for j in range(4):
                    mm = pe.transpose(ps_x[:, j * P:(j + 1) * P], xbc[:, j, cols], c.ident)
                mm.then_inc(xt_ready, 1)
                wait_ge(pe, b_ready, v)
                wait_ge(pe, cb_ready, v)
                pe.transpose(ps_bc[:, 0:P], xbc[:, 4, cols], c.ident)
                pe.matmul(ps_bc[:, P:2 * P], xbc[:, 4, cols], xbc[:, 5, cols], start=True, stop=True
                          ).then_inc(bc_ready, 1)
                wait_ge(pe, segin_ready, v + 1)
                wait_ge(pe, exp_ready, v)
                if t == 0:
                    wait_ge(pe, pad_ready, 4 * n_conv * (g + 1))
                for q in range(2):
                    pe.matmul(ps_seg[q][:, :], m.tri_strict[:, :], seg_part(t, 0)[:, 4 * q:4 * q + 4, :],
                              start=True, stop=False)
                    mm = pe.matmul(ps_seg[q][:, :], m.tri_strict[:, :], seg_part(t, 1)[:, 4 * q:4 * q + 4, :],
                                   start=False, stop=True)
                mm.then_inc(seg_ready, 1)

            def project_z(g, t):
                if t == 0:
                    weights(z_unit(isinstance(g, int) and g == 0, n_z - 1), g)
                wait_ge(pe, zt_ready, TT * g + t)
                for k in range(KD):
                    xh, xl = c.x_hi[:, k, chunk(t)], c.x_lo[:, k, chunk(t)]
                    pe.matmul(ps_z[:, :], xh, wz_hi[:, k, :], start=(k == 0), stop=False)
                    pe.matmul(ps_z[:, :], xl, wz_hi[:, k, :], start=False, stop=False)
                    mm = pe.matmul(ps_z[:, :], xh, wz_lo[:, k, :], start=False, stop=(k == KD - 1))
                mm.then_inc(z_ready, 1)

            def own_part(g, t):
                v, p = TT * g + t, t % 2
                wait_ge(pe, w_ready, v + 1)
                wait_ge(pe, xdt_ready, v + 1)
                wait_ge(pe, yd_used, v)
                if t == 0:
                    wait_ge(pe, y_ready, per_out * g)
                for h in range(SHPG):
                    mm = pe.matmul(ps_yd[:, h * SHD:(h + 1) * SHD], e[:, p, h, :], xdt[:, p, h * SHD:(h + 1) * SHD],
                                   start=True, stop=True)
                mm.then_inc(yd_ready, 1)

            def from_state(g, t):
                v, p = TT * g + t, t % 2
                wait_ge(pe, yo_used, v)
                wait_ge(pe, xdec_ready, v + 1)
                wait_ge(pe, h_ready, t + 1 + PER_H * g)
                pe.matmul(ps_yo[:, :], xbc[:, 5, chunk(t)], state[:, 0, :], start=True, stop=True
                          ).then_inc(yo_ready, 1)
                wait_ge(pe, b_ready, v + 1)
                pe.matmul(ps_st[:, :], b_tok[:, p, :], xdec[:, p, :], start=True, stop=True
                          ).then_inc(st_ready, 1)

            def from_stream_states(g, streams):
                v, p = TT * g + LAST, LAST % 2
                if streams[0] == 0:
                    wait_ge(pe, yo_used, v)
                    wait_ge(pe, xdec_ready, v + 1)
                    wait_ge(pe, cm_ready, STREAMS + STREAMS * g)
                    wait_ge(pe, bm_ready, 1 + g)
                for k in streams:
                    r = ring[k]
                    wait_ge(pe, state_loaded[r], 16 * (turn[k] + 1) + 16 * uses[r] * g)
                    mm = pe.matmul(ps_yo[:, :], seg_in[:, 1 - p, k, :], state[:, r, :], start=(k == 0),
                                   stop=(k == STREAMS - 1))
                    if k == STREAMS - 1:
                        mm.then_inc(yo_ready, 1)
                    wait_ge(pe, h_ready, LAST + 1 + k + PER_H * g)
                    pe.matmul(ps_st[:, :], e[:, 1 - p, k, :], xdec[:, p, :], start=True, stop=True
                              ).then_inc(st_ready, 1)

            def turn_back(g, t):
                wait_ge(pe, yn_ready, t + 1 + TT * g)
                wait_ge(pe, x_copied, min(t + 3, TT) + TT * g)
                wait_ge(pe, glo_ready, t + TT * g)
                for j in range(4):
                    mm = pe.transpose(ps_x[:, j * P:(j + 1) * P], xbc[:, j, chunk(t)], c.ident)
                mm.then_inc(t_ready, 1)

            def project_out(g, turn, unit0, parts):
                banks = conv_bank if unit0 == END else out_bank
                for q, n, b in parts:
                    weights(unit0 + q, turn)
                    par = (s + unit0 + q) % 2
                    if q == 0 and n == 0:
                        if unit0 == END:
                            wait_ge(pe, exp_ready if b else zt_ready, TT * (g + 1))
                        else:
                            wait_ge(pe, (yo_used, yd_used, h_ready)[b], (TT, TT, PER_H)[b] * (g + 1))
                        wait_ge(pe, glo_ready, 3 * (b + 1) + TT * g)
                    else:
                        wait_ge(pe, y_ready, 3 * (2 * q + n - 1) + b + 1 + per_out * g)
                    for k in range(4):
                        lo = (2 * k + n) * P
                        wh, wl = (w[:, par, lo:lo + P] for w in (c.w_hi, c.w_lo))
                        pe.matmul(banks[b][:, 0:BW], wh, g_hi[:, k, blk(b)], start=(k == 0), stop=False)
                        pe.matmul(banks[b][:, 0:BW], wh, g_lo[:, k, blk(b)], start=False, stop=False)
                        mm = pe.matmul(banks[b][:, 0:BW], wl, g_hi[:, k, blk(b)], start=False, stop=(k == 3))
                    mm.then_inc(out_acc, 1)

            OUT_PARTS = [(q, n, b) for q in range(n_out) for n in range(2) for b in range(BLOCKS)]

            def group(g, first, last):
                if first:
                    weights(0, g)
                    for b in range(BLOCKS):
                        project_first(b)
                for j in range(1, n_conv):
                    weights(j, g)
                    project(g, j, range(0, 2))
                    if j == 1 and not first:
                        turn_back(g - 1, LAST)
                    project(g, j, range(2, BLOCKS))
                if not first:
                    project_out(g - 1, g, n_conv, OUT_PARTS)
                wait_ge(pe, xbc_ready, n_conv + n_conv * g)
                for i in range(TT):
                    inputs(g, i)
                    if i:
                        own_part(g, i - 1)
                        from_state(g, i - 1)
                    if i >= 2:
                        turn_back(g, i - 2)
                    project_z(g, i)
                own_part(g, LAST)
                if last:
                    turn_back(g, LAST - 1)
                    project_out(g, g, END, OUT_PARTS[:2])
                    from_stream_states(g, range(STREAMS))
                    return
                weights(n_units - (n_out if first else 0), g)
                wait_ge(pe, zt_ready, TT * (g + 1))
                wait_ge(pe, exp_ready, TT * (g + 1))
                project_first(0)
                turn_back(g, LAST - 1)
                from_stream_states(g, range(0, 3))
                project_first(1)
                from_stream_states(g, range(3, 6))
                project_first(2)
                from_stream_states(g, range(6, STREAMS))

            def end():
                turn_back(SG - 1, LAST)
                project_out(SG - 1, SG - 1, END, OUT_PARTS[2:])

            each_group(pe, group, end)

        @block.scalar
        def _(act):
            act.wait_ge(small_loaded, 64)

            def split(g, j, z=None):
                u = turn_base(g) + j
                wait_ge(act, c.w_loaded[u % 2], 16 * (u // 2 + 1) + 16 * (n_units // 2) * g)
                if z is not None:
                    wait_ge(act, z_ready, TT * g)
                    q = 2 * z
                    out = wz_hi[:, q:q + 2, :].rearrange("p a b -> p (a b)")
                else:
                    out = c.w_hi[:, u % 2, 0:UNIT]
                nc.scalar.activation(out, c.w_raw[:, u % 2, 0:UNIT], AF.Copy, scale=WSCALE
                                     ).then_inc(c.w_hi_ready, 1)

            def conv_input(g, j):
                for b in range(BLOCKS):
                    wait_ge(act, conv_acc, 3 * j + b + 1 + per_conv * g)
                    if b == 0 and j >= 2:
                        wait_ge(act, tap_done, 8 * (j - 1) + 8 * n_conv * g)
                        wait_ge(act, hist_kept, j - 1 + n_conv * g)
                    elif b == 0:
                        wait_ge(act, tap_done, 8 * n_conv * g)
                        wait_ge(act, hist_kept, n_conv * g)
                    lo, hi = b * BW, min((b + 1) * BW, SEQ)
                    nc.scalar.mul(pad[:, j % 2, 3 + lo:3 + hi], conv_bank[b][:, 0:hi - lo], 1 / WSCALE
                                  ).then_inc(pad_ready, 1)
                _, streams = sequences(pad[:, j % 2, :], 3)
                nc.scalar.mul(streams(3), conv_bank[2][:, SEQ - 2 * BW:BW].rearrange("p (s t) -> p s t", s=STREAMS),
                              1 / WSCALE).then_inc(pad_ready, 1)

            def silu(g, j):
                wait_ge(act, tap_done, 8 * (j + 1) + 8 * n_conv * g)
                nc.scalar.activation(xbc[:, j, :], xbc[:, j, :], AF.Silu, bias=bias[:, ds(n_conv * g + j, 1)]
                                     ).then_inc(xbc_ready, 1)

            def tanh(g, t):
                v = TT * g + t
                wait_ge(act, z_ready, v + 1)
                wait_ge(act, gated, v)
                nc.scalar.activation(zt, ps_z[:, :], AF.Tanh, scale=0.5 / WSCALE).then_inc(tanh_ready, 1)

            def inputs(g, t):
                v, p = TT * g + t, t % 2
                wait_ge(act, xt_ready, v + 1)
                wait_ge(act, y_done, (v - 1 if t >= 2 else TT * g))
                nc.scalar.copy(x_tok[:, p, :], ps_x[:, :]).then_inc(x_copied, 1)
                wait_ge(act, seg_ready, v + 1)
                if t == 1:
                    wait_ge(act, st_ready, PER_ST * g)
                else:
                    wait_ge(act, yd_ready, v - 1 if t else v)
                for q in range(2):
                    ins = nc.scalar.activation(e[:, p, 4 * q:4 * q + 4, :],
                                               ps_seg[q][:, :].rearrange("p (h k) -> p h k", h=4), AF.Exp)
                ins.then_inc(exp_ready, 1)

            def mean(g, t):
                v = TT * g + t
                wait_ge(act, gated, v + 1)
                nc.scalar.activation(junk.rearrange("p (j k) -> p j k", j=4), xbc[:, 0:4, chunk(t)],
                                     AF.Square, accum_out=ssq[:, t:t + 1]).then_inc(sq_done, 1)
                wait_ge(act, sq_done, v + 1)
                nc.scalar.activation(root[:, t:t + 1], ssq[:, t:t + 1], AF.Sqrt, bias=c.eps[:, 0:1], scale=1.0 / GW
                                     ).then_inc(root_ready, 1)

            def result_hi(g, t):
                wait_ge(act, t_ready, t + 1 + TT * g)
                if t == 0:
                    wait_ge(act, out_acc, per_out * g)
                alone(act)
                for j in range(4):
                    ins = nc.scalar.activation(g_hi[:, j, chunk(t)], ps_x[:, j * P:(j + 1) * P], AF.Copy,
                                               scale=gains[:, ds(4 * g + j, 1)])
                ins.then_inc(ghi_ready, 1)

            def group(g, first, last):
                if first:
                    conv_input(g, 0)
                for j in range(n_conv):
                    if j:
                        conv_input(g, j)
                    if j == 1 and not first:
                        result_hi(g - 1, LAST)
                    if j < n_conv - 2 or not first:
                        split(g, j + 2)
                    else:
                        split(g, j + 2, j + 2 - n_conv)
                    if j:
                        silu(g, j - 1)
                silu(g, n_conv - 1)
                if first:
                    split(g, z_unit(first, 2), 2)
                    split(g, z_unit(first, 3), 3)
                    split(g, z_unit(first, 4))
                    split(g, z_unit(first, 5))
                else:
                    for q, units in enumerate(((8,), (9, 10), (11, 12), (13, 14, 15))):
                        wait_ge(act, out_acc, 6 * (q + 1) + per_out * (g - 1))
                        for j in units:
                            split(g, j, j - 10 if 10 <= j < 14 else None)
                wait_ge(act, hist_kept, n_conv + n_conv * g)
                for i in range(TT + 1):
                    if 1 <= i <= TT:
                        tanh(g, i - 1)
                    if i < TT:
                        inputs(g, i)
                    if i >= 2:
                        result_hi(g, i - 2)
                    if i == TT and not last:
                        conv_input(g + 1, 0)
                    if 1 <= i <= TT:
                        mean(g, i - 1)

            def end():
                g = SG - 1
                result_hi(g, LAST)
                for q in range(n_out):
                    for n in range(2):
                        for b in range(BLOCKS):
                            y_n = 6 * q + 3 * n + b
                            wait_ge(act, y_ready, y_n + 1 + per_out * g)
                            wait_ge(act, ysum_done, max(0, y_n - 2))
                            nc.scalar.activation(sq[:, b, :], c.y[:, 2 * q + n, blk(b)], AF.Square
                                                 ).then_inc(ysq_ready, 1)
                    c.split_hi(act, turn_base(g) + n_units * g + END + q + 2, 0, out_acc, 6 * (q + 1) + per_out * g)

            each_group(act, group, end)

        @block.vector
        def _(dve):
            v_ = nc.vector
            dve.wait_ge(small_loaded, 64)

            def split(g, j, z=None):
                u = turn_base(g) + j
                wait_ge(dve, c.w_hi_ready, u + 1 + n_units * g)
                if z is not None:
                    q = 2 * z
                    hi, lo = (w[:, q:q + 2, :].rearrange("p a b -> p (a b)") for w in (wz_hi, wz_lo))
                    wait_ge(dve, z_ready, TT * g)
                else:
                    hi, lo = c.w_hi[:, u % 2, 0:UNIT], c.w_lo[:, u % 2, 0:UNIT]
                v_.scalar_tensor_tensor(lo, c.w_raw[:, u % 2, 0:UNIT], WSCALE, hi, ALU.mult, ALU.subtract
                                        ).then_inc(c.w_lo_ready, 1)

            def convolve(g, j):
                wait_ge(dve, pad_ready, 4 * (j + 1) + 4 * n_conv * g)
                if j == 0:
                    wait_ge(dve, t_ready, TT * g)
                wait_ge(dve, hist_put, j + 1 + n_conv * g)
                seqs = sequences(pad[:, j % 2, :], 3)
                outs = xbc[:, j, 0:SEQ], by_stream(xbc[:, j, :])
                for tap in range(4):
                    wt = taps[:, tap, ds(n_conv * g + j, 1)]
                    if tap:
                        wait_ge(dve, tap_done, 8 * j + 2 * tap + 8 * n_conv * g)
                    for out, seq in zip(outs, seqs):
                        if tap == 0:
                            ins = v_.tensor_scalar(out, seq(0), wt, None, ALU.mult)
                        else:
                            ins = v_.scalar_tensor_tensor(out, seq(tap), wt, out, ALU.mult, ALU.add)
                        ins.then_inc(tap_done, 1)

            def silu_z(g, t):
                v = TT * g + t
                wait_ge(dve, tanh_ready, v + 1)
                v_.scalar_tensor_tensor(zt, zt, 1.0, ps_z[:, :], ALU.add, ALU.mult).then_inc(zt_ready, 1)

            def inputs(g, t):
                v, p = TT * g + t, t % 2
                wait_ge(dve, bc_ready, v + 1)
                wait_ge(dve, st_ready, max(0, t - 1) + PER_ST * g)
                if t < 2:
                    wait_ge(dve, bm_ready, g)
                v_.tensor_copy(b_tok[:, p, :], ps_bc[:, 0:P]).then_inc(b_ready, 1)
                wait_ge(dve, w_ready, v)
                v_.tensor_tensor(cbm, ps_bc[:, P:2 * P], c.tri_incl if t < LAST else c.tri_block, ALU.mult
                                 ).then_inc(cb_ready, 1)
                wait_ge(dve, cb_ready, v + 1)
                wait_ge(dve, exp_ready, v + 1)
                v_.tensor_tensor(e[:, p], e[:, p], cbm.unsqueeze(1).to_broadcast([P, SHPG, P]), ALU.mult
                                 ).then_inc(w_ready, 1)
                wait_ge(dve, xdt_ready, v + 1)
                v_.tensor_tensor(heads(xdec[:, p, :]), heads(xdt[:, p, :]), of_heads(head_cols(m.dend[:, t, :], g)),
                                 ALU.mult).then_inc(xdec_ready, 1)

            def outputs(g, t):
                v, p = TT * g + t, t % 2
                for k in range(STREAMS if t == LAST else 1):
                    wait_ge(dve, st_ready, t + 1 + k + PER_ST * g)
                    wait_ge(dve, dec_ready, t + 1 + k + PER_ST * g)
                    v_.tensor_tensor(state[:, ring[k] if t == LAST else 0, :], decayed, ps_st[:, :], ALU.add
                                     ).then_inc(h_ready, 1)
                wait_ge(dve, yo_ready, v + 1)
                wait_ge(dve, gated, v)
                v_.tensor_tensor(heads(yt), heads(ps_yo[:, :]), of_heads(head_cols(m.ea[:, t, :], g)), ALU.mult
                                 ).then_inc(yo_used, 1)
                wait_ge(dve, yo_used, v + 1)
                wait_ge(dve, yd_ready, v + 1)
                v_.tensor_tensor(yt, ps_yd[:, :], yt, ALU.add).then_inc(yd_used, 1)
                wait_ge(dve, yd_used, v + 1)
                wait_ge(dve, xd_ready, v + 1)
                v_.tensor_tensor(yt, yt, x_tok[:, p, :], ALU.add).then_inc(y_done, 1)
                wait_ge(dve, y_done, v + 1)
                wait_ge(dve, zt_ready, v + 1)
                v_.scalar_tensor_tensor(xbc[:, 0:4, chunk(t)], yt.rearrange("p (j k) -> p j k", j=4), 0.5 / WSCALE,
                                        zt.rearrange("p (j k) -> p j k", j=4), ALU.mult, ALU.mult
                                        ).then_inc(gated, 1)

            def normed(g, t):
                v = TT * g + t
                wait_ge(dve, root_ready, v + 1)
                v_.reciprocal(inv[:, t:t + 1], root[:, t:t + 1]).then_inc(inv_ready, 1)
                wait_ge(dve, inv_ready, v + 1)
                yc = xbc[:, 0:4, chunk(t)]
                v_.tensor_scalar(yc, yc, inv[:, t:t + 1], None, ALU.mult).then_inc(yn_ready, 1)

            def result_lo(g, t):
                wait_ge(dve, ghi_ready, t + 1 + TT * g)
                for j in range(4):
                    ins = v_.scalar_tensor_tensor(g_lo[:, j, chunk(t)], ps_x[:, j * P:(j + 1) * P],
                                                  gains[:, ds(4 * g + j, 1)], g_hi[:, j, chunk(t)],
                                                  ALU.mult, ALU.subtract)
                ins.then_inc(glo_ready, 1)

            def add_output(g, q, squares=False):
                bank = conv_bank if squares else out_bank
                for n in range(2):
                    for b in range(BLOCKS):
                        y_n = 6 * q + 3 * n + b
                        wait_ge(dve, out_acc, y_n + 1 + per_out * g)
                        y = c.y[:, 2 * q + n, blk(b)]
                        v_.scalar_tensor_tensor(y, bank[b][:, 0:BW], 1 / WSCALE, y, ALU.mult, ALU.add
                                                ).then_inc(y_ready, 1)
                        if squares and y_n:
                            add_square(y_n - 1)

            def add_square(n):
                b = n % 3
                dve.wait_ge(ysq_ready, n + 1)
                if n < 3:
                    ins = v_.tensor_copy(c.acc[:, blk(b)], sq[:, b, :])
                else:
                    dve.wait_ge(ysum_done, n - 2)
                    ins = v_.tensor_tensor(c.acc[:, blk(b)], c.acc[:, blk(b)], sq[:, b, :], ALU.add)
                ins.then_inc(ysum_done, 1)

            def group(g, first, last):
                if not first:
                    normed(g - 1, LAST)
                for j in range(n_conv):
                    wait_ge(dve, conv_acc, 3 * (j + 1) + per_conv * g)
                    if j < n_conv - 2 or not first:
                        split(g, j + 2)
                    else:
                        split(g, j + 2, j + 2 - n_conv)
                    convolve(g, j)
                    if j == 0 and not first:
                        result_lo(g - 1, LAST)
                if first:
                    split(g, z_unit(first, 2), 2)
                    split(g, z_unit(first, 3), 3)
                    split(g, z_unit(first, 4))
                    split(g, z_unit(first, 5))
                    wait_ge(dve, y_zeroed, 1)
                else:
                    for q, units in enumerate(((8,), (9, 10), (11, 12), (13, 14, 15))):
                        add_output(g - 1, q)
                        for j in units:
                            split(g, j, j - 10 if 10 <= j < 14 else None)
                for r in range(SLOTS):
                    wait_ge(dve, state_stored[r], 16 * (uses[r] + (r == 0)) * g)
                v_.memset(state[:, 0, :], 0.0).then_inc(h_ready, 1)
                for i in range(TT + 1):
                    if i >= 2:
                        normed(g, i - 2)
                    if 1 <= i <= TT:
                        silu_z(g, i - 1)
                    if i < TT:
                        inputs(g, i)
                    if 1 <= i <= TT:
                        outputs(g, i - 1)
                    if i >= 2:
                        result_lo(g, i - 2)

            def end():
                g = SG - 1
                normed(g, LAST)
                result_lo(g, LAST)
                for q in range(n_out):
                    add_output(g, q, True)
                    c.split_lo(dve, turn_base(g) + n_units * g + END + q + 2, 0, out_acc, 6 * (q + 1) + per_out * g)
                add_square(per_out - 1)

            each_group(dve, group, end)

        @block.gpsimd
        def _(pool):
            p_ = nc.gpsimd
            pool.wait_ge(small_loaded, 64)

            def keep_history(g, j):
                _, streams = sequences(pad[:, j % 2, :], 3)
                row = n_conv * g + j
                old = hist[:, ds(row, 1), 0, :].rearrange("p a t -> p (a t)")
                olds = hist[:, ds(row, 1), 1:1 + STREAMS, :].rearrange("p a s t -> p (a s) t")
                if j < 2:
                    wait_ge(pool, tap_done, 8 * n_conv * g)
                else:
                    wait_ge(pool, tap_done, 8 * (j - 1) + 8 * n_conv * g)
                p_.tensor_copy(pad[:, j % 2, 0:3], old)
                p_.tensor_copy(streams(0, 3), olds).then_inc(hist_put, 1)
                wait_ge(pool, pad_ready, 4 * (j + 1) + 4 * n_conv * g)
                wait_ge(pool, hist_put, j + 1 + n_conv * g)
                alone(pool)
                p_.tensor_copy(old, pad[:, j % 2, SEQ:SEQ + 3])
                p_.tensor_copy(olds, streams(STEP, 3)).then_inc(hist_kept, 1)

            def seg_input(g, t):
                v, p = TT * g + t, t % 2
                if t == 1:
                    wait_ge(pool, yo_ready, TT * g)
                else:
                    wait_ge(pool, seg_ready, v - 1 if t else v)
                for part, da in enumerate((m.da_hi, m.da_lo)):
                    ins = p_.tensor_tensor(seg_part(t, part), c.tri_incl.unsqueeze(1).to_broadcast([P, SHPG, P]),
                                           head_cols(da[:, t, :], g).unsqueeze(2).to_broadcast([P, SHPG, P]),
                                           ALU.mult)
                ins.then_inc(segin_ready, 1)

            def inputs(g, t):
                v, p = TT * g + t, t % 2
                wait_ge(pool, x_copied, v + 1)
                wait_ge(pool, yd_ready, v - 1 if t >= 2 else TT * g)
                wait_ge(pool, xdec_ready, v - 1 if t >= 2 else TT * g)
                p_.tensor_tensor(heads(xdt[:, p, :]), heads(x_tok[:, p, :]), of_heads(head_cols(m.dt[:, t, :], g)),
                                 ALU.mult).then_inc(xdt_ready, 1)
                if t < LAST:
                    wait_ge(pool, h_ready, t + 1 + PER_H * g)
                    p_.tensor_tensor(heads(decayed), heads(state[:, 0, :]),
                                     of_heads(head_cols(m.chunk_decay[:, t, :], g)), ALU.mult).then_inc(dec_ready, 1)
                wait_ge(pool, xdt_ready, v + 1)
                alone(pool)
                p_.tensor_tensor(heads(x_tok[:, p, :]), heads(x_tok[:, p, :]), of_heads(head_cols(m.d, g)),
                                 ALU.mult).then_inc(xd_ready, 1)

            def streams_inputs(g):
                q = 1 - LAST % 2
                wait_ge(pool, seg_ready, TT - 1 + TT * g)
                alone(pool)
                p_.memset(seg_in[:, q], 0.0).then_inc(cm_zero, 1)
                wait_ge(pool, cm_zero, 1 + g)
                alone(pool)
                for k in range(STREAMS):
                    p_.tensor_copy(seg_in[:, q, k, k * STEP:(k + 1) * STEP],
                                   xbc[:, 5, SEQ + k * STEP:SEQ + (k + 1) * STEP]).then_inc(cm_ready, 1)
                wait_ge(pool, yd_ready, TT - 1 + TT * g)
                wait_ge(pool, b_ready, TT + TT * g)
                p_.tensor_tensor(e[:, q], b_tok[:, LAST % 2, :].unsqueeze(1).to_broadcast([P, STREAMS, P]),
                                 c.stream_mask.unsqueeze(2).to_broadcast([P, STREAMS, P]), ALU.mult
                                 ).then_inc(bm_ready, 1)

            def stream_decays(g):
                for k in range(STREAMS):
                    r = ring[k]
                    wait_ge(pool, state_loaded[r], 16 * (turn[k] + 1) + 16 * uses[r] * g)
                    wait_ge(pool, h_ready, LAST + 1 + k + PER_H * g)
                    p_.tensor_tensor(heads(decayed), heads(state[:, r, :]),
                                     of_heads(head_cols(m.stream_decay[:, k, :], g)), ALU.mult
                                     ).then_inc(dec_ready, 1)

            def group(g, first, last):
                for j in range(n_conv):
                    keep_history(g, j)
                if first:
                    p_.memset(c.y[:, :, :], 0.0).then_inc(y_zeroed, 1)
                seg_input(g, 0)
                for t in range(TT):
                    if t < LAST:
                        seg_input(g, t + 1)
                    inputs(g, t)
                streams_inputs(g)
                stream_decays(g)

            each_group(pool, group)



MATRICES = ("ident", "ones", "swap", "tri_incl", "tri_strict", "tri_block", "block_ones")


def build(nc, a):
    c_ctx = ExitStack()
    with c_ctx as ctx:
        c = Core(nc, ctx, [(a["ab_w_in"], UNIT), (a["ab_w_out"], UNIT), (a["gate_up0"], UNIT),
                           (a["down0"], DOWN_K * P), (a["dt_w"], KD * SHEADS), (a["ssm_w"], UNIT),
                           (a["gate_up1"], UNIT), (a["down1"], DOWN_K * P)])
        starts = c.starts
        c.x_hi, c.x_lo = c.sbuf("x_hi", [P, KD, T], F16), c.sbuf("x_lo", [P, KD, T], F16)
        c.y = c.sbuf("y", [P, KD, T], F32)
        c.acc = c.sbuf("acc", [P, T], F32)
        c.eps = c.sbuf("eps", [P, 1], F32)
        c.consts = c.sbuf("consts", [P, len(MATRICES) * P + STREAMS], F32)
        c.gains = c.sbuf("gains", [P, 2 * 4 * KD], F32)
        (c.ident, c.ones, c.swap, c.tri_incl, c.tri_strict, c.tri_block, c.block_ones) = (
            c.consts[:, n * P:(n + 1) * P] for n in range(len(MATRICES)))
        c.stream_mask = c.consts[:, len(MATRICES) * P:]
        c.gain = lambda layer, which, j: c.gains[:, (layer * 4 + which) * KD + j:(layer * 4 + which) * KD + j + 1]
        x1, x2, x3 = a["x1"], a["x2"], a["x3"]

        with ExitStack() as mixer:
            c.cat_hi, c.cat_lo = (c.sbuf(n, [P, KD, T], F16, mixer) for n in ("cat_hi", "cat_lo"))
            with ExitStack() as heads:
                q = c.y[:, 0:4, :].rearrange("p j t -> p (j t)")
                c.q_prompt = q[:, 0:4 * SEQ].rearrange("p (n j q) -> p n j q", j=4, q=CHUNK)
                c.q_stream = q[:, 4 * SEQ:4 * T].rearrange("p (n j q) -> p n j q", j=4, q=STEP)
                c.k, c.v = c.y[:, 4, :], c.y[:, 5, :]
                stage_qkv(c, a, 0)
                c.end_stage()
                stage_mixer(c, a, 6)
                c.end_stage()
            stage_project_y(c, "ao", starts[1], 1, KD, c.cat_hi, c.cat_lo, (0, 1), a["x"], x1)
            c.end_stage()
        feed_forward(c, "f0", starts[2], 0, a["x"], x1, x2, True)
        with ExitStack() as mixer:
            m = SSM(c, mixer)
            stage_dt(c, a, starts[4], m, x1, x2)
            c.end_stage()
            stage_ssm(c, a, starts[5], m)
            c.end_stage()
        feed_forward(c, "f1", starts[6], 1, x2, x3, a["y_out"], False)
        stage_final(c, a, x3)
        c.end_stage()



def _units(w, k_tiles):
    k, n = w.shape
    w = w.reshape(k // (k_tiles * P), k_tiles, P, n // P, P)
    return w.transpose(3, 0, 2, 1, 4).reshape(-1, P, k_tiles * P)


def _features(x):
    t, f = x.shape
    return x.T.reshape(f // P, P, t).transpose(1, 0, 2)


def _constants():
    i = np.arange(P)
    same = (i[:, None] // STEP) == (i[None, :] // STEP)
    swap = np.zeros((P, P), np.float32)
    for r in range(P):
        d = r % HD
        if d < ROPE:
            swap[r - d + (d + ROPE // 2) % ROPE, r] = 1
    mats = [np.eye(P), np.ones((P, P)), swap, i[:, None] <= i[None, :], i[:, None] > i[None, :],
            (i[:, None] <= i[None, :]) & same, same, i[:, None] // STEP == np.arange(STREAMS)[None, :]]
    return np.concatenate([x.astype(np.float32) for x in mats], axis=1)


def _rope():
    half = ROPE // 2
    inv = np.power(np.float32(500000.0), -np.arange(half, dtype=np.float32) / np.float32(half)).astype(np.float32)
    pos = np.concatenate([np.arange(SEQ), np.tile(PAST + np.arange(STEP), STREAMS)]).astype(np.float32)
    ang = (inv[:, None] * pos[None, :]).astype(np.float32).astype(np.float64)
    cos, sin = np.ones((P, T)), np.zeros((P, T))
    for r in range(P):
        d = r % HD
        if d < ROPE:
            cos[r] = np.cos(ang[d % half])
            sin[r] = np.sin(ang[d % half]) * (-1 if d < half else 1)
    return np.stack([cos, sin], axis=1).astype(np.float32)


def _head_order(w, axis):
    w = np.moveaxis(w, axis, 0)
    w = w.reshape((2, GROUP, HD) + w.shape[1:]).swapaxes(0, 1).reshape((HEADS * HD,) + w.shape[1:])
    return np.moveaxis(w, 0, axis)


def _group_order(w):
    x, b, c = np.split(w, [SG * GW, SG * GW + SG * SN], axis=-1)
    lead = w.shape[:-1]
    parts = [y.reshape(lead + (SG, -1)) for y in (x, b, c)]
    return np.concatenate(parts, axis=-1)


def _arrays(i):
    f = np.ascontiguousarray
    out = {}
    tokens = np.concatenate([i["x_prompt"][0], i["x_sample"].reshape(STREAMS * STEP, D)])
    out["x"] = _features(tokens)
    out["consts"] = _constants()
    out["rope"] = _rope()
    out["norm_g"] = i["norm_g"].reshape(2 * 4 * KD, P).T
    w = i["ab_w_in"][0]
    q, rest = w[:, :HEADS * HD], w[:, HEADS * HD:]
    kv, gb, gc, hx = rest[:, :256], rest[:, 256:768], rest[:, 768:1280], rest[:, 1280:1792]
    triples = np.stack([x.reshape(D, 4, P) for x in (gc, hx, gb)], axis=2).reshape(D, -1)
    out["ab_w_in"] = _units(np.concatenate([_head_order(q, 1), kv, triples], axis=1), KD)
    w = i["ab_w_out"][0]
    out["ab_w_out"] = _units(np.concatenate([_head_order(w[:512], 0), w[512:]]), KD)
    out["sconv_w"] = i["sconv_w"][0].reshape(3, 4, P).transpose(2, 0, 1)
    out["sconv_hist"] = i["state_sconv"][0].reshape(STREAMS, 2, 4, P).transpose(3, 2, 0, 1)
    out["cache_k"] = i["cache_attn_k"][0].reshape(STREAMS, P, P).transpose(2, 0, 1)
    out["cache_v"] = i["cache_attn_v"][0].reshape(STREAMS, P, P).transpose(1, 0, 2)
    sinks = i["attn_sinks"][0].reshape(2, GROUP)
    prompt = np.repeat(sinks.reshape(4, 2), CHUNK, axis=1).T
    stream = np.concatenate([np.repeat(sinks, STEP, axis=1).T] * 2)
    both = np.zeros((P, 2, 8), np.float32)
    both[:, 0, :4], both[:, 1, :2] = prompt, stream
    out["sinks"] = both
    for layer in range(2):
        g, u = (i[n][layer].reshape(D, FT, 1, P) for n in ("ffn_w_gate", "ffn_w_up"))
        out[f"gate_up{layer}"] = _units(np.concatenate([g, u], axis=2).reshape(D, 2 * DFF), KD)
        out[f"down{layer}"] = _units(i["ffn_w_down"][layer], DOWN_K)
    w = i["ssm_w_in"][0]
    z, xbc, dt = np.split(w, [SG * GW, 2 * SG * GW + 2 * SG * SN], axis=1)
    out["dt_w"] = dt.reshape(KD, P, SHEADS).transpose(1, 0, 2).reshape(1, P, KD * SHEADS)
    grouped = _group_order(xbc)
    units, last_o = [], []
    for n in range(SG):
        z_n = z[:, n * GW:(n + 1) * GW].reshape(KD // 2, 2, P, GW).transpose(0, 2, 1, 3).reshape(-1, P, UNIT)
        o_n = i["ssm_w_out"][0][n * GW:(n + 1) * GW].reshape(4, P, 4, 2 * P).transpose(2, 1, 0, 3).reshape(-1, P, UNIT)
        units += [_units(grouped[:, n], KD), *last_o, z_n]
        last_o = [o_n]
    out["ssm_w"] = np.concatenate(units + last_o)
    rows = np.stack([i["ssm_dt_bias"][0], i["ssm_a_log"][0], i["ssm_d"][0]])
    out["ssm_rows"] = np.repeat(rows[None], P, axis=0)
    out["ssm_taps"] = _group_order(i["ssm_conv_w"][0]).reshape(4, 24, P).transpose(2, 0, 1)
    out["ssm_bias"] = _group_order(i["ssm_conv_b"][0]).reshape(24, P).T
    hist = _group_order(i["state_ssm_conv"][0]).reshape(STREAMS, 3, 24, P).transpose(3, 2, 0, 1)
    out["ssm_hist"] = np.concatenate([np.zeros((P, 24, 1, 3), np.float32), hist], axis=2)
    out["ssm_gains"] = i["ssm_norm_g"][0].reshape(16, P).T
    out["state"] = i["state_ssm"][0].reshape(STREAMS, SHEADS * SHD, SN).transpose(0, 2, 1)
    return {k: f(v) for k, v in out.items()}


OUTS = {"y_out": (P, KD, T), "kv_prompt": (2, P, P), "kv_sample": (2, P, P), "new_sconv": (P, 4, 1 + STREAMS, 2),
        "new_ssm_hist": (P, 24, 1 + STREAMS, 3), "new_state_prompt": (P, SHEADS * SHD),
        "new_state": (STREAMS, P, SHEADS * SHD)}


def _results(r):
    y = r["y_out"].transpose(2, 1, 0).reshape(T, D)
    kvp = r["kv_prompt"].transpose(0, 2, 1).reshape(2, 1, 1, P, 2, HD)
    kvs = r["kv_sample"].transpose(0, 2, 1).reshape(2, 1, STREAMS, STEP, 2, HD)
    sc = r["new_sconv"].transpose(2, 3, 1, 0).reshape(1 + STREAMS, 2, 512)
    h = r["new_ssm_hist"].transpose(2, 3, 1, 0).reshape(1 + STREAMS, 3, SG, 6 * P)
    x, b, cc = (p.reshape(1 + STREAMS, 3, -1) for p in (h[..., :GW], h[..., GW:GW + SN], h[..., GW + SN:]))
    hist = np.concatenate([x, b, cc], axis=-1)
    sp = r["new_state_prompt"].T.reshape(1, 1, SHEADS, SHD, SN)
    ss = r["new_state"].transpose(0, 2, 1).reshape(1, STREAMS, SHEADS, SHD, SN)
    outs = (y[:SEQ].reshape(1, SEQ, D), y[SEQ:].reshape(STREAMS, STEP, D), kvp[0], kvp[1], sc[None, :1],
            hist[None, :1], sp, kvs[0], kvs[1], sc[None, 1:], hist[None, 1:], ss)
    return tuple(np.ascontiguousarray(o) for o in outs)


def kernel(**inputs):
    import concourse.bacc as bacc
    from concourse.bass_utils import run_bass_kernel_spmd

    arrays = _arrays({k: np.asarray(v) for k, v in inputs.items()})
    nc = bacc.Bacc("TRN2", target_bir_lowering=False, num_devices=1, dynamic_dma_scratch_size=1024)
    aps = {k: nc.dram_tensor("in_" + k, v.shape, F32, kind="ExternalInput").ap() for k, v in arrays.items()}
    aps |= {k: nc.dram_tensor("out_" + k, s, F32, kind="ExternalOutput").ap() for k, s in OUTS.items()}
    aps |= {k: nc.dram_tensor("mid_" + k, (P, KD, T), F32, kind="Internal").ap() for k in ("x1", "x2", "x3")}
    build(nc, aps)
    r = run_bass_kernel_spmd(nc, [{"in_" + k: v for k, v in arrays.items()}], core_ids=[0]).results[0]
    return _results({k: r["out_" + k] for k in OUTS})
```
